# Optimizing a Trainium2 kernel written in Bass

```python
import jax, jax.numpy as jnp
from jax import lax
import numpy as np

D_MODEL = 1024
BATCH = 1
SEQ = 256
DEPTH = 2

N_MIXERS = 2
NORM_EPS = 1e-6

GDN_K_HEADS = 8
GDN_V_HEADS = 16
GDN_HEAD_K = 128
GDN_HEAD_V = 128
GDN_CONV = 4
GDN_CHUNK = 64
GDN_QK = GDN_K_HEADS * GDN_HEAD_K
GDN_V = GDN_V_HEADS * GDN_HEAD_V
GDN_CONV_DIM = 2 * GDN_QK + GDN_V
GDN_PROJ = GDN_CONV_DIM + GDN_V + 2 * GDN_V_HEADS

SC_WIDTH = 2 * D_MODEL
SC_CONV = 3
SC_PROJ = 4 * SC_WIDTH

N_GDN_LAYERS = (DEPTH + 1) // 2
N_SC_LAYERS = DEPTH // 2


def rms_norm(x, w):
    xf = x.astype(jnp.float32)
    y = xf * lax.rsqrt(jnp.mean(xf * xf, axis=-1, keepdims=True) + NORM_EPS)
    return y * w.astype(jnp.float32)

def l2_normalize(x):
    xf = x.astype(jnp.float32)
    return xf * lax.rsqrt(jnp.sum(xf * xf, axis=-1, keepdims=True) + NORM_EPS)

def causal_depthwise_conv(x, w):
    width = w.shape[0]
    t = x.shape[1]
    xp = jnp.pad(x, ((0, 0), (width - 1, 0), (0, 0)))
    return sum(w[j] * xp[:, j:j + t] for j in range(width))

def chunked_gated_delta_rule(q, k, v, g, beta):
    b, h, t, dk = q.shape
    dv = v.shape[-1]
    c = GDN_CHUNK
    n = t // c
    q = q * (dk ** -0.5)
    kb = k * beta[..., None]
    vb = v * beta[..., None]
    q, k, kb = [a.reshape(b, h, n, c, dk) for a in (q, k, kb)]
    vb = vb.reshape(b, h, n, c, dv)
    g = jnp.cumsum(g.reshape(b, h, n, c), axis=-1)
    incl = jnp.tril(jnp.ones((c, c), dtype=bool))
    strict = jnp.tril(jnp.ones((c, c), dtype=bool), k=-1)
    diff = g[..., :, None] - g[..., None, :]
    decay = jnp.where(incl, jnp.exp(jnp.where(incl, diff, 0.0)), 0.0)
    a_mat = jnp.where(strict, jnp.einsum('bhnid,bhnjd->bhnij', kb, k) * decay, 0.0)
    ia = a_mat + jnp.eye(c, dtype=a_mat.dtype)
    u = lax.linalg.triangular_solve(ia, vb, left_side=True, lower=True, unit_diagonal=True)
    w = lax.linalg.triangular_solve(ia, kb * jnp.exp(g)[..., None], left_side=True, lower=True,
                                    unit_diagonal=True)
    qk = jnp.where(incl, jnp.einsum('bhnid,bhnjd->bhnij', q, k) * decay, 0.0)
    q_dec = q * jnp.exp(g)[..., None]
    g_last = g[..., -1]
    k_dec = k * jnp.exp(g_last[..., None] - g)[..., None]
    state_decay = jnp.exp(g_last)

    def step(s, xs):
        q_c, k_c, u_c, w_c, qk_c, sd_c = xs
        v_new = u_c - jnp.einsum('bhck,bhkv->bhcv', w_c, s)
        o_c = jnp.einsum('bhck,bhkv->bhcv', q_c, s) + jnp.einsum('bhij,bhjv->bhiv', qk_c, v_new)
        s = s * sd_c[..., None, None] + jnp.einsum('bhck,bhcv->bhkv', k_c, v_new)
        return s, o_c

    xs = tuple(jnp.moveaxis(a, 2, 0) for a in (q_dec, k_dec, u, w, qk, state_decay))
    s0 = jnp.zeros((b, h, dk, dv), dtype=jnp.float32)
    _, o = lax.scan(step, s0, xs)
    return jnp.moveaxis(o, 0, 2).reshape(b, h, t, dv)

def gated_deltanet_mixer(h, w_in, conv_w, a_log, dt_bias, norm_w, w_out):
    bsz, t, _ = h.shape
    proj = h @ w_in
    qkv, z, b_logit, a_logit = jnp.split(
        proj, [GDN_CONV_DIM, GDN_CONV_DIM + GDN_V, GDN_CONV_DIM + GDN_V + GDN_V_HEADS], axis=-1)
    qkv = jax.nn.silu(causal_depthwise_conv(qkv, conv_w))
    q, k, v = jnp.split(qkv, [GDN_QK, 2 * GDN_QK], axis=-1)
    rep = GDN_V_HEADS // GDN_K_HEADS
    q = jnp.repeat(l2_normalize(q.reshape(bsz, t, GDN_K_HEADS, GDN_HEAD_K)), rep, axis=2)
    k = jnp.repeat(l2_normalize(k.reshape(bsz, t, GDN_K_HEADS, GDN_HEAD_K)), rep, axis=2)
    v = v.reshape(bsz, t, GDN_V_HEADS, GDN_HEAD_V).astype(jnp.float32)
    beta = jax.nn.sigmoid(b_logit.astype(jnp.float32))
    g = -jnp.exp(a_log.astype(jnp.float32)) * jax.nn.softplus(
        a_logit.astype(jnp.float32) + dt_bias.astype(jnp.float32))
    to_bht = lambda a: jnp.swapaxes(a, 1, 2)
    o = chunked_gated_delta_rule(to_bht(q), to_bht(k), to_bht(v), to_bht(g), to_bht(beta))
    o = jnp.swapaxes(o, 1, 2)
    gate = jax.nn.silu(z.reshape(bsz, t, GDN_V_HEADS, GDN_HEAD_V).astype(jnp.float32))
    o = rms_norm(o, norm_w) * gate
    return o.reshape(bsz, t, GDN_V).astype(h.dtype) @ w_out

def short_conv_mixer(h, w_in, conv_w, w_out):
    u, b_gate, c_gate, z = jnp.split(h @ w_in, 4, axis=-1)
    y = b_gate * causal_depthwise_conv(c_gate * u, conv_w)
    return (y * jax.nn.silu(z)) @ w_out

def first_inputs(seed: int = 0) -> dict:
    key = jax.random.key(seed)
    ks = jax.random.split(key, 12)
    f32 = jnp.float32
    x = jax.random.normal(ks[0], (BATCH, SEQ, D_MODEL), f32)
    pre_norm_w = 1.0 + 0.05 * jax.random.normal(ks[1], (DEPTH, D_MODEL), f32)
    post_norm_w = 1.0 + 0.05 * jax.random.normal(ks[2], (DEPTH, D_MODEL), f32)
    gdn_w_in = jax.random.normal(ks[3], (N_GDN_LAYERS, D_MODEL, GDN_PROJ), f32) * D_MODEL ** -0.5
    gdn_conv_w = jax.random.normal(ks[4], (N_GDN_LAYERS, GDN_CONV, GDN_CONV_DIM), f32) * GDN_CONV ** -0.5
    gdn_A_log = jnp.log(jax.random.uniform(ks[5], (N_GDN_LAYERS, GDN_V_HEADS), f32, 1.0, 16.0))
    dt = jnp.exp(jax.random.uniform(ks[6], (N_GDN_LAYERS, GDN_V_HEADS), f32,
                                    float(np.log(1e-3)), float(np.log(1e-1))))
    gdn_dt_bias = dt + jnp.log(-jnp.expm1(-dt))
    gdn_norm_w = 1.0 + 0.05 * jax.random.normal(ks[7], (N_GDN_LAYERS, GDN_HEAD_V), f32)
    gdn_w_out = jax.random.normal(ks[8], (N_GDN_LAYERS, GDN_V, D_MODEL), f32) * GDN_V ** -0.5
    sc_w_in = jax.random.normal(ks[9], (N_SC_LAYERS, D_MODEL, SC_PROJ), f32) * D_MODEL ** -0.5
    sc_conv_w = jax.random.normal(ks[10], (N_SC_LAYERS, SC_CONV, SC_WIDTH), f32) * SC_CONV ** -0.5
    sc_w_out = jax.random.normal(ks[11], (N_SC_LAYERS, SC_WIDTH, D_MODEL), f32) * SC_WIDTH ** -0.5
    return {"x": x, "pre_norm_w": pre_norm_w, "post_norm_w": post_norm_w,
            "gdn_w_in": gdn_w_in, "gdn_conv_w": gdn_conv_w, "gdn_A_log": gdn_A_log,
            "gdn_dt_bias": gdn_dt_bias, "gdn_norm_w": gdn_norm_w, "gdn_w_out": gdn_w_out,
            "sc_w_in": sc_w_in, "sc_conv_w": sc_conv_w, "sc_w_out": sc_w_out}

def first_block(x, pre_norm_w, post_norm_w, gdn_w_in, gdn_conv_w, gdn_A_log, gdn_dt_bias, gdn_norm_w,
              gdn_w_out, sc_w_in, sc_conv_w, sc_w_out):
    for i in range(DEPTH):
        h = rms_norm(x, pre_norm_w[i]).astype(x.dtype)
        j = i // N_MIXERS
        if i % N_MIXERS == 0:
            y = gated_deltanet_mixer(h, gdn_w_in[j], gdn_conv_w[j], gdn_A_log[j], gdn_dt_bias[j],
                                     gdn_norm_w[j], gdn_w_out[j])
        else:
            y = short_conv_mixer(h, sc_w_in[j], sc_conv_w[j], sc_w_out[j])
        x = x + rms_norm(y, post_norm_w[i]).astype(x.dtype)
    return x


DEPTH_2 = 1

RET_HEADS = D_MODEL // 256
RET_QK_DIM = D_MODEL
RET_V_DIM = 2 * D_MODEL
RET_HEAD_QK = RET_QK_DIM // RET_HEADS
RET_HEAD_V = RET_V_DIM // RET_HEADS
RET_CHUNK = 128
ROPE_BASE = 10000.0
GN_EPS = 1e-5
CONV_DIM = D_MODEL
CONV_WIDTH = 31
LN_EPS = 1e-5
RMS_EPS = 1e-6
IN_SPLITS = (RET_QK_DIM, RET_QK_DIM, RET_V_DIM, RET_V_DIM, CONV_DIM, CONV_DIM, CONV_DIM, D_MODEL, D_MODEL)
IN_WIDTH = sum(IN_SPLITS)


def rmsnorm(x, g):
    xf = x.astype(jnp.float32)
    y = xf * lax.rsqrt(jnp.mean(xf * xf, axis=-1, keepdims=True) + RMS_EPS)
    return (y * g.astype(jnp.float32)).astype(x.dtype)

def layernorm(x, g, b):
    xf = x.astype(jnp.float32)
    mu = jnp.mean(xf, axis=-1, keepdims=True)
    var = jnp.mean(jnp.square(xf - mu), axis=-1, keepdims=True)
    y = (xf - mu) * lax.rsqrt(var + LN_EPS)
    return (y * g.astype(jnp.float32) + b.astype(jnp.float32)).astype(x.dtype)

def head_groupnorm(o):
    of = o.astype(jnp.float32)
    mu = jnp.mean(of, axis=-1, keepdims=True)
    var = jnp.mean(jnp.square(of - mu), axis=-1, keepdims=True)
    return (of - mu) * lax.rsqrt(var + GN_EPS)

def rotary(t, positions):
    dh = t.shape[-1]
    half = dh // 2
    inv_freq = ROPE_BASE ** (-jnp.arange(half, dtype=jnp.float32) / half)
    ang = positions.astype(jnp.float32)[..., None] * inv_freq
    cos = jnp.cos(ang)[:, :, None, :]
    sin = jnp.sin(ang)[:, :, None, :]
    t1, t2 = t[..., :half], t[..., half:]
    return jnp.concatenate([t1 * cos - t2 * sin, t1 * sin + t2 * cos], axis=-1)

def retention_chunkwise(q, k, v):
    B, S, H, dk = q.shape
    dv = v.shape[-1]
    C = RET_CHUNK
    N = S // C
    log_g = jnp.log1p(-jnp.exp2(-5.0 - jnp.arange(H, dtype=jnp.float32)))
    idx = jnp.arange(C, dtype=jnp.float32)
    diff = idx[:, None] - idx[None, :]
    causal = diff >= 0
    decay_mask = jnp.where(causal, jnp.exp(log_g[:, None, None] * jnp.where(causal, diff, 0.0)), 0.0)
    xi = jnp.exp(log_g[:, None] * (idx + 1.0))
    zeta = jnp.exp(log_g[:, None] * (C - 1.0 - idx))
    g_chunk = jnp.exp(log_g * C)

    def to_chunks(t):
        return t.reshape(B, N, C, H, t.shape[-1]).transpose(1, 0, 3, 2, 4)

    def step(state, inp):
        qc, kc, vc = inp
        scores = jnp.einsum('bhid,bhjd->bhij', qc, kc) * decay_mask[None]
        inner = jnp.einsum('bhij,bhje->bhie', scores, vc)
        cross = jnp.einsum('bhid,bhde->bhie', qc, state) * xi[None, :, :, None]
        new_state = state * g_chunk[None, :, None, None] + jnp.einsum(
            'bhjd,bhje->bhde', kc * zeta[None, :, :, None], vc)
        return new_state, inner + cross

    state0 = jnp.zeros((B, H, dk, dv), jnp.float32)
    _, o = lax.scan(step, state0, (to_chunks(q), to_chunks(k), to_chunks(v)))
    return o.transpose(1, 0, 3, 2, 4).reshape(B, S, H, dv)

def causal_depthwise_conv_2(u, w, b):
    out = lax.conv_general_dilated(
        u, w[:, None, :].astype(u.dtype), window_strides=(1,),
        padding=[(CONV_WIDTH - 1, 0)],
        dimension_numbers=('NWC', 'WIO', 'NWC'),
        feature_group_count=u.shape[-1])
    return out + b.astype(u.dtype)

def second_inputs(seed: int = 0) -> dict:
    key = jax.random.key(seed)
    ks = jax.random.split(key, 16)
    f32 = jnp.float32
    x = jax.random.normal(ks[0], (BATCH, SEQ, D_MODEL), f32)
    c = jax.random.normal(ks[1], (BATCH, D_MODEL), f32)
    offsets = jax.random.randint(ks[2], (BATCH, 1), 0, 4096, dtype=jnp.int32)
    positions = offsets + jnp.arange(SEQ, dtype=jnp.int32)[None, :]
    w_ada = jax.random.normal(ks[3], (DEPTH_2, D_MODEL, 3 * D_MODEL), f32) * (0.1 * D_MODEL ** -0.5)
    b_ada = jax.random.normal(ks[4], (DEPTH_2, 3 * D_MODEL), f32) * 0.02
    pre_norm_g = 1.0 + 0.05 * jax.random.normal(ks[5], (DEPTH_2, D_MODEL), f32)
    w_in = jax.random.normal(ks[6], (DEPTH_2, D_MODEL, IN_WIDTH), f32) * D_MODEL ** -0.5
    conv_w = jax.random.normal(ks[7], (DEPTH_2, CONV_WIDTH, CONV_DIM), f32) * CONV_WIDTH ** -0.5
    conv_b = jax.random.normal(ks[8], (DEPTH_2, CONV_DIM), f32) * 0.02
    conv_ln_g = 1.0 + 0.05 * jax.random.normal(ks[9], (DEPTH_2, CONV_DIM), f32)
    conv_ln_b = jax.random.normal(ks[10], (DEPTH_2, CONV_DIM), f32) * 0.02
    w_ret_out = jax.random.normal(ks[11], (DEPTH_2, RET_V_DIM, D_MODEL), f32) * RET_V_DIM ** -0.5
    w_conv_out = jax.random.normal(ks[12], (DEPTH_2, CONV_DIM, D_MODEL), f32) * CONV_DIM ** -0.5
    w_out = jax.random.normal(ks[13], (DEPTH_2, D_MODEL, D_MODEL), f32) * D_MODEL ** -0.5
    post_norm_g = 1.0 + 0.05 * jax.random.normal(ks[14], (DEPTH_2, D_MODEL), f32)
    return {"x": x, "c": c, "positions": positions, "w_ada": w_ada, "b_ada": b_ada,
            "pre_norm_g": pre_norm_g, "w_in": w_in, "conv_w": conv_w, "conv_b": conv_b,
            "conv_ln_g": conv_ln_g, "conv_ln_b": conv_ln_b, "w_ret_out": w_ret_out,
            "w_conv_out": w_conv_out, "w_out": w_out, "post_norm_g": post_norm_g}

def second_block(x, c, positions, w_ada, b_ada, pre_norm_g, w_in, conv_w, conv_b,
              conv_ln_g, conv_ln_b, w_ret_out, w_conv_out, w_out, post_norm_g):
    B, S, _ = x.shape
    split_at = [int(v) for v in np.cumsum(IN_SPLITS)[:-1]]
    for l in range(DEPTH_2):
        mod = c @ w_ada[l] + b_ada[l]
        shift, scale, gate = jnp.split(mod, 3, axis=-1)
        h = rmsnorm(x, pre_norm_g[l]) * (1.0 + scale[:, None, :]) + shift[:, None, :]

        proj = h @ w_in[l]
        q, k, v, z_ret, u_val, u_gate, z_conv, g_a, g_b = jnp.split(proj, split_at, axis=-1)

        qh = rotary(q.reshape(B, S, RET_HEADS, RET_HEAD_QK).astype(jnp.float32), positions)
        kh = rotary(k.reshape(B, S, RET_HEADS, RET_HEAD_QK).astype(jnp.float32), positions) * RET_HEAD_QK ** -0.5
        vh = v.reshape(B, S, RET_HEADS, RET_HEAD_V).astype(jnp.float32)
        ret = head_groupnorm(retention_chunkwise(qh, kh, vh)).reshape(B, S, RET_V_DIM).astype(x.dtype)
        y_a = (ret * jax.nn.silu(z_ret)) @ w_ret_out[l]

        a = u_val * jax.nn.sigmoid(u_gate)
        a = causal_depthwise_conv_2(a, conv_w[l], conv_b[l])
        a = jax.nn.silu(layernorm(a, conv_ln_g[l], conv_ln_b[l]))
        y_b = (a * jax.nn.silu(z_conv)) @ w_conv_out[l]

        merged = jax.nn.sigmoid(g_a) * y_a + jax.nn.sigmoid(g_b) * y_b
        y = merged @ w_out[l]

        x = x + gate[:, None, :] * rmsnorm(y, post_norm_g[l])
    return x


def setup_inputs(seed=0):
    out = dict(first_inputs(seed))
    for name, value in second_inputs(seed + 1).items():
        if name != "x":
            out[name + "_2"] = value
    return out


def reference(
    x, pre_norm_w, post_norm_w, gdn_w_in, gdn_conv_w, gdn_A_log, gdn_dt_bias, gdn_norm_w,
    gdn_w_out, sc_w_in, sc_conv_w, sc_w_out, c_2, positions_2, w_ada_2, b_ada_2, pre_norm_g_2,
    w_in_2, conv_w_2, conv_b_2, conv_ln_g_2, conv_ln_b_2, w_ret_out_2, w_conv_out_2, w_out_2,
    post_norm_g_2,
):
    x = first_block(
        x, pre_norm_w, post_norm_w, gdn_w_in, gdn_conv_w, gdn_A_log, gdn_dt_bias, gdn_norm_w,
        gdn_w_out, sc_w_in, sc_conv_w, sc_w_out,
    )
    return second_block(
        x, c_2, positions_2, w_ada_2, b_ada_2, pre_norm_g_2, w_in_2, conv_w_2, conv_b_2,
        conv_ln_g_2, conv_ln_b_2, w_ret_out_2, w_conv_out_2, w_out_2, post_norm_g_2,
    )


_drawn_inputs = setup_inputs


def setup_inputs(seed=0):
    import zlib

    import numpy as np

    out = dict(_drawn_inputs(seed))
    spreads = {}
    factors = {'b_ada_2': 4.65,
     'pre_norm_g_2': 8.0,
     'conv_b_2': 23.637,
     'conv_ln_g_2': 8.0,
     'conv_ln_b_2': 42.948,
     'post_norm_g_2': 8.0}
    for name, (base, spread) in spreads.items():
        noise = np.random.default_rng([zlib.crc32(name.encode()), seed]).standard_normal(out[name].shape)
        drawn = base * np.exp(spread * noise) if base else spread * noise
        out[name] = __import__('jax').numpy.asarray(drawn.astype(out[name].dtype))
    for name, factor in factors.items():
        out[name] = (out[name] * factor).astype(out[name].dtype)
    return out
```

```python
import math
from contextlib import ExitStack

import numpy as np

import concourse.bass as bass
from concourse import mybir

F32 = mybir.dt.float32
F32R = mybir.dt.float32r
I32 = mybir.dt.int32
ACT = mybir.ActivationFunctionType
ALU = mybir.AluOpType
AX_X = mybir.AxisListType.X

P = 128
SEQ = 256
NT = SEQ // P
D = 1024
KT = D // P
ROPE_BASE = 10000.0
RMS_EPS = 1e-6
NORM_EPS = 1e-5

VH, KH = 16, 8
HD = 128
GQK, GV = KH * HD, VH * HD
GCONV = 4
GQKV = 2 * GQK + GV
SCW = 2 * D
SCONV = 3
RH, RDK, RDV = 4, 256, 512
CW = 31
CPAD = CW - 1
HG = 4
NPAIR = VH // HG
NLEV = 7

CC = 256
RING = 4
PHASES = [("qkv", 16), ("z", 8), ("gdn_out", 8), ("sc_in", 32), ("sc_out", 8), ("glu", 8), ("qk", 8), ("v", 8),
          ("zret", 8), ("zconv", 4), ("gates", 8), ("conv_out", 4), ("ret_out", 8), ("w_out", 4)]
FIRST = {}
COUNT = dict(PHASES)
_g = 0
for _n, _c in PHASES:
    FIRST[_n] = _g
    _g += _c
CHUNKS = _g
ADA_PIECES = COUNT["qkv"] + COUNT["z"]
assert ADA_PIECES * P == 3 * D

C_ID, C_ONE, C_LOW, C_INC, C_M0, C_M0T, C_MASK = 0, 1, 2, 3, 4, 5, 6
NCONST = C_MASK + NLEV - 1

V_PRE, V_PRE2, V_BADA, V_CB, V_LG, V_LB, V_C, V_SC = 0, 16, 24, 48, 56, 64, 72, 80
G_ROW = 32


def build(nc, x_in, pre_norm_w, post_norm_w, gdn_w_in, gdn_conv_w, gdn_A_log, gdn_dt_bias, gdn_norm_w, gdn_w_out,
          sc_w_in, sc_conv_w, sc_w_out, c_2, positions_2, w_ada_2, b_ada_2, pre_norm_g_2, w_in_2, conv_w_2, conv_b_2,
          conv_ln_g_2, conv_ln_b_2, w_ret_out_2, w_conv_out_2, w_out_2, post_norm_g_2, masks, decays, freqs, out):
    ctx = ExitStack()
    with ctx:
        def sem(name):
            return ctx.enter_context(nc.semaphore(name))

        base = (nc.sbuf_base + 63) // 64 * 64
        fence = ctx.enter_context(nc.sbuf_tensor("fence", [P, (nc.sbuf_usable_end - base) // 64 * 16 - 16], F32))
        top = [base]

        def at(name, offset, shape, dt=F32):
            return nc.alloc_sbuf_tensor_at(name, shape, dt, offset=offset)

        def room(nbytes):
            offset = top[0]
            top[0] += (nbytes + 31) // 32 * 32
            assert top[0] <= nc.sbuf_usable_end, (top[0], nc.sbuf_usable_end)
            return offset

        def new(name, shape, dt=F32):
            n = 4
            for s in shape[1:]:
                n *= s
            return at(name, room(n), shape, dt)

        K = 1024
        raw = [new(f"w_raw{s}", [P, KT, CC]) for s in range(RING)]
        w_hi = [new(f"w_hi{s}", [P, KT, CC], F32R) for s in range(2)]
        w_lo = [new(f"w_lo{s}", [P, KT, CC], F32R) for s in range(2)]
        x = new("x", [P, NT, D])
        o_hT, o_yT, o_ada, o_ar = room(16 * K), room(32 * K), room(8 * K), room(64 * K)
        hT_hi, hT_lo = at("hT_hi", o_hT, [P, KT, SEQ], F32R), at("hT_lo", o_hT + 8 * K, [P, KT, SEQ], F32R)
        yT_hi, yT_lo = at("yT_hi", o_yT, [P, 2 * KT, SEQ], F32R), at("yT_lo", o_yT + 16 * K, [P, 2 * KT, SEQ], F32R)
        ada = [at(f"ada{s}", o_ada + 4 * K * s, [P, KT, P]) for s in range(2)]
        const = new("const", [P, NCONST, P])
        ident, ones = const[:, C_ID, :], const[:, C_ONE, :]
        o_row = room(4 * K)
        row = at("row", o_row, [P, D])
        nw_row = new("nw_row", [P, HD])
        par = new("par", [P, 4, P])
        bg = new("bg", [P, SEQ])
        bgt = new("bgt", [P, NT, P])
        eg = new("eg", [P, NT, VH])
        nbeg = new("nbeg", [P, NT, VH])
        wdec = new("wdec", [P, VH])
        acols = new("acols", [P, 4])
        mod = new("mod", [P, 3 * KT])
        gain2 = new("gain2", [P, KT])
        zeros = new("zeros", [P, KT])
        eps_r, eps_n = new("eps_r", [P, 1]), new("eps_n", [P, 1])
        ss, ms, rstd = new("ss", [P, 4]), new("ms", [P, 4]), new("rstd", [P, 4])
        o_ss, o_rs = new("o_ss", [P, NT, VH]), new("o_rs", [P, NT, VH])
        freq = new("freq", [P, 1])
        gst, gmv, grs = new("gst", [P, NT, 6]), new("gmv", [P, NT, 2]), new("grs", [P, NT])

        xn = at("xn", o_ar, [P, NT, D])
        hx = at("hx", o_ar + 8 * K, [P, KT, SEQ])
        junk = at("junk", o_ar + 8 * K, [P, NT, D])
        vecs = at("vecs", o_ar + 16 * K, [P, 4, P])
        qkvT = at("qkvT", o_ar, [P, 4 * KT, SEQ])
        S = at("S", o_ar + 16 * K, [P, NPAIR, NT, HG, P])
        zo = at("zo", o_ar + 32 * K, [P, NT, GV])
        PT = at("PT", o_ar + 48 * K, [P, NPAIR, NT, HG, P])
        cacc = [at(f"cacc{s}", o_ar + (48 + 2 * s) * K, [P, 2, SEQ]) for s in range(2)]
        ba_raw = at("ba_raw", o_ar + 52 * K, [P, KT, P])
        ba_hi = at("ba_hi", o_ar + 56 * K, [P, KT, P], F32R)
        ba_lo = at("ba_lo", o_ar + 60 * K, [P, KT, P], F32R)
        vb = at("vb", o_yT, [P, NT, VH, HD])
        ktok = at("ktok", o_yT + 16 * K, [P, KH, HD])
        LT = [[at(f"LT{q}{t}", o_yT + (20 + 2 * (2 * q + t)) * K, [P, HG, P]) for t in range(NT)] for q in range(2)]
        Z = [at(f"Z{t}", o_yT + (28 + 2 * t) * K, [P, HG, P]) for t in range(NT)]
        sq = [at(f"sq{s}", o_yT + (20 + 2 * s) * K, [P, 2, SEQ]) for s in range(2)]
        rn = [at(f"rn{s}", o_yT + (24 + 2 * s) * K, [P, 2, SEQ]) for s in range(2)]
        gz, gl, gs = (at(f"gate{s}", o_hT + (6 + s) * K, [P, SEQ]) for s in range(3))
        E, Di, A = (at(n, o_hT + 2 * s * K, [P, HG, P]) for s, n in enumerate(("E", "Di", "A")))
        T = [[at(f"T{q}{t}", o_hT + (6 + 2 * (2 * q + t)) * K, [P, HG, P]) for t in range(NT)] for q in range(2)]
        qS = at("qS", o_hT + 14 * K, [P, HG, P])
        kdec, R, U, s1 = (at(n, o_ada + 2 * s * K, [P, HG, P]) for s, n in enumerate(("kdec", "R", "U", "s1")))
        osq = at("osq", o_row, [P, HG, P])
        sc_u = at("sc_u", o_ar + 16 * K, [P, 2, SEQ])
        sc_cu = at("sc_cu", o_ar + 18 * K, [P, 2, SEQ])
        sc_v = at("sc_v", o_ar + 20 * K, [P, 2, SEQ])
        sc_y = at("sc_y", o_ar + 22 * K, [P, 2, SEQ])
        sc_z = at("sc_z", o_ar + 24 * K, [P, 2, SEQ])
        sc_yz = at("sc_yz", o_ar + 26 * K, [P, 2, SEQ])
        aP = at("aP", o_ar, [P, KT, CPAD + SEQ])
        cv = at("cv", o_ar + 9728, [P, KT, SEQ])
        o_q = o_ar + 9728 + 8 * K
        qkT = at("qkT", o_q, [P, 2 * KT, SEQ])
        vt = at("vt", o_q + 16 * K, [P, NT, 2 * D])
        o_t = o_q + 32 * K
        st = at("st", o_t, [P, RH, 3 * P])
        glu, rp1, rp2 = (at(n, o_t + 2 * s * K, [P, 2, SEQ]) for s, n in enumerate(("glu", "rp1", "rp2")))
        cvo = at("cvo", o_t + 6 * K, [P, SEQ])
        lnm = at("lnm", o_t + 7 * K, [P, 2, SEQ])
        og = [at(f"og{t}", o_t + (9 + 2 * t) * K, [P, RDV]) for t in range(NT)]
        zr = at("zr", o_yT, [P, NT, 2 * D])
        zc = at("zc", o_q, [P, KT, SEQ])
        gab = at("gab", o_q + 8 * K, [P, 2 * KT, SEQ])
        a2 = at("a2", o_q + 24 * K, [P, KT, SEQ])
        decay = at("decay", o_ada, [P, RH, 3 * P])
        trig = at("trig", o_ada + 6 * K, [P, 2, SEQ])
        pos_i = at("pos_i", o_q + 16 * K, [P, SEQ], I32)
        ang, turn = at("ang", o_q + 17 * K, [P, SEQ]), at("turn", o_q + 18 * K, [P, 2, SEQ])
        gdiag = at("gdiag", o_t, [P, KT, P])

        psum = ctx.enter_context(nc.psum_tensor("psum", [P, 8, 512], F32))

        def bank(b, inner=SEQ):
            return psum[:, b, :].rearrange("p (a n) -> p a n", n=inner)

        raw_ready = [sem(f"raw_ready{s}") for s in range(RING)]
        hi_ready, lo_ready = sem("hi_ready"), sem("lo_ready")
        chunk_done = sem("chunk_done")
        bank_free = sem("bank_free")
        ada_ready = [sem(f"ada_ready{s}") for s in range(2)]
        ada_used = sem("ada_used")
        x_loaded, vecs_loaded, small_loaded, ba_loaded, rope_loaded = sem("x_loaded"), sem("vecs_loaded"), sem("small_loaded"), sem("ba_loaded"), sem("rope_loaded")
        row_loaded, decay_loaded, cleared, padded = sem("row_loaded"), sem("decay_loaded"), sem("cleared"), sem("padded")
        par_turned, par_ready = sem("par_turned"), sem("par_ready")
        pre_ss, pre_std, pre_rstd, xn_ready = sem("pre_ss"), sem("pre_std"), sem("pre_rstd"), sem("xn_ready")
        turned, hx_ready, hhi_ready, h_ready = sem("turned"), sem("hx_ready"), sem("hhi_ready"), sem("h_ready")
        y_ready, post_ss, post_std, post_rstd = sem("y_ready"), sem("post_ss"), sem("post_std"), sem("post_rstd")
        post_scaled, x_ready, row_ready = sem("post_scaled"), sem("x_ready"), sem("row_ready")
        out_done = sem("out_done")
        tap0, tap_step, qkv_ready = sem("tap0"), sem("tap_step"), sem("qkv_ready")
        ba_hi_ready, ba_lo_ready, ba_done = sem("ba_hi_ready"), sem("ba_lo_ready"), sem("ba_done")
        beta_ready, gate_v, gate_a, g_ready = sem("beta_ready"), sem("gate_v"), sem("gate_a"), sem("g_ready")
        bg_turned, bgt_ready, eg_ready, nbeg_ready = sem("bg_turned"), sem("bgt_ready"), sem("eg_ready"), sem("nbeg_ready")
        sq_ready, l2_sum, l2_ln, l2_r, qk_ready = sem("sq_ready"), sem("l2_sum"), sem("l2_ln"), sem("l2_r"), sem("qk_ready")
        v_turned, vb_ready, k_turned, ktok_ready = sem("v_turned"), sem("vb_ready"), sem("k_turned"), sem("ktok_ready")
        zn_ready = sem("zn_ready")
        grow_ready, kq_ready, d_ready, e_ready, masked = sem("grow_ready"), sem("kq_ready"), sem("d_ready"), sem("e_ready"), sem("masked")
        wd_ready, wd_sub = sem("wd_ready"), sem("wd_sub")
        ap_ready, ap_turned, lt_ready, pt_ready = sem("ap_ready"), sem("ap_turned"), sem("lt_ready"), sem("pt_ready")
        l_ready, chain_ready = sem("l_ready"), sem("chain_ready")
        w_done = [sem(f"w_done{t}") for t in range(NT)]
        z_ready = [sem(f"z_ready{t}") for t in range(NT)]
        ts_done = [sem(f"ts_done{t}") for t in range(NT)]
        t_ready = [sem(f"t_ready{t}") for t in range(NT)]
        s_ready = [sem(f"s_ready{t}") for t in range(NT)]
        kdec_ready, u_done, u_ready, o0_done, s1_done, s1_ready = (sem(n) for n in ("kdec_ready", "u_done", "u_ready", "o0_done", "s1_done", "s1_ready"))
        ks_done, r_ready, qs_ready, vn_done, vn_ready, o1_done, o_ready = (sem(n) for n in ("ks_done", "r_ready", "qs_ready", "vn_done", "vn_ready", "o1_done", "o_ready"))
        osq_ready, oss_ready, o_std, o_rstd, og_ready = (sem(n) for n in ("osq_ready", "oss_ready", "o_std", "o_rstd", "og_ready"))
        yT_turned, yhi_ready, y_op_ready = sem("yT_turned"), sem("yhi_ready"), sem("y_op_ready")
        sc_u_ready, sc_cu_ready, sc_v0, sc_step, sc_y_ready, sc_z_ready, sc_yz_ready = (
            sem(n) for n in ("sc_u_ready", "sc_cu_ready", "sc_v0", "sc_step", "sc_y_ready", "sc_z_ready", "sc_yz_ready"))
        mod_ready, gain2_ready = sem("mod_ready"), sem("gain2_ready")
        glu_ready, ang_step, ang_ready, trig_ready = sem("glu_ready"), sem("ang_step"), sem("ang_ready"), sem("trig_ready")
        rp_step, vt_ready, zr_ready = sem("rp_step"), sem("vt_ready"), sem("zr_ready")
        sco_done, st_ready, ro_done, gn_step, gn_std, gn_ready, og_free = (sem(n) for n in ("sco_done", "st_ready", "ro_done", "gn_step", "gn_std", "gn_ready", "og_free"))
        rg_ready = sem("rg_ready")
        cv_step, cv_ready, mean_done, xc_ready, a2_ready, var_done, ln_step, ln_ready = (sem(n) for n in ("cv_step", "cv_ready", "mean_done", "xc_ready", "a2_ready", "var_done", "ln_step", "ln_ready"))
        lna_ready, lns_ready, lnz_ready, zc_ready, gab_ready = (sem(n) for n in ("lna_ready", "lns_ready", "lnz_ready", "zc_ready", "gab_ready"))
        chi_ready, cop_ready, yb_ready, ya_step, mg_ready, mhi_ready, mop_ready = (sem(n) for n in ("chi_ready", "cop_ready", "yb_ready", "ya_step", "mg_ready", "mhi_ready", "mop_ready"))
        qs_done, o1_ready, gn_rec, ln_mean = sem("qs_done"), sem("o1_ready"), sem("gn_rec"), sem("ln_mean")
        gate_diag, gate_row, row_mul = sem("gate_diag"), sem("gate_row"), sem("row_mul")
        block = ctx.enter_context(nc.Block())

        def loop(eng, n, step):
            if n == 1:
                step(0)
            else:
                with eng.Fori(0, n) as i:
                    step(i)

        def heads(ap, n):
            return ap.rearrange("p (a n) -> p a n", a=1).to_broadcast([P, n, ap.shape[-1]])

        @block.sync
        def _(sp):
            def cols(w, r0, c, n=CC):
                return w[r0:r0 + D, bass.ds(c, n)].rearrange("(k p) n -> p k n", p=P)

            def chunk(g, slot, src, wait=True):
                if wait:
                    sp.wait_ge(lo_ready, g - RING + 1)
                sp.dma_start(raw[slot][:, :, :], src).then_inc(raw_ready[slot], 16)

            def ada_piece(a, slot, wait=True):
                if wait:
                    sp.wait_ge(ada_used, a - 1)
                sp.dma_start(ada[slot][:, :, :], cols(w_ada_2[0], 0, a * P, P)).then_inc(ada_ready[slot], 16)

            def phase(name, where, with_ada=None, start=0):
                g0 = FIRST[name]

                def step(i):
                    for j in range(4):
                        w, r0, c = where(i, j)
                        g = i * 4 + (g0 + j)
                        chunk(g, j, cols(w, r0, c))
                        if with_ada is not None:
                            ada_piece(i * 4 + (with_ada + j), j % 2)
                if start:
                    with sp.Fori(start, COUNT[name] // 4) as i:
                        step(i)
                else:
                    loop(sp, COUNT[name] // 4, step)

            sp.dma_start(x[:, :, :], x_in[0].rearrange("(t p) d -> p t d", p=P)).then_inc(x_loaded, 16)
            sp.dma_start(const[:, :, :], masks).then_inc(vecs_loaded, 16)
            sp.dma_start(vecs[:, 0, :], gdn_conv_w[0].rearrange("j (n p) -> (j n) p", p=P)).then_inc(vecs_loaded, 16)
            for at_row, v in ((V_PRE, pre_norm_w), (V_PRE2, pre_norm_g_2), (V_BADA, b_ada_2), (V_CB, conv_b_2),
                              (V_LG, conv_ln_g_2), (V_LB, conv_ln_b_2), (V_C, c_2)):
                n = v.shape[0] * v.shape[1] // P
                sp.dma_start(vecs[at_row:at_row + n, 1, :], v.rearrange("l (k p) -> (l k) p", p=P)).then_inc(vecs_loaded, 16)
            sp.dma_start(vecs[V_SC:P, 1, :], sc_conv_w[0].rearrange("j (n p) -> (j n) p", p=P)).then_inc(vecs_loaded, 16)
            sp.dma_start(vecs[:, 2, :], conv_w_2[0, 0:16].rearrange("j (n p) -> (j n) p", p=P)).then_inc(vecs_loaded, 16)
            sp.dma_start(vecs[0:120, 3, :], conv_w_2[0, 16:CW].rearrange("j (n p) -> (j n) p", p=P)).then_inc(vecs_loaded, 16)
            chunk(0, 0, cols(gdn_w_in[0], 0, 0), wait=False)
            sp.dma_start(acols[G_ROW:G_ROW + VH, 0:1], gdn_A_log.rearrange("l h -> h l")).then_inc(small_loaded, 16)
            sp.dma_start(acols[G_ROW:G_ROW + VH, 1:2], gdn_dt_bias.rearrange("l h -> h l")).then_inc(small_loaded, 16)
            sp.dma_start(freq[:, :], freqs).then_inc(small_loaded, 16)
            sp.dma_start(nw_row[:, :], gdn_norm_w.to_broadcast([P, HD])).then_inc(small_loaded, 16)
            for j in range(4):
                if j:
                    chunk(j, j, cols(gdn_w_in[0], 0, j * CC), wait=False)
                ada_piece(j, j % 2, wait=j >= 2)
            sp.wait_ge(padded, 1)
            ba0 = GQKV + GV
            sp.dma_start(ba_raw[:, :, 0:VH], cols(gdn_w_in[0], 0, ba0, VH)).then_inc(ba_loaded, 16)
            sp.dma_start(ba_raw[:, :, G_ROW:G_ROW + VH], cols(gdn_w_in[0], 0, ba0 + VH, VH)).then_inc(ba_loaded, 16)
            phase("qkv", lambda i, j: (gdn_w_in[0], 0, i * 1024 + j * CC), with_ada=0, start=1)
            phase("z", lambda i, j: (gdn_w_in[0], 0, i * 1024 + (GQKV + j * CC)), with_ada=COUNT["qkv"])

            def two_halves(w):
                return lambda i, j: (w, j % 2 * D, i * 512 + j // 2 * CC)

            phase("gdn_out", two_halves(gdn_w_out[0]))
            sp.wait_ge(o_ready, 2 * NPAIR)
            sp.dma_start(row[:, :], post_norm_w[0:1, :].to_broadcast([P, D])).then_inc(row_loaded, 16)
            phase("sc_in", lambda i, j: (sc_w_in[0], 0, i * CC + (0, 2 * SCW, SCW, 3 * SCW)[j]))
            sp.wait_ge(x_ready, NT)
            sp.dma_start(row[:, :], post_norm_w[1:2, :].to_broadcast([P, D])).then_inc(row_loaded, 16)
            sp.dma_start(decay[:, :, :], decays).then_inc(decay_loaded, 16)
            sp.dma_start(pos_i[:, :], positions_2.to_broadcast([P, SEQ])).then_inc(rope_loaded, 16)
            phase("sc_out", two_halves(sc_w_out[0]))
            win = w_in_2[0]
            o_k, o_v, o_zr, o_uv, o_ug, o_zc, o_g = 0, 2 * D, 4 * D, 6 * D, 7 * D, 8 * D, 9 * D
            phase("glu", lambda i, j: (win, 0, i * 512 + ((o_uv if j % 2 else o_ug) + j // 2 * CC)))
            phase("qk", lambda i, j: (win, 0, i * 1024 + (o_k + j * CC)))
            phase("v", lambda i, j: (win, 0, i * 1024 + (o_v + j * CC)))
            phase("zret", lambda i, j: (win, 0, i * 1024 + (o_zr + j * CC)))
            phase("zconv", lambda i, j: (win, 0, o_zc + j * CC))
            phase("gates", lambda i, j: (win, 0, i * 1024 + (o_g + j * CC)))
            phase("conv_out", lambda i, j: (w_conv_out_2[0], 0, j * CC))
            sp.wait_ge(x_ready, 2 * NT)
            sp.dma_start(row[:, :], post_norm_g_2[0:1, :].to_broadcast([P, D])).then_inc(row_loaded, 16)
            phase("ret_out", two_halves(w_ret_out_2[0]))
            phase("w_out", lambda i, j: (w_out_2[0], 0, j * CC))
            for t in range(NT):
                sp.wait_ge(x_ready, 2 * NT + t + 1)
                sp.dma_start(out[0, t * P:(t + 1) * P, :], x[:, t, :]).then_inc(out_done, 16)
            sp.wait_ge(out_done, 16 * NT)

        VECS, SMALL = 16 * 12, 16 * 4

        @block.tensor
        def _(pe):
            def product(o, l_hi, l_lo, r_hi, r_lo, start, stop, open_bank):
                pe.matmul(o, l_hi, r_hi, start=start, stop=False, skip_group_check=open_bank)
                pe.matmul(o, l_hi, r_lo, start=False, stop=False, skip_group_check=open_bank)
                return pe.matmul(o, l_lo, r_hi, start=False, stop=stop, skip_group_check=open_bank)

            def chunk(g, j, b, a_hi, a_lo, k0, channels, half=None):
                s = j % 2
                pe.wait_ge(lo_ready, g + 1)
                if half is None:
                    pe.wait_ge(bank_free, g + 1)
                elif half == 0:
                    pe.wait_ge(bank_free, g + 2)
                for m in range(2):
                    o = bank(b)[:, m, :]
                    for k in range(KT):
                        first = k == 0 and (half is None or (half == 0 and m == 0))
                        last = k == KT - 1 and half != 0
                        mine = slice(m * P, (m + 1) * P)
                        if channels:
                            mm = product(o, w_hi[s][:, k, mine], w_lo[s][:, k, mine], a_hi[:, k0 + k, :], a_lo[:, k0 + k, :],
                                         first, last, half is not None)
                        else:
                            mm = product(o, a_hi[:, k0 + k, mine], a_lo[:, k0 + k, mine], w_hi[s][:, k, :], w_lo[s][:, k, :],
                                         first, last, half is not None)
                mm.then_inc(chunk_done, 1)

            def ada_piece(a, slot):
                pe.wait_ge(ada_ready[slot], a // 2 * 16 + 16 if isinstance(a, int) else a[0] * 32 + 16 * (a[1] // 2 + 1))
                o = psum[:, 7, a:a + 1] if isinstance(a, int) else psum[:, 7, bass.ds(a[0] * 4 + a[1], 1)]
                for k in range(KT):
                    mm = pe.matmul(o, ada[slot][:, k, :], par[:, 1, V_C + k:V_C + k + 1], start=(k == 0), stop=(k == KT - 1))
                mm.then_inc(ada_used, 1)

            def phase(name, a_hi, a_lo, channels, halves=False, with_ada=None):
                g0 = FIRST[name]
                if g0:
                    pe.wait_ge(bank_free, 4 + g0)

                def step(i):
                    for j in range(4):
                        g = i * 4 + (g0 + j)
                        if halves:
                            chunk(g, j, j // 2, a_hi, a_lo, j % 2 * KT, channels, j % 2)
                        else:
                            chunk(g, j, j, a_hi, a_lo, 0, channels)
                        if with_ada is not None:
                            ada_piece((i, with_ada + j), j % 2)
                loop(pe, COUNT[name] // 4, step)

            def pre_norm(n):
                pe.wait_ge(xn_ready, NT * (n + 1))
                for kp in range(KT // 2):
                    b = bank(4 + kp, P)
                    for k in range(2):
                        for t in range(NT):
                            mm = pe.transpose(b[:, 2 * k + t, :], xn[:, t, (2 * kp + k) * P:(2 * kp + k + 1) * P], ident)
                    mm.then_inc(turned, 1)
                pe.wait_ge(h_ready, KT // 2 * (n + 1))

            pe.wait_ge(vecs_loaded, VECS)
            for n in range(4):
                r = 120 if n == 3 else P
                mm = pe.transpose(bank(7, P)[:, n, 0:r], vecs[0:r, n, :], ident[0:r, 0:r])
            mm.then_inc(par_turned, 1)
            pe.wait_ge(par_ready, 1)
            pre_norm(0)
            phase("qkv", hT_hi, hT_lo, True, with_ada=0)
            phase("z", hT_hi, hT_lo, False, with_ada=COUNT["qkv"])

            pe.wait_ge(ba_lo_ready, 1)
            for k in range(KT):
                mm = product(psum[:, 6, 0:SEQ], ba_hi[:, k, :], ba_lo[:, k, :], hT_hi[:, k, :], hT_lo[:, k, :], k == 0, k == KT - 1, False)
            mm.then_inc(ba_done, 1)
            for n in range(KT):
                pe.wait_ge(sq_ready, n + 1)
                if n >= 2:
                    pe.wait_ge(l2_ln, n - 1)
                pe.matmul(psum[:, 4 + n % 2, :], ones, sq[n % 2].rearrange("p a n -> p (a n)"), start=True, stop=True).then_inc(l2_sum, 1)
            pe.wait_ge(g_ready, NT)
            for t in range(NT):
                mm = pe.transpose(bank(6, P)[:, t, :], bg[:, t * P:(t + 1) * P], ident)
            mm.then_inc(bg_turned, 1)
            pe.wait_ge(qkv_ready, COUNT["qkv"])
            pe.wait_ge(bank_free, 4 + FIRST["gdn_out"])
            for n in range(2 * NPAIR):
                t, q = n // NPAIR, n % NPAIR
                if n >= 2:
                    pe.wait_ge(vb_ready, n - 1)
                for a in range(HG):
                    mm = pe.transpose(bank(2 + n % 2, P)[:, a, :], qkvT[:, 2 * KT + HG * q + a, t * P:(t + 1) * P], ident)
                mm.then_inc(v_turned, 1)
            pe.wait_ge(vb_ready, 2 * NPAIR)
            pe.wait_ge(qk_ready, KT)
            for n in range(2):
                for a in range(HG):
                    mm = pe.transpose(bank(2 + n, P)[:, a, :], qkvT[:, KT + HG * n + a, 0:P], ident)
                mm.then_inc(k_turned, 1)
            pe.wait_ge(ktok_ready, 2)
            pe.wait_ge(mod_ready, 1)

            def prep(p, c, stage):
                n, cs = NT * p + c, slice(c * P, (c + 1) * P)
                if stage == 1:
                    if n:
                        pe.wait_ge(lt_ready, n)
                    for a in range(HG):
                        r = G_ROW + HG * p + a
                        mm = pe.matmul(bank(4, P)[:, a, :], ident[:, r:r + 1].to_broadcast([P, P]), bg[:, cs], start=True, stop=True)
                    mm.then_inc(grow_ready, 1)
                    if n:
                        pe.wait_ge(pt_ready, n)
                    for e in range(2):
                        k = qkvT[:, KT + 2 * p + e, cs]
                        pe.matmul(bank(5, P)[:, e, :], k, k, start=True, stop=True)
                        mm = pe.matmul(bank(5, P)[:, 2 + e, :], qkvT[:, 2 * p + e, cs], k, start=True, stop=True)
                    mm.then_inc(kq_ready, 1)
                if stage == 2:
                    pe.wait_ge(ap_ready, n + 1)
                    for a in range(HG):
                        pe.transpose(bank(4, P)[:, a, :], A[:, a, :], ident)
                        mm = pe.transpose(bank(5, P)[:, a, :], Di[:, a, :], ident)
                    mm.then_inc(ap_turned, 1)

            def level_w(p, l):
                for c in range(NT):
                    if l == 1:
                        pe.wait_ge(chain_ready, NT * p + c + 1)
                    else:
                        pe.wait_ge(t_ready[c], (NLEV - 2) * p + l - 1)
                    for a in range(HG):
                        mm = pe.matmul(bank(2 * c, P)[:, a, :], LT[p % 2][c][:, a, :], T[p % 2][c][:, a, :], start=True, stop=True)
                    mm.then_inc(w_done[c], 1)

            def level_ts(p, l):
                for c in range(NT):
                    done = (NLEV - 1) * p + l
                    pe.wait_ge(z_ready[c], done)
                    if done > 1:
                        pe.wait_ge(s_ready[c], done - 1)
                    for a in range(HG):
                        if l < NLEV - 1:
                            pe.matmul(bank(2 * c, P)[:, a, :], S[:, p, c, a, :], Z[c][:, a, :], start=True, stop=True)
                        mm = pe.matmul(bank(2 * c + 1, P)[:, a, :], Z[c][:, a, :], S[:, p, c, a, :], start=True, stop=True)
                    mm.then_inc(ts_done[c], 1)

            def apply(p, stage):
                b6, b7 = bank(6, P), bank(7, P)

                def four(b, left, right, done):
                    for a in range(HG):
                        mm = pe.matmul(b[:, a, :], left(a), right(a), start=True, stop=True)
                    mm.then_inc(done, 1)
                last_s = (NLEV - 1) * (p + 1)
                if stage == 1:
                    pe.wait_ge(s_ready[0], last_s)
                    if p:
                        pe.wait_ge(vn_ready, p)
                    four(b6, lambda a: S[:, p, 0, a, :], lambda a: vb[:, 0, HG * p + a, :], u_done)
                if stage == 2:
                    pe.wait_ge(u_ready, p + 1)
                    pe.wait_ge(kdec_ready, p + 1)
                    if p:
                        pe.wait_ge(o_ready, 2 * p)
                    four(b7, lambda a: PT[:, p, 0, a, :], lambda a: U[:, a, :], o0_done)
                    four(b6, lambda a: kdec[:, a, :], lambda a: U[:, a, :], s1_done)
                if stage == 3:
                    pe.wait_ge(s1_ready, p + 1)
                    four(b6, lambda a: qkvT[:, KT + (HG * p + a) // 2, P:2 * P], lambda a: s1[:, a, :], ks_done)
                    pe.wait_ge(o_ready, 2 * p + 1)
                    four(b7, lambda a: qkvT[:, (HG * p + a) // 2, P:2 * P], lambda a: s1[:, a, :], qs_done)
                if stage == 4:
                    pe.wait_ge(s_ready[1], last_s)
                    pe.wait_ge(r_ready, p + 1)
                    four(b6, lambda a: S[:, p, 1, a, :], lambda a: R[:, a, :], vn_done)
                if stage == 5:
                    pe.wait_ge(vn_ready, p + 1)
                    pe.wait_ge(qs_ready, p + 1)
                    four(b7, lambda a: PT[:, p, 1, a, :], lambda a: U[:, a, :], o1_done)

            for c in range(NT):
                prep(0, c, 1)
                prep(0, c, 2)
            for p in range(NPAIR + 1):
                for l in range(1, NLEV):
                    if p < NPAIR:
                        level_w(p, l)
                    if p >= 1:
                        apply(p - 1, l)
                    if p < NPAIR - 1:
                        prep(p + 1, (l - 1) // 3, (l - 1) % 3 + 1)
                    if p < NPAIR:
                        level_ts(p, l)

            def turn_y(src, b0, done, wait):
                for kp in range(KT):
                    wait(kp)
                    if kp >= 4:
                        pe.wait_ge(y_op_ready, done + kp - 3)
                    for k in range(2):
                        for t in range(NT):
                            mm = pe.transpose(bank(b0 + kp % 4, P)[:, 2 * k + t, :], src[:, t, (2 * kp + k) * P:(2 * kp + k + 1) * P], ident)
                    mm.then_inc(yT_turned, 1)

            turn_y(zo, 0, 0, lambda kp: pe.wait_ge(og_ready, NT))
            pe.wait_ge(y_op_ready, KT)
            phase("gdn_out", yT_hi, yT_lo, False, halves=True)

            pre_norm(1)
            phase("sc_in", hT_hi, hT_lo, True)
            pe.wait_ge(y_op_ready, 2 * KT)
            phase("sc_out", yT_hi, yT_lo, False, halves=True)

            pre_norm(2)
            phase("glu", hT_hi, hT_lo, True)
            phase("qk", hT_hi, hT_lo, True)
            phase("v", hT_hi, hT_lo, False)
            phase("zret", hT_hi, hT_lo, False)
            pe.wait_ge(bank_free, 4 + FIRST["zconv"])
            for h in range(RH):
                b = psum[:, 4 + h, :]
                for o, keys, queries in ((b[:, 0:SEQ], slice(0, P), slice(0, SEQ)), (b[:, SEQ:SEQ + P], slice(P, SEQ), slice(P, SEQ))):
                    for d in range(2):
                        mm = pe.matmul(o, qkT[:, KT + 2 * h + d, keys], qkT[:, 2 * h + d, queries], start=(d == 0), stop=(d == 1))
                mm.then_inc(sco_done, 1)
            for h in range(RH):
                pe.wait_ge(st_ready, h + 1)
                vh = slice(h * RDV, (h + 1) * RDV)
                for t in range(NT):
                    n = NT * h + t
                    if n >= 4:
                        pe.wait_ge(gn_ready, n - 3)
                    o = psum[:, n % 4, :]
                    mm = pe.matmul(o, st[:, h, t * P:(t + 1) * P], vt[:, 0, vh], start=True, stop=(t == 0))
                    if t:
                        mm = pe.matmul(o, st[:, h, SEQ:SEQ + P], vt[:, 1, vh], start=False, stop=True)
                    mm.then_inc(ro_done, 1)
            turn_y(vt, 4, 2 * KT, lambda kp: pe.wait_ge(rg_ready, NT * (kp // 2 + 1)))
            phase("zconv", hT_hi, hT_lo, True)
            phase("gates", hT_hi, hT_lo, True)
            pe.wait_ge(y_op_ready, 3 * KT)
            for n in range(KT):
                pe.wait_ge(cv_ready, n + 1)
                mm = pe.matmul(psum[:, 4, 0:SEQ], ones, cv[:, n, :], start=(n == 0), stop=(n == KT - 1))
            mm.then_inc(mean_done, 1)
            pe.wait_ge(gate_diag, 1)
            for k in range(KT):
                mm = pe.matmul(bank(6 + k // 4, P)[:, k % 4, :], ones, gdiag[:, k, :], start=True, stop=True)
            mm.then_inc(gate_row, 1)
            for n in range(KT):
                pe.wait_ge(a2_ready, n // 2 + 1)
                mm = pe.matmul(psum[:, 5, 0:SEQ], ones, a2[:, n, :], start=(n == 0), stop=(n == KT - 1))
            mm.then_inc(var_done, 1)
            pe.wait_ge(cop_ready, KT // 2)
            phase("conv_out", hT_hi, hT_lo, True)
            phase("ret_out", yT_hi, yT_lo, True, halves=True)
            pe.wait_ge(mop_ready, KT // 2)
            phase("w_out", hT_hi, hT_lo, False)

        @block.scalar
        def _(act):
            def split_hi(g0, i, j):
                if isinstance(i, int) and g0 + 4 * i + j >= CHUNKS:
                    return
                slot = j % RING
                act.wait_ge(raw_ready[slot], i * 16 + 16 * (g0 // 4 + j // 4 + 1))
                act.wait_ge(chunk_done, i * 4 + (g0 + j + 1))
                act.activation(w_hi[j % 2][:, :, :], raw[slot][:, :, :], ACT.Copy).then_inc(hi_ready, 1)

            def chunks(name, each=None):
                g0 = FIRST[name]

                def step(i):
                    for j in range(4):
                        split_hi(g0, i, j + 1)
                        if each is not None:
                            each(i, j, i * 4 + (g0 + j + 3))
                loop(act, COUNT[name] // 4, step)

            def square_sums(src, n, done):
                act.activation(junk[:, n % 2, :], src, ACT.Square, accum_out=ss[:, n:n + 1]).then_inc(done, 1)

            def pre_norm(n):
                for t in range(NT):
                    if n == 0:
                        act.wait_ge(x_loaded, 16)
                    else:
                        act.wait_ge(x_ready, NT * (n - 1) + t + 1)
                    square_sums(x[:, t, :], t, pre_ss)
                if n == 0:
                    split_hi(0, 0, 0)
                act.wait_ge(pre_ss, NT * (n + 1))
                act.activation(ms[:, 0:2], ss[:, 0:2], ACT.Sqrt, scale=1.0 / D, bias=eps_r[:, :]).then_inc(pre_std, 1)
                for kp in range(KT // 2):
                    act.wait_ge(hx_ready, KT // 2 * n + kp + 1)
                    act.activation(hT_hi[:, 2 * kp:2 * kp + 2, :], hx[:, 2 * kp:2 * kp + 2, :], ACT.Copy).then_inc(hhi_ready, 1)

            def post_norm(n, name):
                act.wait_ge(bank_free, 4 + FIRST[name] + COUNT[name])
                for t in range(NT):
                    square_sums(xn[:, t, :], 2 + t, post_ss)
                act.wait_ge(post_ss, NT * (n + 1))
                act.activation(ms[:, 2:4], ss[:, 2:4], ACT.Sqrt, scale=1.0 / D, bias=eps_r[:, :]).then_inc(post_std, 1)

            act.wait_ge(cleared, 1)
            pre_norm(0)
            act.wait_ge(par_ready, 1)

            def qkv_step(i):
                g0 = FIRST["qkv"]

                def silu(j):
                    act.wait_ge(bank_free, i * 4 + (4 + g0 + j + 1))
                    act.activation(qkvT[:, bass.ds(i * 8 + 2 * j, 2), :], cacc[j % 2][:, :, :], ACT.Silu).then_inc(qkv_ready, 1)
                for j in range(4):
                    split_hi(g0, i, j + 1)
                    act.wait_ge(chunk_done, i * 4 + (g0 + j + 3))
                    for m in range(2):
                        w = par[:, 0, bass.ds(i * 8 + ((GCONV - 1) * 32 + 2 * j + m), 1)]
                        a = act.activation(cacc[j % 2][:, m, :], bank(j)[:, m, :], ACT.Copy, scale=w)
                    a.then_inc(tap0, 1)
                    if j:
                        silu(j - 1)
                        act.wait_ge(qkv_ready, i * 4 + j)
                silu(3)
                act.wait_ge(qkv_ready, i * 4 + 4)
            loop(act, COUNT["qkv"] // 4, qkv_step)
            act.wait_ge(ba_loaded, 32)
            act.activation(ba_hi[:, :, :], ba_raw[:, :, :], ACT.Copy).then_inc(ba_hi_ready, 1)

            def z_out(i, j, done):
                act.wait_ge(chunk_done, done)
                act.activation(zo[:, :, bass.ds(i * 1024 + j * CC, CC)], bank(j), ACT.Silu).then_inc(bank_free, 1)
            chunks("z", z_out)

            gr = slice(G_ROW, G_ROW + VH)
            act.wait_ge(small_loaded, SMALL)
            act.wait_ge(ba_done, 1)
            act.wait_ge(cleared, 2)
            act.activation(bg[0:VH, :], psum[0:VH, 6, 0:SEQ], ACT.Sigmoid).then_inc(beta_ready, 1)
            act.activation(acols[gr, 2:3], acols[gr, 0:1], ACT.Exp).then_inc(gate_a, 1)
            act.wait_ge(gate_v, 2)
            act.activation(gl[gr, :], gl[gr, :], ACT.Exp, scale=-1.0).then_inc(gate_a, 1)
            act.wait_ge(gate_a, 2)
            act.activation(gs[gr, :], gl[gr, :], ACT.Ln, bias=1.0).then_inc(gate_a, 1)
            for n in range(KT):
                act.wait_ge(l2_sum, n + 1)
                if n >= 2:
                    act.wait_ge(qk_ready, n - 1)
                f = rn[n % 2].rearrange("p a n -> p (a n)")
                act.activation(f, psum[:, 4 + n % 2, :], ACT.Ln, bias=eps_r[:, :]).then_inc(l2_ln, 1)
                act.wait_ge(l2_ln, n + 1)
                act.activation(f, f, ACT.Exp, scale=-0.5).then_inc(l2_r, 1)
            act.wait_ge(bgt_ready, 1)
            act.activation(eg[:, :, :], bgt[:, :, gr], ACT.Exp).then_inc(eg_ready, 1)

            def prep(p, c, stage):
                n = NT * p + c
                if stage == 1:
                    act.wait_ge(d_ready, n + 1)
                    act.activation(E[:, :, :], E[:, :, :], ACT.Exp, scale=-1.0).then_inc(e_ready, 1)
                    if c == 0:
                        act.wait_ge(wd_sub, p + 1)
                        w = wdec[:, HG * p:HG * (p + 1)]
                        act.activation(w, w, ACT.Exp).then_inc(wd_ready, 1)
                if stage == 3:
                    act.wait_ge(ap_turned, n + 1)
                    act.activation(PT[:, p, c, :, :], bank(5, P), ACT.Copy).then_inc(pt_ready, 1)

            def level(p, l):
                for c in range(NT):
                    act.wait_ge(ts_done[c], (NLEV - 1) * p + l)
                    if l < NLEV - 1:
                        act.activation(T[p % 2][c][:, :, :], bank(2 * c, P), ACT.Copy).then_inc(t_ready[c], 1)

            def apply(p, stage):
                if stage == 1:
                    act.wait_ge(u_done, p + 1)
                    act.activation(U[:, :, :], bank(6, P), ACT.Copy).then_inc(u_ready, 1)
                if stage == 2:
                    act.wait_ge(o0_done, p + 1)
                    act.activation(osq[:, :, :], bank(7, P), ACT.Square).then_inc(osq_ready, 1)
                    act.wait_ge(s1_done, p + 1)
                    act.activation(s1[:, :, :], bank(6, P), ACT.Copy).then_inc(s1_ready, 1)
                if stage == 3:
                    act.wait_ge(qs_done, p + 1)
                    for a in range(HG):
                        h = HG * p + a
                        i = act.activation(qS[:, a, :], bank(7, P)[:, a, :], ACT.Copy, scale=eg[:, 1, h:h + 1])
                    i.then_inc(qs_ready, 1)
                if stage == 4:
                    act.wait_ge(vn_done, p + 1)
                    act.activation(U[:, :, :], bank(6, P), ACT.Copy).then_inc(vn_ready, 1)
                if stage == 5:
                    act.wait_ge(o1_ready, p + 1)
                    act.activation(osq[:, :, :], qS[:, :, :], ACT.Square).then_inc(osq_ready, 1)

            for c in range(NT):
                prep(0, c, 1)
                prep(0, c, 3)
            for p in range(NPAIR + 1):
                for l in range(1, NLEV):
                    if p >= 1:
                        apply(p - 1, l)
                    if p < NPAIR - 1:
                        prep(p + 1, (l - 1) // 3, (l - 1) % 3 + 1)
                    if p < NPAIR:
                        level(p, l)
            act.wait_ge(o_ready, 2 * NPAIR)
            act.activation(o_rs[:, :, :], o_ss[:, :, :], ACT.Sqrt, scale=1.0 / HD, bias=eps_r[:, :]).then_inc(o_std, 1)

            def turn_y(b0, turns):
                for kp in range(KT):
                    act.wait_ge(yT_turned, turns + kp + 1)
                    act.activation(yT_hi[:, 2 * kp:2 * kp + 2, :], bank(b0 + kp % 4), ACT.Copy).then_inc(yhi_ready, 1)

            turn_y(0, 0)

            def y_halves(i, j, done):
                if j % 2:
                    act.wait_ge(chunk_done, done)
                    act.activation(xn[:, :, bass.ds(i * 512 + j // 2 * CC, CC)], bank(j // 2), ACT.Copy).then_inc(bank_free, 2)
            chunks("gdn_out", y_halves)
            post_norm(0, "gdn_out")
            pre_norm(1)

            def sc_each(i, j, done):
                g = FIRST["sc_in"]
                if j == 0:
                    act.wait_ge(chunk_done, done)
                    act.activation(sc_u[:, :, :], bank(0), ACT.Copy).then_inc(sc_u_ready, 1)
                if j == 2:
                    act.wait_ge(bank_free, i * 4 + (4 + g + 2))
                    for m in range(2):
                        w = par[:, 1, bass.ds(i * 2 + (V_SC + (SCONV - 1) * 16 + m), 1)]
                        a = act.activation(sc_v[:, m, :], sc_cu[:, m, :], ACT.Copy, scale=w)
                    a.then_inc(sc_v0, 1)
                if j == 3:
                    act.wait_ge(chunk_done, done)
                    act.activation(sc_z[:, :, :], bank(3), ACT.Silu).then_inc(sc_z_ready, 1)
                    act.wait_ge(bank_free, i * 4 + (4 + g + 4))
                    act.activation(yT_hi[:, bass.ds(i * 2, 2), :], sc_yz[:, :, :], ACT.Copy).then_inc(yhi_ready, 1)
            chunks("sc_in", sc_each)
            chunks("sc_out", y_halves)
            post_norm(1, "sc_out")
            pre_norm(2)

            act.wait_ge(ang_ready, 1)
            act.activation(trig[:, :, :], turn[:, :, :], ACT.Sin).then_inc(trig_ready, 1)

            def glu_each(i, j, done):
                if j % 2 == 0:
                    act.wait_ge(chunk_done, done)
                    act.activation((glu, rp1)[j // 2][:, :, :], bank(j), ACT.Sigmoid).then_inc(glu_ready, 1)
            chunks("glu", glu_each)
            chunks("qk")

            def tokens_out(dst, func):
                def each(i, j, done):
                    act.wait_ge(chunk_done, done)
                    act.activation(dst[:, :, bass.ds(i * 1024 + j * CC, CC)], bank(j), func).then_inc(bank_free, 1)
                return each

            def channels_out(dst, func):
                def each(i, j, done):
                    act.wait_ge(chunk_done, done)
                    act.activation(dst[:, bass.ds(i * 8 + 2 * j, 2), :], bank(j), func).then_inc(bank_free, 1)
                return each
            chunks("v", tokens_out(vt, ACT.Copy))
            chunks("zret", tokens_out(zr, ACT.Silu))
            for h in range(RH):
                act.wait_ge(gn_step, 2 * NT * (h + 1))
                act.activation(grs[:, :], gmv[:, :, 1], ACT.Sqrt, bias=eps_n[:, :]).then_inc(gn_std, 1)
            act.wait_ge(rg_ready, NT * RH)
            turn_y(4, KT)
            chunks("zconv", channels_out(zc, ACT.Silu))
            chunks("gates", channels_out(gab, ACT.Sigmoid))
            for q in range(KT // 2):
                pair = slice(2 * q, 2 * q + 2)
                act.wait_ge(xc_ready, q + 1)
                act.activation(a2[:, pair, :], cv[:, pair, :], ACT.Square).then_inc(a2_ready, 1)
            act.wait_ge(var_done, 1)
            act.activation(lnm[:, 1, :], psum[:, 5, 0:SEQ], ACT.Ln, scale=1.0 / D, bias=eps_n[:, :]).then_inc(ln_step, 1)
            act.wait_ge(ln_step, 1)
            act.activation(lnm[:, 1, :], lnm[:, 1, :], ACT.Exp, scale=-0.5).then_inc(ln_step, 1)
            for n in range(KT):
                act.wait_ge(lns_ready, n // 2 + 1)
                act.activation(cv[:, n, :], cv[:, n, :], ACT.Silu, scale=par[:, 1, V_LG + n:V_LG + n + 1],
                               bias=par[:, 1, V_LB + n:V_LB + n + 1]).then_inc(lna_ready, 1)
            for q in range(KT // 2):
                pair = slice(2 * q, 2 * q + 2)
                act.wait_ge(lnz_ready, q + 1)
                act.activation(hT_hi[:, pair, :], cv[:, pair, :], ACT.Copy).then_inc(chi_ready, 1)
            chunks("conv_out")

            def merged(i, j, done):
                if j % 2:
                    b = i * 2 + j // 2
                    act.wait_ge(mg_ready, b + 1)
                    act.activation(hT_hi[:, bass.ds(b * 2, 2), :], rp2[:, :, :], ACT.Copy).then_inc(mhi_ready, 1)
            chunks("ret_out", merged)

            def y_out(i, j, done):
                act.wait_ge(chunk_done, done)
                act.activation(xn[:, :, j * CC:(j + 1) * CC], bank(j), ACT.Copy).then_inc(bank_free, 1)
            chunks("w_out", y_out)
            post_norm(2, "w_out")

        @block.gpsimd
        def _(pool):
            pool.memset(ba_raw[:, :, :], 0.0).then_inc(padded, 1)
            for n in range(KT):
                pool.wait_ge(qkv_ready, n + 1)
                if n >= 2:
                    pool.wait_ge(l2_sum, n - 1)
                qk = qkvT[:, 2 * n:2 * n + 2, :]
                pool.tensor_tensor(sq[n % 2][:, :, :], qk, qk, ALU.mult).then_inc(sq_ready, 1)
            pool.wait_ge(bank_free, 4 + FIRST["gdn_out"])
            pool.wait_ge(small_loaded, SMALL)
            for t in range(NT):
                z = zo[:, t, :].rearrange("p (h d) -> p h d", d=HD)
                pool.tensor_tensor(z, z, heads(nw_row[:, :], VH), ALU.mult).then_inc(zn_ready, 1)

            def prep(p, c, stage):
                n = NT * p + c
                if stage == 1:
                    pool.wait_ge(e_ready, n + 1)
                    if n:
                        pool.wait_ge(ap_turned, n)
                    pool.tensor_tensor(Di[:, :, :], E[:, :, :], heads(const[:, C_INC, :], HG), ALU.mult)
                    pool.tensor_tensor(E[:, :, :], E[:, :, :], heads(const[:, C_LOW, :], HG), ALU.mult).then_inc(masked, 1)
                if stage == 3:
                    pool.wait_ge(ap_turned, n + 1)
                    pool.tensor_tensor(A[:, :, :], A[:, :, :], heads(ident, HG), ALU.add).then_inc(l_ready, 1)
                    pool.wait_ge(l_ready, n + 1)
                    pool.tensor_tensor(T[p % 2][c][:, :, :], A[:, :, :], heads(const[:, C_M0, :], HG), ALU.mult)
                    pool.wait_ge(lt_ready, n + 1)
                    pool.tensor_tensor(S[:, p, c, :, :], LT[p % 2][c][:, :, :], heads(const[:, C_M0T, :], HG), ALU.mult).then_inc(chain_ready, 1)

            def apply(p, stage):
                if stage == 1:
                    pool.wait_ge(wd_ready, p + 1)
                    pool.wait_ge(ktok_ready, 2)
                    if p:
                        pool.wait_ge(s1_done, p)
                    for a in range(HG):
                        h = HG * p + a
                        i = pool.tensor_scalar(kdec[:, a, :], ktok[:, h // 2, :], wdec[:, h:h + 1], None, ALU.mult)
                    i.then_inc(kdec_ready, 1)

            for c in range(NT):
                prep(0, c, 1)
                prep(0, c, 3)
            for p in range(NPAIR + 1):
                for l in range(1, NLEV):
                    if p >= 1:
                        apply(p - 1, l)
                    if p < NPAIR - 1:
                        prep(p + 1, (l - 1) // 3, (l - 1) % 3 + 1)
            for h in range(RH):
                for t in range(NT):
                    n = NT * h + t
                    pool.wait_ge(gn_ready, n + 1)
                    vh = slice(h * RDV, (h + 1) * RDV)
                    pool.tensor_tensor(vt[:, t, vh], og[t][:, :], zr[:, t, vh], ALU.mult).then_inc(rg_ready, 1)

        @block.vector
        def _(dve):
            def part_lo(o, whole, hi):
                return dve.tensor_tensor(o, whole, hi.bitcast(F32), ALU.subtract)

            def split_lo(g0, i, j):
                if isinstance(i, int) and g0 + 4 * i + j >= CHUNKS:
                    return
                dve.wait_ge(hi_ready, i * 4 + (g0 + j + 1))
                part_lo(w_lo[j % 2][:, :, :], raw[j % RING][:, :, :], w_hi[j % 2][:, :, :]).then_inc(lo_ready, 1)

            def chunks(name, each=None, unroll=False):
                g0 = FIRST[name]

                def step(i):
                    for j in range(4):
                        split_lo(g0, i, j + 1)
                        if each is not None:
                            each(i, j, i * 4 + (g0 + j + 3))
                if unroll:
                    for i in range(COUNT[name] // 4):
                        step(i)
                else:
                    loop(dve, COUNT[name] // 4, step)

            def pre_norm(n, gain, shift):
                dve.wait_ge(pre_std, n + 1)
                dve.reciprocal(rstd[:, 0:2], ms[:, 0:2]).then_inc(pre_rstd, 1)
                dve.wait_ge(pre_rstd, n + 1)
                for t in range(NT):
                    dve.tensor_scalar(xn[:, t, :], x[:, t, :], rstd[:, t:t + 1], None, ALU.mult).then_inc(xn_ready, 1)
                for kp in range(KT // 2):
                    dve.wait_ge(turned, KT // 2 * n + kp + 1)
                    for k in range(2):
                        kk = 2 * kp + k
                        i = dve.tensor_scalar(hx[:, kk, :], bank(4 + kp)[:, k, :], gain(kk), shift(kk), ALU.mult, ALU.add)
                    i.then_inc(hx_ready, 1)
                for kp in range(KT // 2):
                    pair = slice(2 * kp, 2 * kp + 2)
                    dve.wait_ge(hhi_ready, KT // 2 * n + kp + 1)
                    part_lo(hT_lo[:, pair, :], hx[:, pair, :], hT_hi[:, pair, :]).then_inc(h_ready, 1)

            def post_norm(n):
                dve.wait_ge(post_std, n + 1)
                dve.reciprocal(rstd[:, 2:4], ms[:, 2:4]).then_inc(post_rstd, 1)
                dve.wait_ge(post_rstd, n + 1)
                dve.wait_ge(row_loaded, 16 * (n + 1))
                for t in range(NT):
                    dve.scalar_tensor_tensor(out=xn[:, t, :], in0=xn[:, t, :], scalar=rstd[:, 2 + t:3 + t], in1=row[:, :],
                                             op0=ALU.mult, op1=ALU.mult).then_inc(post_scaled, 1)
                for t in range(NT):
                    dve.wait_ge(post_scaled, NT * n + t + 1)
                    dve.tensor_tensor(x[:, t, :], x[:, t, :], xn[:, t, :], ALU.add).then_inc(x_ready, 1)

            def col(v, k):
                return par[:, 1, v + k:v + k + 1]

            dve.memset(eps_r[:, :], RMS_EPS)
            dve.memset(zeros[:, :], 0.0).then_inc(bank_free, 4)
            dve.memset(eps_n[:, :], NORM_EPS).then_inc(cleared, 1)
            dve.memset(bg[:, :], 0.0).then_inc(cleared, 1)
            dve.memset(gain2[:, :], 0.0).then_inc(chunk_done, 2)
            dve.wait_ge(par_turned, 1)
            dve.tensor_copy(par[:, :, :].rearrange("p a n -> p (a n)")[:, 0:504], psum[:, 7, 0:504]).then_inc(par_ready, 1)
            dve.wait_ge(hi_ready, 1)
            part_lo(w_lo[0][:, :, :], raw[0][:, :, :], w_hi[0][:, :, :]).then_inc(lo_ready, 1)
            dve.wait_ge(par_ready, 1)
            pre_norm(0, lambda k: col(V_PRE, k), lambda k: zeros[:, k:k + 1])

            def taps(i, j, done):
                g0 = FIRST["qkv"]
                dve.wait_ge(tap0, i * 4 + (g0 + j + 1))
                n = 0
                for tap in range(GCONV - 2, -1, -1):
                    s = GCONV - 1 - tap
                    for m in range(2):
                        if n >= 2:
                            dve.wait_ge(tap_step, i * 20 + (5 * j + n - 1))
                        o = cacc[j % 2][:, m, s:SEQ]
                        a = dve.scalar_tensor_tensor(out=o, in0=bank(j)[:, m, 0:SEQ - s],
                                                     scalar=par[:, 0, bass.ds(i * 8 + (tap * 32 + 2 * j + m), 1)],
                                                     in1=o, op0=ALU.mult, op1=ALU.add)
                        n += 1
                        if n < 6:
                            a.then_inc(tap_step, 1)
                        else:
                            a.then_inc(bank_free, 1)
            chunks("qkv", taps)
            dve.wait_ge(ba_hi_ready, 1)
            part_lo(ba_lo[:, :, :], ba_raw[:, :, :], ba_hi[:, :, :]).then_inc(ba_lo_ready, 1)
            chunks("z")

            dve.wait_ge(ada_used, ADA_PIECES)
            dve.tensor_tensor(mod[:, :], psum[:, 7, 0:3 * KT], par[:, 1, V_BADA:V_BADA + 3 * KT], ALU.add).then_inc(mod_ready, 1)
            dve.wait_ge(mod_ready, 1)
            dve.scalar_tensor_tensor(out=gain2[:, :], in0=mod[:, KT:2 * KT], scalar=1.0, in1=par[:, 1, V_PRE2:V_PRE2 + KT],
                                     op0=ALU.add, op1=ALU.mult).then_inc(gain2_ready, 1)
            gr = slice(G_ROW, G_ROW + VH)
            dve.wait_ge(small_loaded, SMALL)
            dve.wait_ge(ba_done, 1)
            dve.wait_ge(beta_ready, 1)
            dve.tensor_scalar(gz[gr, :], psum[gr, 6, 0:SEQ], acols[gr, 1:2], None, ALU.add).then_inc(gate_v, 1)
            dve.wait_ge(gate_v, 1)
            dve.scalar_tensor_tensor(out=gl[gr, :], in0=gz[gr, :], scalar=-1.0, in1=gz[gr, :], op0=ALU.mult, op1=ALU.max).then_inc(gate_v, 1)
            dve.wait_ge(gate_a, 3)
            dve.scalar_tensor_tensor(out=gs[gr, :], in0=gz[gr, :], scalar=0.0, in1=gs[gr, :], op0=ALU.max, op1=ALU.add).then_inc(gate_v, 1)
            dve.wait_ge(gate_v, 3)
            dve.tensor_scalar(gz[gr, :], gs[gr, :], acols[gr, 2:3], -1.0, ALU.mult, ALU.mult).then_inc(gate_v, 1)
            dve.wait_ge(gate_v, 4)
            for t in range(NT):
                cs = slice(t * P, (t + 1) * P)
                dve.tensor_tensor_scan(bg[gr, cs], const[gr, C_ONE, :], gz[gr, cs], 0.0, ALU.mult, ALU.add).then_inc(g_ready, 1)
            for n in range(KT):
                dve.wait_ge(l2_r, n + 1)
                qk = qkvT[:, 2 * n:2 * n + 2, :]
                dve.scalar_tensor_tensor(out=qk, in0=qk, scalar=HD ** -0.5 if n < KT // 2 else 1.0, in1=rn[n % 2][:, :, :],
                                         op0=ALU.mult, op1=ALU.mult).then_inc(qk_ready, 1)
            dve.wait_ge(bg_turned, 1)
            dve.tensor_copy(bgt[:, :, :], bank(6, P)[:, 0:NT, :]).then_inc(bgt_ready, 1)
            dve.wait_ge(bgt_ready, 1)
            dve.wait_ge(eg_ready, 1)
            dve.scalar_tensor_tensor(out=nbeg[:, :, :], in0=bgt[:, :, 0:VH], scalar=-1.0, in1=eg[:, :, :], op0=ALU.mult,
                                     op1=ALU.mult).then_inc(nbeg_ready, 1)
            for n in range(2 * NPAIR):
                t, q = n // NPAIR, n % NPAIR
                dve.wait_ge(v_turned, n + 1)
                for a in range(HG):
                    h = HG * q + a
                    i = dve.tensor_scalar(vb[:, t, h, :], bank(2 + n % 2, P)[:, a, :], bgt[:, t, h:h + 1], None, ALU.mult)
                i.then_inc(vb_ready, 1)
            for n in range(2):
                dve.wait_ge(k_turned, n + 1)
                dve.tensor_copy(ktok[:, HG * n:HG * (n + 1), :], bank(2 + n, P)).then_inc(ktok_ready, 1)

            def prep(p, c, stage):
                n = NT * p + c
                if stage == 1:
                    dve.wait_ge(grow_ready, n + 1)
                    for a in range(HG):
                        g = G_ROW + HG * p + a
                        i = dve.tensor_scalar(E[:, a, :], bank(4, P)[:, a, :], bgt[:, c, g:g + 1], 0.0, ALU.subtract, ALU.max)
                    i.then_inc(d_ready, 1)
                    if c == 0:
                        g = G_ROW + HG * p
                        dve.tensor_tensor(wdec[:, HG * p:HG * (p + 1)], bank(4, P)[:, :, P - 1], bgt[:, 0, g:g + HG], ALU.subtract).then_inc(wd_sub, 1)
                if stage == 2:
                    dve.wait_ge(kq_ready, n + 1)
                    dve.wait_ge(masked, n + 1)
                    if n:
                        dve.wait_ge(chain_ready, n)
                    for a in range(HG):
                        h = HG * p + a
                        dve.scalar_tensor_tensor(out=A[:, a, :], in0=bank(5, P)[:, a // 2, :], scalar=bgt[:, c, h:h + 1],
                                                 in1=E[:, a, :], op0=ALU.mult, op1=ALU.mult)
                    d4 = Di[:, :, :].rearrange("p (e r) n -> p e r n", r=2)
                    q4 = bank(5, P)[:, 2:4, :].rearrange("p e (r n) -> p e r n", r=1).to_broadcast([P, 2, 2, P])
                    dve.tensor_tensor(d4, q4, d4, ALU.mult).then_inc(ap_ready, 1)
                if stage == 3:
                    dve.wait_ge(ap_turned, n + 1)
                    dve.tensor_tensor(LT[p % 2][c][:, :, :], bank(4, P), heads(ident, HG), ALU.add).then_inc(lt_ready, 1)

            def level_z(p, l):
                for c in range(NT):
                    dve.wait_ge(w_done[c], (NLEV - 1) * p + l)
                    dve.tensor_tensor(Z[c][:, :, :], bank(2 * c, P), heads(const[:, C_MASK + l - 1, :], HG), ALU.mult).then_inc(z_ready[c], 1)

            def level_s(p, l):
                for c in range(NT):
                    dve.wait_ge(ts_done[c], (NLEV - 1) * p + l)
                    dve.tensor_copy(S[:, p, c, :, :], bank(2 * c + 1, P)).then_inc(s_ready[c], 1)

            def gated(p, t, o):
                hs = slice(HG * p, HG * (p + 1))
                dve.wait_ge(osq_ready, 2 * p + t + 1)
                dve.tensor_reduce(o_ss[:, t, hs], osq[:, :, :], AX_X, ALU.add)
                z = zo[:, t, HG * p * HD:HG * (p + 1) * HD].rearrange("p (h d) -> p h d", d=HD)
                dve.tensor_tensor(z, o, z, ALU.mult).then_inc(o_ready, 1)

            def apply(p, stage):
                if stage == 2:
                    dve.wait_ge(zn_ready, NT)
                    gated(p, 0, bank(7, P))
                if stage == 3:
                    dve.wait_ge(ks_done, p + 1)
                    for a in range(HG):
                        h = HG * p + a
                        i = dve.scalar_tensor_tensor(out=R[:, a, :], in0=bank(6, P)[:, a, :], scalar=nbeg[:, 1, h:h + 1],
                                                     in1=vb[:, 1, h, :], op0=ALU.mult, op1=ALU.add)
                    i.then_inc(r_ready, 1)
                if stage == 5:
                    dve.wait_ge(o1_done, p + 1)
                    dve.tensor_tensor(qS[:, :, :], bank(7, P), qS[:, :, :], ALU.add).then_inc(o1_ready, 1)
                    dve.wait_ge(o1_ready, p + 1)
                    gated(p, 1, qS[:, :, :])

            for c in range(NT):
                for stage in (1, 2, 3):
                    prep(0, c, stage)
            for p in range(NPAIR + 1):
                for l in range(1, NLEV):
                    if p < NPAIR:
                        level_z(p, l)
                    if p >= 1:
                        apply(p - 1, l)
                    if p < NPAIR - 1:
                        prep(p + 1, (l - 1) // 3, (l - 1) % 3 + 1)
                    if p < NPAIR:
                        level_s(p, l)
            dve.wait_ge(o_std, 1)
            dve.reciprocal(o_rs[:, :, :], o_rs[:, :, :]).then_inc(o_rstd, 1)
            dve.wait_ge(o_rstd, 1)
            dve.wait_ge(o_ready, 2 * NPAIR)
            for t in range(NT):
                z = zo[:, t, :].rearrange("p (h d) -> p h d", d=HD)
                r = o_rs[:, t, :].rearrange("p (h d) -> p h d", d=1).to_broadcast([P, VH, HD])
                dve.tensor_tensor(z, z, r, ALU.mult).then_inc(og_ready, 1)

            def turn_y(b0, done):
                for kp in range(KT):
                    pair = slice(2 * kp, 2 * kp + 2)
                    dve.wait_ge(yhi_ready, done + kp + 1)
                    part_lo(yT_lo[:, pair, :], bank(b0 + kp % 4), yT_hi[:, pair, :]).then_inc(y_op_ready, 1)

            turn_y(0, 0)
            chunks("gdn_out")
            post_norm(0)
            pre_norm(1, lambda k: col(V_PRE + KT, k), lambda k: zeros[:, k:k + 1])

            def sc_each(i, j, done):
                g = FIRST["sc_in"]
                if j == 1:
                    dve.wait_ge(chunk_done, done)
                    dve.wait_ge(sc_u_ready, i + 1)
                    dve.tensor_tensor(sc_cu[:, :, :], bank(1), sc_u[:, :, :], ALU.mult).then_inc(bank_free, 2)
                if j == 2:
                    dve.wait_ge(sc_v0, i + 1)
                    n = 0
                    for tap in range(SCONV - 2, -1, -1):
                        s = SCONV - 1 - tap
                        for m in range(2):
                            if n >= 2:
                                dve.wait_ge(sc_step, i * 4 + (n - 1))
                            o = sc_v[:, m, s:SEQ]
                            dve.scalar_tensor_tensor(out=o, in0=sc_cu[:, m, 0:SEQ - s],
                                                     scalar=par[:, 1, bass.ds(i * 2 + (V_SC + tap * 16 + m), 1)],
                                                     in1=o, op0=ALU.mult, op1=ALU.add).then_inc(sc_step, 1)
                            n += 1
                    dve.wait_ge(chunk_done, done)
                    dve.wait_ge(sc_step, i * 4 + 4)
                    dve.tensor_tensor(sc_y[:, :, :], bank(2), sc_v[:, :, :], ALU.mult).then_inc(bank_free, 1)
                if j == 3:
                    dve.wait_ge(sc_z_ready, i + 1)
                    dve.wait_ge(bank_free, i * 4 + (4 + g + 3))
                    dve.tensor_tensor(sc_yz[:, :, :], sc_y[:, :, :], sc_z[:, :, :], ALU.mult).then_inc(bank_free, 1)
                    dve.wait_ge(yhi_ready, i + (KT + 1))
                    pair = bass.ds(i * 2, 2)
                    part_lo(yT_lo[:, pair, :], sc_yz[:, :, :], yT_hi[:, pair, :]).then_inc(y_op_ready, 1)
            chunks("sc_in", sc_each)
            chunks("sc_out")
            pi = math.pi
            c1 = 6.28125
            c2 = float(np.float32(np.float32((2 * pi - c1) * 2 ** 20).astype(np.int32) / np.float32(2 ** 20)))
            c3 = 2 * pi - c1 - c2
            magic = 1.5 * 2.0 ** 23
            cos_t, sin_t = turn[:, 0, :], turn[:, 1, :]
            steps = [0]

            def angle(i):
                steps[0] += 1
                i.then_inc(ang_step, 1)
                dve.wait_ge(ang_step, steps[0])
            dve.wait_ge(rope_loaded, 16)
            angle(dve.tensor_copy(ang[:, :], pos_i[:, :]))
            angle(dve.tensor_scalar(ang[:, :], ang[:, :], freq[:, :], None, ALU.mult))
            angle(dve.tensor_scalar(cos_t, ang[:, :], 1.0 / (2 * pi), magic, ALU.mult, ALU.add))
            angle(dve.tensor_scalar(cos_t, cos_t, magic, None, ALU.subtract))
            for c in (c1, c2, c3):
                angle(dve.scalar_tensor_tensor(out=ang[:, :], in0=cos_t, scalar=-c, in1=ang[:, :], op0=ALU.mult, op1=ALU.add))
            lim = float(np.nextafter(np.float32(pi), np.float32(0)))
            angle(dve.tensor_scalar(sin_t, ang[:, :], lim, -lim, ALU.min, ALU.max))
            angle(dve.tensor_scalar(ang[:, :], ang[:, :], pi / 2, None, ALU.add))
            angle(dve.tensor_scalar(cos_t, ang[:, :], pi, -2 * pi, ALU.is_gt, ALU.mult))
            angle(dve.tensor_tensor(cos_t, cos_t, ang[:, :], ALU.add))
            dve.tensor_scalar(cos_t, cos_t, lim, -lim, ALU.min, ALU.max).then_inc(ang_ready, 1)
            post_norm(1)
            dve.wait_ge(gain2_ready, 1)
            pre_norm(2, lambda k: gain2[:, k:k + 1], lambda k: mod[:, k:k + 1])
            dve.memset(aP[:, :, 0:CPAD], 0.0).then_inc(padded, 1)

            def glu_each(i, j, done):
                if j % 2:
                    dve.wait_ge(chunk_done, done)
                    dve.wait_ge(glu_ready, i * 2 + (j // 2 + 1))
                    dve.tensor_tensor(aP[:, bass.ds(i * 4 + j // 2 * 2, 2), CPAD:CPAD + SEQ], bank(j), (glu, rp1)[j // 2][:, :, :],
                                      ALU.mult).then_inc(bank_free, 2)
            chunks("glu", glu_each)
            dve.wait_ge(trig_ready, 1)
            cos2, sin2 = (trig[:, s, :].rearrange("p (a n) -> p a n", a=1).to_broadcast([P, 2, SEQ]) for s in range(2))

            def rotate(i, j, done):
                dve.wait_ge(chunk_done, done)
                dve.tensor_tensor(rp1[:, :, :], bank(j), cos2, ALU.mult)
                dve.tensor_tensor(rp2[:, :, :], bank(j), sin2, ALU.mult).then_inc(bank_free, 1)
                dve.wait_ge(bank_free, i * 4 + (4 + FIRST["qk"] + j + 1))
                dve.tensor_tensor(qkT[:, bass.ds(i * 8 + 2 * j, 1), :], rp1[:, 0:1, :], rp2[:, 1:2, :], ALU.subtract)
                dve.tensor_tensor(qkT[:, bass.ds(i * 8 + (2 * j + 1), 1), :], rp2[:, 0:1, :], rp1[:, 1:2, :], ALU.add).then_inc(rp_step, 1)
                dve.wait_ge(rp_step, i * 4 + (j + 1))
            chunks("qk", rotate)

            def conv_op(n, tap):
                def w(j):
                    return par[:, 2 + j // 16, j % 16 * KT + n:j % 16 * KT + n + 1]
                step = CW * n + tap
                if 2 <= tap < CW:
                    dve.wait_ge(cv_step, step - 1)
                if tap == 1 and n:
                    dve.wait_ge(cv_ready, n)
                o = cvo[:, :] if tap % 2 else cv[:, n, :]
                if tap < CW:
                    src = aP[:, n, tap:tap + SEQ]
                if tap == CW:
                    dve.wait_ge(cv_step, step)
                    dve.tensor_tensor(cv[:, n, :], cv[:, n, :], cvo[:, :], ALU.add).then_inc(cv_ready, 1)
                elif tap == 0:
                    dve.tensor_scalar(o, src, w(0), col(V_CB, n), ALU.mult, ALU.add).then_inc(cv_step, 1)
                elif tap == 1:
                    dve.tensor_scalar(o, src, w(1), None, ALU.mult).then_inc(cv_step, 1)
                else:
                    dve.scalar_tensor_tensor(out=o, in0=src, scalar=w(tap), in1=o, op0=ALU.mult, op1=ALU.add).then_inc(cv_step, 1)

            def conv_part(first_tile, per_step):
                def each(i, j, done):
                    for q in range(8 * per_step):
                        n = 8 * per_step * j + q
                        conv_op(first_tile + per_step * i + n // 32, n % 32)
                return each
            dve.wait_ge(padded, 2)
            dve.wait_ge(bank_free, 4 + FIRST["qk"])
            chunks("v", conv_part(0, 1), unroll=True)
            chunks("zret", conv_part(2, 1), unroll=True)
            dve.wait_ge(decay_loaded, 16)
            for h in range(RH):
                dve.wait_ge(sco_done, h + 1)
                dve.tensor_tensor(st[:, h, :], psum[:, 4 + h, 0:3 * P], decay[:, h, :], ALU.mult).then_inc(st_ready, 1)
            for h in range(RH):
                for t in range(NT):
                    n = NT * h + t
                    dve.wait_ge(ro_done, n + 1)
                    dve.bn_stats(gst[:, t, :], psum[:, n % 4, :]).then_inc(gn_step, 1)
                    dve.wait_ge(gn_step, 2 * n + 1)
                    dve.bn_aggr(gmv[:, t, :], gst[:, t, :]).then_inc(gn_step, 1)
                dve.wait_ge(gn_std, h + 1)
                dve.reciprocal(grs[:, :], grs[:, :]).then_inc(gn_rec, 1)
                dve.wait_ge(gn_rec, h + 1)
                for t in range(NT):
                    n = NT * h + t
                    if h:
                        dve.wait_ge(rg_ready, n - 1)
                    dve.tensor_scalar(og[t][:, :], psum[:, n % 4, :], gmv[:, t, 0:1], grs[:, t:t + 1], ALU.subtract,
                                      ALU.mult).then_inc(gn_ready, 1)
            turn_y(4, 2 * KT)
            chunks("zconv", conv_part(4, 2), unroll=True)
            chunks("gates", conv_part(6, 1), unroll=True)
            for k in range(KT):
                i = dve.tensor_scalar(gdiag[:, k, :], ident, mod[:, 2 * KT + k:2 * KT + k + 1], None, ALU.mult)
            i.then_inc(gate_diag, 1)
            mean, inv = (lnm[:, s, :].rearrange("p (a n) -> p a n", a=1).to_broadcast([P, 2, SEQ]) for s in range(2))
            dve.wait_ge(mean_done, 1)
            dve.tensor_scalar(lnm[:, 0, :], psum[:, 4, 0:SEQ], 1.0 / D, None, ALU.mult).then_inc(ln_mean, 1)
            dve.wait_ge(ln_mean, 1)
            pairs = [slice(2 * q, 2 * q + 2) for q in range(KT // 2)]
            for pair in pairs:
                dve.tensor_tensor(cv[:, pair, :], cv[:, pair, :], mean, ALU.subtract).then_inc(xc_ready, 1)
            dve.wait_ge(gate_row, 1)
            dve.wait_ge(row_loaded, 16 * 3)
            for s in range(2):
                half = slice(512 * s, 512 * (s + 1))
                dve.tensor_tensor(row[:, half], row[:, half], psum[:, 6 + s, :], ALU.mult).then_inc(row_mul, 1)
            dve.wait_ge(ln_step, 2)
            dve.wait_ge(xc_ready, KT // 2)
            for pair in pairs:
                dve.tensor_tensor(cv[:, pair, :], cv[:, pair, :], inv, ALU.mult).then_inc(lns_ready, 1)
            for q, pair in enumerate(pairs):
                dve.wait_ge(lna_ready, 2 * q + 2)
                dve.tensor_tensor(cv[:, pair, :], cv[:, pair, :], zc[:, pair, :], ALU.mult).then_inc(lnz_ready, 1)
            for q, pair in enumerate(pairs):
                dve.wait_ge(chi_ready, q + 1)
                part_lo(hT_lo[:, pair, :], cv[:, pair, :], hT_hi[:, pair, :]).then_inc(cop_ready, 1)

            def conv_gated(i, j, done):
                dve.wait_ge(chunk_done, done)
                o = gab[:, KT + 2 * j:KT + 2 * j + 2, :]
                dve.tensor_tensor(o, bank(j), o, ALU.mult).then_inc(bank_free, 1)
            chunks("conv_out", conv_gated)

            def merged(i, j, done):
                if j % 2:
                    b = 2 * i + j // 2
                    pair = slice(2 * b, 2 * b + 2)
                    dve.wait_ge(chunk_done, done)
                    dve.tensor_tensor(rp2[:, :, :], bank(j // 2), gab[:, pair, :], ALU.mult).then_inc(bank_free, 2)
                    dve.wait_ge(bank_free, 4 + FIRST["ret_out"] + 2 * (b + 1))
                    dve.tensor_tensor(rp2[:, :, :], rp2[:, :, :], gab[:, KT + 2 * b:KT + 2 * b + 2, :], ALU.add).then_inc(mg_ready, 1)
                    dve.wait_ge(mg_ready, b + 1)
                    dve.wait_ge(mhi_ready, b + 1)
                    part_lo(hT_lo[:, pair, :], rp2[:, :, :], hT_hi[:, pair, :]).then_inc(mop_ready, 1)
            chunks("ret_out", merged, unroll=True)
            chunks("w_out")
            dve.wait_ge(row_mul, 2)
            post_norm(2)


_INS = ["x", "pre_norm_w", "post_norm_w", "gdn_w_in", "gdn_conv_w", "gdn_A_log", "gdn_dt_bias", "gdn_norm_w",
        "gdn_w_out", "sc_w_in", "sc_conv_w", "sc_w_out", "c_2", "positions_2", "w_ada_2", "b_ada_2", "pre_norm_g_2",
        "w_in_2", "conv_w_2", "conv_b_2", "conv_ln_g_2", "conv_ln_b_2", "w_ret_out_2", "w_conv_out_2", "w_out_2",
        "post_norm_g_2"]


def shape_constants():
    import numpy as _np

    i = _np.arange(P)
    masks = _np.zeros((P, NCONST, P), _np.float32)
    masks[:, C_ID] = _np.eye(P)
    masks[:, C_ONE] = 1.0
    masks[:, C_LOW] = i[:, None] > i[None, :]
    masks[:, C_INC] = i[:, None] >= i[None, :]
    for level in range(NLEV):
        b = 2 ** level
        same = (i[:, None] // (2 * b)) == (i[None, :] // (2 * b))
        low = same & (i[:, None] // b % 2 == 1) & (i[None, :] // b % 2 == 0)
        signed = _np.eye(P) - low
        if level == 0:
            masks[:, C_M0], masks[:, C_M0T] = signed, signed.T
        else:
            masks[:, C_MASK + level - 1] = signed
    log_g = _np.log1p(-_np.exp2(-5.0 - _np.arange(RH)))
    diff = _np.arange(SEQ)[None, :] - i[:, None]
    decays = _np.zeros((P, RH, 3 * P), _np.float32)
    for h in range(RH):
        d = _np.where(diff >= 0, _np.exp(log_g[h] * _np.maximum(diff, 0)), 0.0) * RDK ** -0.5
        decays[:, h, :SEQ] = d
        decays[:, h, SEQ:] = d[:, :P]
    freqs = (_np.float32(ROPE_BASE) ** (-_np.arange(P, dtype=_np.float32) / _np.float32(P))).astype(_np.float32)
    return masks, decays, freqs.reshape(P, 1)


def kernel(**inputs):
    import numpy as _np
    import concourse.bacc as _bacc
    from concourse import mybir as _mybir
    from concourse.bass_utils import run_bass_kernel_spmd as _run

    nc = _bacc.Bacc("TRN2", target_bir_lowering=False, num_devices=1)
    arrays, args = {}, []
    given = [(name, _np.ascontiguousarray(inputs[name])) for name in _INS]
    given += list(zip(("masks", "decays", "freqs"), shape_constants()))
    for name, a in given:
        arrays[f"in_{name}_dram"] = a
        args.append(nc.dram_tensor(f"in_{name}_dram", a.shape, _mybir.dt.from_np(a.dtype), kind="ExternalInput").ap())
    out = nc.dram_tensor("out_0_dram", (1, SEQ, D), F32, kind="ExternalOutput").ap()
    build(nc, *args, out)
    r = _run(nc, [arrays], core_ids=[0])
    return r.results[0]["out_0_dram"]
```

```python
import math
from contextlib import ExitStack

import numpy as np

import concourse.bass as bass
from concourse import mybir

F32 = mybir.dt.float32
F32R = mybir.dt.float32r
I32 = mybir.dt.int32
ACT = mybir.ActivationFunctionType
ALU = mybir.AluOpType
AX_X = mybir.AxisListType.X

P = 128
SEQ = 256
NT = SEQ // P
D = 1024
KT = D // P
KH2 = KT // 2
ROPE_BASE = 10000.0
RMS_EPS = 1e-6
NORM_EPS = 1e-5

VH, KH = 16, 8
HD = 128
GQK, GV = KH * HD, VH * HD
GCONV = 4
GQKV = 2 * GQK + GV
SCW = 2 * D
SCONV = 3
RH, RDK, RDV = 4, 256, 512
CW = 31
CPAD = CW - 1
CONV_DVE = 5
HG = 4
NPAIR = VH // HG
LIVE = 3
NLEV = 7

CC = 256
RING = 4
PHASES = [("qkv", 16), ("z", 8), ("gdn_out", 8), ("sc_in", 32), ("sc_out", 8), ("glu", 8), ("qk", 8), ("v", 8),
          ("zret", 8), ("zconv", 4), ("gates", 8), ("conv_out", 4), ("ret_out", 8), ("w_out", 4)]
FIRST = {}
COUNT = dict(PHASES)
_g = 0
for _n, _c in PHASES:
    FIRST[_n] = _g
    _g += _c
CHUNKS = _g
ADA_PIECES = 3 * D // P
ADA_SLOTS = ADA_PIECES // (COUNT["sc_in"] // 4)
assert ADA_SLOTS * COUNT["sc_in"] == 4 * ADA_PIECES and ADA_SLOTS <= 4

C_ID, C_ONE, C_LOW, C_FLOOR, C_M0, C_M0T, C_MASK = 0, 1, 2, 3, 4, 5, 6
NCONST = C_MASK + NLEV - 1

V_PRE, V_PRE2, V_BADA, V_CB, V_LG, V_LB, V_C, V_SC = 0, 16, 24, 48, 56, 64, 72, 80
E_LEAST = 0.5 * math.log(RMS_EPS) - 0.1
G_ROW = 32


def build(nc, x_in, pre_norm_w, post_norm_w, gdn_w_in, gdn_conv_w, gdn_A_log, gdn_dt_bias, gdn_norm_w, gdn_w_out,
          sc_w_in, sc_conv_w, sc_w_out, c_2, positions_2, w_ada_2, b_ada_2, pre_norm_g_2, w_in_2, conv_w_2, conv_b_2,
          conv_ln_g_2, conv_ln_b_2, w_ret_out_2, w_conv_out_2, w_out_2, post_norm_g_2, masks, decays, freqs, out):
    ctx = ExitStack()
    with ctx:
        def sem(name):
            return ctx.enter_context(nc.semaphore(name))

        base = (nc.sbuf_base + 63) // 64 * 64
        fence = ctx.enter_context(nc.sbuf_tensor("fence", [P, (nc.sbuf_usable_end - base) // 64 * 16 - 16], F32))
        top = [base]

        def at(name, offset, shape, dt=F32):
            return nc.alloc_sbuf_tensor_at(name, shape, dt, offset=offset)

        def room(nbytes):
            offset = top[0]
            top[0] += (nbytes + 31) // 32 * 32
            assert top[0] <= nc.sbuf_usable_end, (top[0], nc.sbuf_usable_end)
            return offset

        def new(name, shape, dt=F32):
            n = 4
            for s in shape[1:]:
                n *= s
            return at(name, room(n), shape, dt)

        K = 1024
        o_raw = top[0]
        raw = [new(f"w_raw{s}", [P, KT, CC]) for s in range(RING)]
        w_hi = [new(f"w_hi{s}", [P, KH2, CC], F32R) for s in range(4)]
        w_lo = [new(f"w_lo{s}", [P, KH2, CC], F32R) for s in range(4)]
        x = new("x", [P, NT, D])
        o_hT, o_yT, o_ada, o_ar = room(16 * K), room(32 * K), room(8 * K), room(64 * K)
        hT_hi, hT_lo = at("hT_hi", o_hT, [P, KT, SEQ], F32R), at("hT_lo", o_hT + 8 * K, [P, KT, SEQ], F32R)
        yT_hi, yT_lo = at("yT_hi", o_yT, [P, 2 * KT, SEQ], F32R), at("yT_lo", o_yT + 16 * K, [P, 2 * KT, SEQ], F32R)
        ada = [at(f"ada{s}", o_ar + (44 + 4 * s) * K, [P, KT, P]) for s in range(ADA_SLOTS)]
        ada_sum = at("ada_sum", o_ar + 32 * K, [P, ADA_PIECES, P])
        const = new("const", [P, NCONST, P])
        ident, ones = const[:, C_ID, :], const[:, C_ONE, :]
        o_row = room(4 * K)
        row = at("row", o_row, [P, D])
        nw_row = new("nw_row", [P, HD])
        par = new("par", [P, 4, P])
        bg = new("bg", [P, SEQ])
        bgt = new("bgt", [P, NT, P])
        eg = new("eg", [P, NT, VH])
        nbeg = new("nbeg", [P, NT, VH])
        wdec = new("wdec", [P, VH])
        lnss = at("lnss", o_ar + 63 * K, [P, NT, 2 * KH])
        gk, brk = (at(n, o_ar + 63 * K + 128 * (s + 1), [P, NT, VH]) for s, n in enumerate(("gk", "brk")))
        rqs = at("rqs", o_ar + 63 * K + 384, [P, NT, KH])
        acols = new("acols", [P, 4])
        mod = new("mod", [P, 3 * KT])
        gain2 = new("gain2", [P, KT])
        eps_r, eps_n = new("eps_r", [P, 1]), new("eps_n", [P, 1])
        ss, ms, rstd, yss = new("ss", [P, 4]), new("ms", [P, 4]), new("rstd", [P, 4]), new("yss", [P, NT, D // CC])
        o_ss, o_rs = new("o_ss", [P, NT, VH]), new("o_rs", [P, NT, VH])
        freq = new("freq", [P, 1])
        gst, gmv, grs, gnm = new("gst", [P, NT, 6]), new("gmv", [P, NT, 2]), new("grs", [P, NT]), new("gnm", [P, NT])

        xn = at("xn", o_ar, [P, NT, D])
        hx = at("hx", o_ar + 8 * K, [P, KT, SEQ])
        junk = at("junk", o_ar + 8 * K, [P, NT, D])
        vecs = at("vecs", o_ar + 16 * K, [P, 4, P])
        qkvT = at("qkvT", o_ar, [P, 4 * KT, SEQ])
        S = at("S", o_ar + 16 * K, [P, LIVE, NT, HG, P])
        zo = at("zo", o_ar + 32 * K, [P, NT, GV])
        PT = at("PT", o_ar + 48 * K, [P, LIVE, NT, HG, P])
        cacc = [at(f"cacc{s}", o_ar + (48 + 2 * s) * K, [P, 2, SEQ]) for s in range(2)]
        ba_raw = at("ba_raw", o_ar + 52 * K, [P, KT, P])
        ba_hi = at("ba_hi", o_ar + 56 * K, [P, KT, P], F32R)
        ba_lo = at("ba_lo", o_ar + 60 * K, [P, KT, P], F32R)
        vb = at("vb", o_yT, [P, NT, VH, HD])
        ktok = at("ktok", o_yT + 16 * K, [P, KH, HD])
        LT = [[at(f"LT{q}{t}", o_yT + (20 + 2 * (2 * q + t)) * K, [P, HG, P]) for t in range(NT)] for q in range(2)]
        o_Z = [o_yT + 28 * K, o_ar + 28 * K] + [o_raw + (16 + 4 * l) * K for l in range(NLEV - 3)]
        Z = [None] + [[at(f"Z{l + 1}{t}", o_Z[l] + 2 * t * K, [P, HG, P]) for t in range(NT)] for l in range(NLEV - 1)]
        sq = [at(f"sq{s}", o_yT + (20 + 2 * s) * K, [P, 2, SEQ]) for s in range(2)]
        gz, gl, gs = (at(f"gate{s}", o_ar + (60 + s) * K, [P, SEQ]) for s in range(3))
        E, Di, A = (at(n, o_hT + 2 * s * K, [P, HG, P]) for s, n in enumerate(("E", "Di", "A")))
        T = [[at(f"T{q}{t}", o_hT + (6 + 2 * (2 * q + t)) * K, [P, HG, P]) for t in range(NT)] for q in range(2)]
        qS = at("qS", o_hT + 14 * K, [P, HG, P])
        kdec, R, U, s1 = (at(n, o_ada + 2 * s * K, [P, HG, P]) for s, n in enumerate(("kdec", "R", "U", "s1")))
        osq = at("osq", o_row, [P, HG, P])
        sc_u = at("sc_u", o_ar + 16 * K, [P, 2, SEQ])
        sc_cu = at("sc_cu", o_ar + 18 * K, [P, 2, SEQ])
        sc_v = at("sc_v", o_ar + 20 * K, [P, 2, SEQ])
        sc_y = at("sc_y", o_ar + 22 * K, [P, 2, SEQ])
        sc_z = at("sc_z", o_ar + 24 * K, [P, 2, SEQ])
        sc_yz = at("sc_yz", o_ar + 26 * K, [P, 2, SEQ])
        aP = at("aP", o_ar, [P, KT, CPAD + SEQ])
        cv = at("cv", o_ar + 9728, [P, KT, SEQ])
        o_q = o_ar + 9728 + 8 * K
        qkT = at("qkT", o_q, [P, 2 * KT, SEQ])
        vt = at("vt", o_q + 16 * K, [P, NT, 2 * D])
        o_t = o_q + 32 * K
        st = at("st", o_t, [P, RH, 3 * P])
        glu, rp1, rp2 = (at(n, o_t + 2 * s * K, [P, 2, SEQ]) for s, n in enumerate(("glu", "rp1", "rp2")))
        cvo = at("cvo", o_t + 6 * K, [P, SEQ])
        lnm = at("lnm", o_t + 7 * K, [P, 2, SEQ])
        tapped = at("tapped", o_t + 7 * K, [P, 2, SEQ])
        cT_hi, cT_lo = at("cT_hi", o_ar, [P, KT, SEQ], F32R), at("cT_lo", o_q + 24 * K, [P, KT, SEQ], F32R)
        og = [at(f"og{t}", o_t + (9 + 2 * t) * K, [P, RDV]) for t in range(NT)]
        zr = at("zr", o_yT, [P, NT, 2 * D])
        zc = at("zc", o_q, [P, KT, SEQ])
        gab = at("gab", o_q + 8 * K, [P, 2 * KT, SEQ])
        a2 = at("a2", o_q + 24 * K, [P, KT, SEQ])
        decay = at("decay", o_ada, [P, RH, 3 * P])
        trig = at("trig", o_ada + 6 * K, [P, 2, SEQ])
        pos_i = at("pos_i", o_ar + 28 * K, [P, SEQ], I32)
        ang, turn = at("ang", o_ar + 29 * K, [P, SEQ]), at("turn", o_ar + 30 * K, [P, 2, SEQ])
        gdiag = at("gdiag", o_t, [P, KT, P])

        psum = ctx.enter_context(nc.psum_tensor("psum", [P, 8, 512], F32))

        def bank(b, inner=SEQ):
            return psum[:, b, :].rearrange("p (a n) -> p a n", n=inner)

        raw_ready = [sem(f"raw_ready{s}") for s in range(RING)]
        hi_ready, lo_ready = sem("hi_ready"), sem("lo_ready")
        half_done = sem("half_done")
        bank_free = sem("bank_free")
        ada_ready = [sem(f"ada_ready{s}") for s in range(ADA_SLOTS)]
        ada_step = sem("ada_step")
        ada_used = sem("ada_used")
        x_loaded = [sem(f"x_loaded{t}") for t in range(NT)]
        vecs_loaded, small_loaded, ba_loaded, rope_loaded = sem("vecs_loaded"), sem("small_loaded"), sem("ba_loaded"), sem("rope_loaded")
        row_loaded, decay_loaded, cleared, padded = sem("row_loaded"), sem("decay_loaded"), sem("cleared"), sem("padded")
        par_turned, par_ready = sem("par_turned"), sem("par_ready")
        pre_ss, pre_rstd, xn_ready = sem("pre_ss"), sem("pre_rstd"), sem("xn_ready")
        turned, hx_ready, hhi_ready, h_ready = sem("turned"), sem("hx_ready"), sem("hhi_ready"), sem("h_ready")
        y_ready, post_rstd = sem("y_ready"), sem("post_rstd")
        x_ready = sem("x_ready")
        out_done = sem("out_done")
        post_ss, post_std, pre_std, ln_rstd, o_std, gn_std = (sem(n) for n in ("post_ss", "post_std", "pre_std", "ln_rstd", "o_std", "gn_std"))
        tapped_ready, cv_pool_step = sem("tapped_ready"), sem("cv_pool_step")
        lnss_ready, gk_ready, glast_ready, rows_step = (sem(n) for n in ("lnss_ready", "gk_ready", "glast_ready", "rows_step"))
        tap0, tap_step, qkv_ready = sem("tap0"), sem("tap_step"), sem("qkv_ready")
        ba_hi_ready, ba_lo_ready, ba_done = sem("ba_hi_ready"), sem("ba_lo_ready"), sem("ba_done")
        beta_ready, gate_v, gate_a, g_ready = sem("beta_ready"), sem("gate_v"), sem("gate_a"), sem("g_ready")
        bg_turned, bgt_ready, eg_ready, nbeg_ready = sem("bg_turned"), sem("bgt_ready"), sem("eg_ready"), sem("nbeg_ready")
        sq_ready, l2_sum, odd_ready = sem("sq_ready"), sem("l2_sum"), sem("odd_ready")
        v_turned, vb_ready, k_turned, ktok_ready = sem("v_turned"), sem("vb_ready"), sem("k_turned"), sem("ktok_ready")
        zn_ready = sem("zn_ready")
        grow_ready, kq_ready, d_ready, e_ready, masked = sem("grow_ready"), sem("kq_ready"), sem("d_ready"), sem("e_ready"), sem("masked")
        wd_ready, wd_sub = sem("wd_ready"), sem("wd_sub")
        ap_ready, ap_turned, lt_ready, pt_ready = sem("ap_ready"), sem("ap_turned"), sem("lt_ready"), sem("pt_ready")
        l_ready, chain_ready = sem("l_ready"), sem("chain_ready")
        w_done = [sem(f"w_done{t}") for t in range(NT)]
        z_ready = [sem(f"z_ready{t}") for t in range(NT)]
        ts_done = [sem(f"ts_done{t}") for t in range(NT)]
        t_ready = [sem(f"t_ready{t}") for t in range(NT)]
        s_ready = [sem(f"s_ready{t}") for t in range(NT)]
        kdec_ready, u_done, u_ready, o0_done, s1_done, s1_ready = (sem(n) for n in ("kdec_ready", "u_done", "u_ready", "o0_done", "s1_done", "s1_ready"))
        ks_done, r_ready, qs_ready, vn_done, vn_ready, o1_done, o_ready = (sem(n) for n in ("ks_done", "r_ready", "qs_ready", "vn_done", "vn_ready", "o1_done", "o_ready"))
        osq_ready, o_rstd, og_ready = (sem(n) for n in ("osq_ready", "o_rstd", "og_ready"))
        yT_turned, yhi_ready, y_op_ready = sem("yT_turned"), sem("yhi_ready"), sem("y_op_ready")
        sc_u_ready, sc_v0, sc_step, sc_z_ready = (sem(n) for n in ("sc_u_ready", "sc_v0", "sc_step", "sc_z_ready"))
        mod_done, mod_ready, gain2_ready = sem("mod_done"), sem("mod_ready"), sem("gain2_ready")
        glu_ready, ang_step, ang_ready, trig_ready = sem("glu_ready"), sem("ang_step"), sem("ang_ready"), sem("trig_ready")
        rp_step = sem("rp_step")
        sco_done, st_ready, ro_done, gn_step, gn_ready = (sem(n) for n in ("sco_done", "st_ready", "ro_done", "gn_step", "gn_ready"))
        rg_ready = sem("rg_ready")
        cv_step, cv_ready, mean_done, xc_ready, a2_ready, var_done, ln_step = (sem(n) for n in ("cv_step", "cv_ready", "mean_done", "xc_ready", "a2_ready", "var_done", "ln_step"))
        lna_ready, lns_ready, lnz_ready = (sem(n) for n in ("lna_ready", "lns_ready", "lnz_ready"))
        chi_ready, cop_ready, mg_ready, mhi_ready, mop_ready = (sem(n) for n in ("chi_ready", "cop_ready", "mg_ready", "mhi_ready", "mop_ready"))
        qs_done, o1_ready, gn_rec, ln_mean = sem("qs_done"), sem("o1_ready"), sem("gn_rec"), sem("ln_mean")
        gate_diag, gate_row, row_mul = sem("gate_diag"), sem("gate_row"), sem("row_mul")
        block = ctx.enter_context(nc.Block())

        def loop(eng, n, step):
            if n == 1:
                step(0)
            else:
                with eng.Fori(0, n) as i:
                    step(i)

        def half(ap, l, odd):
            return ap.rearrange("p (n two b) -> p n two b", two=2, b=2 ** l)[:, :, odd, :]

        def half_heads(ap, l, odd):
            return ap.rearrange("p h (n two b) -> p h n two b", two=2, b=2 ** l)[:, :, :, odd, :]

        def half_of_each(ap, l, odd):
            o = half(ap, l, odd)
            return o.rearrange("p (h n) b -> p h n b", h=1).to_broadcast([P, HG, P // 2 // 2 ** l, 2 ** l])

        def two_each(ap):
            return ap.rearrange("p t (n r) -> p t n r", r=1).to_broadcast([P, NT, KH, 2])

        def heads(ap, n):
            return ap.rearrange("p (a n) -> p a n", a=1).to_broadcast([P, n, ap.shape[-1]])

        @block.sync
        def _(sp):
            def cols(w, r0, c, n=CC):
                return w[r0:r0 + D, bass.ds(c, n)].rearrange("(k p) n -> p k n", p=P)

            def chunk(g, slot, src, wait=True):
                if wait:
                    sp.wait_ge(lo_ready, g * 2 - 2 * (RING - 1))
                sp.dma_start(raw[slot][:, :, :], src).then_inc(raw_ready[slot], 16)

            def phase(name, where, with_ada=False, start=0):
                g0 = FIRST[name]

                def step(i):
                    for j in range(4):
                        w, r0, c = where(i, j)
                        g = i * 4 + (g0 + j)
                        chunk(g, j, cols(w, r0, c))
                        if with_ada and j < ADA_SLOTS:
                            if not isinstance(i, int):
                                sp.wait_ge(ada_used, i * ADA_SLOTS + (j + 1 - ADA_SLOTS))
                            sp.dma_start(ada[j][:, :, :], cols(w_ada_2[0], 0, i * (ADA_SLOTS * P) + j * P, P)).then_inc(ada_ready[j], 16)
                if with_ada:
                    step(0)
                    start = 1
                if COUNT[name] // 4 - start > 1:
                    with sp.Fori(start, COUNT[name] // 4) as i:
                        step(i)
                else:
                    step(start)

            for t in range(NT):
                sp.dma_start(x[:, t, :], x_in[0, t * P:(t + 1) * P, :]).then_inc(x_loaded[t], 16)
            sp.dma_start(const[:, 0:2, :], masks[:, 0:2, :]).then_inc(vecs_loaded, 16)
            sp.dma_start(vecs[:, 0, :], gdn_conv_w[0].rearrange("j (n p) -> (j n) p", p=P)).then_inc(vecs_loaded, 16)
            for at_row, v in ((V_PRE, pre_norm_w), (V_PRE2, pre_norm_g_2), (V_BADA, b_ada_2), (V_CB, conv_b_2),
                              (V_LG, conv_ln_g_2), (V_LB, conv_ln_b_2), (V_C, c_2)):
                n = v.shape[0] * v.shape[1] // P
                sp.dma_start(vecs[at_row:at_row + n, 1, :], v.rearrange("l (k p) -> (l k) p", p=P)).then_inc(vecs_loaded, 16)
            sp.dma_start(vecs[V_SC:P, 1, :], sc_conv_w[0].rearrange("j (n p) -> (j n) p", p=P)).then_inc(vecs_loaded, 16)
            sp.dma_start(vecs[:, 2, :], conv_w_2[0, 0:16].rearrange("j (n p) -> (j n) p", p=P)).then_inc(vecs_loaded, 16)
            sp.dma_start(vecs[0:120, 3, :], conv_w_2[0, 16:CW].rearrange("j (n p) -> (j n) p", p=P)).then_inc(vecs_loaded, 16)
            chunk(0, 0, cols(gdn_w_in[0], 0, 0), wait=False)
            sp.dma_start(acols[G_ROW:G_ROW + VH, 0:1], gdn_A_log.rearrange("l h -> h l")).then_inc(small_loaded, 16)
            sp.dma_start(acols[G_ROW:G_ROW + VH, 1:2], gdn_dt_bias.rearrange("l h -> h l")).then_inc(small_loaded, 16)
            sp.dma_start(freq[:, :], freqs).then_inc(small_loaded, 16)
            sp.dma_start(const[:, 2:NCONST, :], masks[:, 2:NCONST, :]).then_inc(small_loaded, 16)
            sp.dma_start(nw_row[:, :], gdn_norm_w.to_broadcast([P, HD])).then_inc(small_loaded, 16)
            for j in range(4):
                if j:
                    chunk(j, j, cols(gdn_w_in[0], 0, j * CC), wait=False)
            sp.wait_ge(padded, 1)
            ba0 = GQKV + GV
            sp.dma_start(ba_raw[:, :, 0:VH], cols(gdn_w_in[0], 0, ba0, VH)).then_inc(ba_loaded, 16)
            sp.dma_start(ba_raw[:, :, G_ROW:G_ROW + VH], cols(gdn_w_in[0], 0, ba0 + VH, VH)).then_inc(ba_loaded, 16)
            phase("qkv", lambda i, j: (gdn_w_in[0], 0, i * 1024 + j * CC), start=1)
            phase("z", lambda i, j: (gdn_w_in[0], 0, i * 1024 + (GQKV + j * CC)))

            def two_halves(w):
                return lambda i, j: (w, j % 2 * D, i * 512 + j // 2 * CC)

            for j in range(4):
                if j == 2:
                    sp.wait_ge(o_ready, 2 * NPAIR)
                chunk(FIRST["gdn_out"] + j, j, cols(gdn_w_out[0], j % 2 * D, j // 2 * CC))
            sp.dma_start(row[:, :], post_norm_w[0:1, :].to_broadcast([P, D])).then_inc(row_loaded, 16)
            phase("gdn_out", two_halves(gdn_w_out[0]), start=1)
            sp.wait_ge(y_op_ready, KT)
            phase("sc_in", lambda i, j: (sc_w_in[0], 0, i * CC + (0, 2 * SCW, SCW, 3 * SCW)[j]), with_ada=True)
            sp.wait_ge(x_ready, NT)
            sp.dma_start(row[:, :], post_norm_w[1:2, :].to_broadcast([P, D])).then_inc(row_loaded, 16)
            sp.dma_start(decay[:, :, :], decays).then_inc(decay_loaded, 16)
            sp.dma_start(pos_i[:, :], positions_2.to_broadcast([P, SEQ])).then_inc(rope_loaded, 16)
            phase("sc_out", two_halves(sc_w_out[0]))
            win = w_in_2[0]
            o_k, o_v, o_zr, o_uv, o_ug, o_zc, o_g = 0, 2 * D, 4 * D, 6 * D, 7 * D, 8 * D, 9 * D
            phase("glu", lambda i, j: (win, 0, i * 512 + ((o_uv if j % 2 else o_ug) + j // 2 * CC)))
            sp.wait_ge(x_ready, 2 * NT)
            sp.dma_start(row[:, :], post_norm_g_2[0:1, :].to_broadcast([P, D])).then_inc(row_loaded, 16)
            phase("qk", lambda i, j: (win, 0, i * 1024 + (o_k + j * CC)))
            phase("v", lambda i, j: (win, 0, i * 1024 + (o_v + j * CC)))
            phase("zret", lambda i, j: (win, 0, i * 1024 + (o_zr + j * CC)))
            phase("zconv", lambda i, j: (win, 0, o_zc + j * CC))
            phase("gates", lambda i, j: (win, 0, i * 1024 + (o_g + j * CC)))
            phase("conv_out", lambda i, j: (w_conv_out_2[0], 0, j * CC))
            phase("ret_out", two_halves(w_ret_out_2[0]))
            phase("w_out", lambda i, j: (w_out_2[0], 0, j * CC))
            for t in range(NT):
                sp.wait_ge(x_ready, 2 * NT + t + 1)
                sp.dma_start(out[0, t * P:(t + 1) * P, :], x[:, t, :]).then_inc(out_done, 16)
            sp.wait_ge(out_done, 16 * NT)

        VECS, SMALL = 16 * 12, 16 * 5

        @block.tensor
        def _(pe):
            def product(o, l_hi, l_lo, r_hi, r_lo, start, stop):
                pe.matmul(o, l_hi, r_hi, start=start, stop=False, skip_group_check=True)
                pe.matmul(o, l_hi, r_lo, start=False, stop=False, skip_group_check=True)
                return pe.matmul(o, l_lo, r_hi, start=False, stop=stop, skip_group_check=True)

            def chunk(i, g0, j, b, a_hi, a_lo, k0, channels, part, norm=None):
                o = bank(b)
                if part is None:
                    pe.wait_ge(bank_free, i * 4 + (g0 + j + 1))
                elif part == 0:
                    pe.wait_ge(bank_free, i * 4 + (g0 + j + 2))
                for h in range(2):
                    s = j % 2 * 2 + h
                    if j == 0 and norm is not None:
                        pe.wait_ge(h_ready, KT // 2 * norm + KT // 4 * (h + 1))
                    pe.wait_ge(lo_ready, i * 8 + (2 * (g0 + j) + h + 1))
                    for m in range(2):
                        mine = slice(m * P, (m + 1) * P)
                        for k in range(KH2):
                            ka = k0 + h * KH2 + k
                            first = m == 0 and h == 0 and k == 0 and part != 1
                            last = h == 1 and k == KH2 - 1 and part != 0
                            if channels:
                                mm = product(o[:, m, :], w_hi[s][:, k, mine], w_lo[s][:, k, mine], a_hi[:, ka, :], a_lo[:, ka, :], first, last)
                            else:
                                mm = product(o[:, m, :], a_hi[:, ka, mine], a_lo[:, ka, mine], w_hi[s][:, k, :], w_lo[s][:, k, :], first, last)
                    mm.then_inc(half_done, 1)

            def phase(name, a_hi, a_lo, channels, deep=False, norm=None, beside=None, loop_beside=None):
                g0 = FIRST[name]
                if g0:
                    pe.wait_ge(bank_free, 4 + g0)

                def step(i, i_beside=None):
                    for j in range(4):
                        if deep:
                            chunk(i, g0, j, j // 2, a_hi, a_lo, j % 2 * KT, channels, j % 2)
                        else:
                            chunk(i, g0, j, j, a_hi, a_lo, 0, channels, None, norm)
                        if beside is not None:
                            beside(4 * i + j)
                        if i_beside is not None:
                            loop_beside(i_beside, j)
                if beside is not None:
                    for i in range(COUNT[name] // 4):
                        step(i)
                elif loop_beside is not None:
                    n = COUNT[name] // 4
                    with pe.Fori(0, n - KT // 4) as i:
                        step(i)
                    with pe.Fori(0, KT // 4) as i:
                        step(i + (n - KT // 4), i)
                else:
                    loop(pe, COUNT[name] // 4, step)

            def pre_norm(n):
                for t in range(NT):
                    pe.wait_ge(xn_ready, NT * n + t + 1)
                    for k in range(KT):
                        mm = pe.transpose(bank(4 + k // 2, P)[:, k % 2 * NT + t, :], xn[:, t, k * P:(k + 1) * P], ident)
                        if t == NT - 1 and k % 2:
                            mm.then_inc(turned, 1)

            pe.wait_ge(vecs_loaded, VECS)
            for n in range(4):
                r = 120 if n == 3 else P
                mm = pe.transpose(bank(7, P)[:, n, 0:r], vecs[0:r, n, :], ident[0:r, 0:r])
            mm.then_inc(par_turned, 1)
            pe.wait_ge(par_ready, 1)
            pre_norm(0)
            def squares(i, j):
                pe.wait_ge(sq_ready, i * 4 + (j + 1))
                for m in range(2):
                    for t in range(NT):
                        mm = pe.matmul(psum[:, 7, bass.ds(i * 8 + (t * VH + 2 * j + m), 1)], sq[j % 2][:, m, t * P:(t + 1) * P],
                                       ones[:, 0:1], start=True, stop=True)
                mm.then_inc(l2_sum, 1)
            phase("qkv", hT_hi, hT_lo, True, norm=0, loop_beside=squares)
            def beside_z(c):
                if c == 0:
                    pe.wait_ge(ba_lo_ready, 1)
                    for k in range(KT):
                        mm = product(psum[:, 6, 0:SEQ], ba_hi[:, k, :], ba_lo[:, k, :], hT_hi[:, k, :], hT_lo[:, k, :], k == 0, k == KT - 1)
                    mm.then_inc(ba_done, 1)
                if c == 3:
                    pe.wait_ge(g_ready, NT)
                    for t in range(NT):
                        mm = pe.transpose(bank(6, P)[:, t, :], bg[:, t * P:(t + 1) * P], ident)
                    mm.then_inc(bg_turned, 1)
                    pe.wait_ge(lnss_ready, 1)
                    pe.matmul(psum[:, 7, 2 * VH:3 * VH], bg[:, P - 1:P].to_broadcast([P, P]), ident[:, G_ROW:G_ROW + VH], start=True,
                              stop=True).then_inc(glast_ready, 1)
                    pe.wait_ge(qkv_ready, COUNT["qkv"])
                if c >= 4:
                    for n in (2 * (c - 4), 2 * (c - 4) + 1):
                        t, q = n // NPAIR, n % NPAIR
                        if n >= 2:
                            pe.wait_ge(vb_ready, n - 1)
                        elif n == 0:
                            pe.wait_ge(bgt_ready, 1)
                        else:
                            pe.wait_ge(wd_sub, 1)
                        for a in range(HG):
                            mm = pe.transpose(bank(6 + n % 2, P)[:, a, :], qkvT[:, 2 * KT + HG * q + a, t * P:(t + 1) * P], ident)
                        mm.then_inc(v_turned, 1)
                if c == COUNT["z"] - 1:
                    pe.wait_ge(vb_ready, 2 * NPAIR)
                    for n in range(2):
                        for a in range(HG):
                            mm = pe.transpose(bank(6 + n, P)[:, a, :], qkvT[:, KT + HG * n + a, 0:P], ident)
                        mm.then_inc(k_turned, 1)
            phase("z", hT_hi, hT_lo, False, beside=beside_z)
            pe.wait_ge(ktok_ready, 2)
            pe.wait_ge(gk_ready, 1)

            def prep(p, c, stage):
                n, cs = NT * p + c, slice(c * P, (c + 1) * P)
                if stage == 1:
                    if n:
                        pe.wait_ge(lt_ready, n)
                    for a in range(HG):
                        h = HG * p + a
                        mm = pe.matmul(bank(4, P)[:, a, :], gk[:, c, h:h + 1].to_broadcast([P, P]), ident, start=True, stop=True)
                    mm.then_inc(grow_ready, 1)
                    if n:
                        pe.wait_ge(pt_ready, n)
                    for e in range(2):
                        k = qkvT[:, KT + 2 * p + e, cs]
                        pe.matmul(bank(5, P)[:, e, :], k, k, start=True, stop=True)
                        mm = pe.matmul(bank(5, P)[:, 2 + e, :], qkvT[:, 2 * p + e, cs], k, start=True, stop=True)
                    mm.then_inc(kq_ready, 1)
                if stage == 2:
                    pe.wait_ge(ap_ready, n + 1)
                    for a in range(HG):
                        pe.transpose(bank(4, P)[:, a, :], A[:, a, :], ident)
                        mm = pe.transpose(bank(5, P)[:, a, :], Di[:, a, :], ident)
                    mm.then_inc(ap_turned, 1)

            def level_w(p, l):
                for c in range(NT):
                    if l == 1:
                        pe.wait_ge(chain_ready, NT * p + c + 1)
                    else:
                        pe.wait_ge(t_ready[c], (NLEV - 2) * p + l - 1)
                    for a in range(HG):
                        mm = pe.matmul(bank(2 * c, P)[:, a, :], LT[p % 2][c][:, a, :], T[p % 2][c][:, a, :], start=True, stop=True)
                    mm.then_inc(w_done[c], 1)

            def level_ts(p, l):
                for c in range(NT):
                    done = (NLEV - 1) * p + l
                    pe.wait_ge(z_ready[c], done)
                    if p == 0:
                        pe.wait_ge(odd_ready, l)
                    if done > 1:
                        pe.wait_ge(s_ready[c], done - 1)
                    for a in range(HG):
                        if l < NLEV - 1:
                            pe.matmul(bank(2 * c, P)[:, a, :], S[:, p % LIVE, c, a, :], Z[l][c][:, a, :], start=True, stop=True)
                        mm = pe.matmul(bank(2 * c + 1, P)[:, a, :], Z[l][c][:, a, :], S[:, p % LIVE, c, a, :], start=True, stop=True)
                    mm.then_inc(ts_done[c], 1)

            def apply(p, stage):
                b6, b7 = bank(6, P), bank(7, P)

                def four(b, left, right, done):
                    for a in range(HG):
                        mm = pe.matmul(b[:, a, :], left(a), right(a), start=True, stop=True)
                    mm.then_inc(done, 1)
                last_s = (NLEV - 1) * (p + 1)
                if stage == 1:
                    pe.wait_ge(s_ready[0], last_s)
                    if p:
                        pe.wait_ge(vn_ready, p)
                    four(b6, lambda a: S[:, p % LIVE, 0, a, :], lambda a: vb[:, 0, HG * p + a, :], u_done)
                if stage == 2:
                    pe.wait_ge(u_ready, p + 1)
                    pe.wait_ge(kdec_ready, p + 1)
                    if p:
                        pe.wait_ge(o_ready, 2 * p)
                    four(b7, lambda a: PT[:, p % LIVE, 0, a, :], lambda a: U[:, a, :], o0_done)
                    four(b6, lambda a: kdec[:, a, :], lambda a: U[:, a, :], s1_done)
                if stage == 3:
                    pe.wait_ge(s1_ready, p + 1)
                    four(b6, lambda a: qkvT[:, KT + (HG * p + a) // 2, P:2 * P], lambda a: s1[:, a, :], ks_done)
                    pe.wait_ge(o_ready, 2 * p + 1)
                    four(b7, lambda a: qkvT[:, (HG * p + a) // 2, P:2 * P], lambda a: s1[:, a, :], qs_done)
                if stage == 4:
                    pe.wait_ge(s_ready[1], last_s)
                    pe.wait_ge(r_ready, p + 1)
                    four(b6, lambda a: S[:, p % LIVE, 1, a, :], lambda a: R[:, a, :], vn_done)
                if stage == 5:
                    pe.wait_ge(vn_ready, p + 1)
                    pe.wait_ge(qs_ready, p + 1)
                    four(b7, lambda a: PT[:, p % LIVE, 1, a, :], lambda a: U[:, a, :], o1_done)

            for c in range(NT):
                prep(0, c, 1)
                prep(0, c, 2)
            for p in range(NPAIR + 1):
                for l in range(1, NLEV):
                    if p < NPAIR:
                        level_w(p, l)
                    if p >= 1:
                        apply(p - 1, l)
                    if p < NPAIR - 1:
                        prep(p + 1, (l - 1) // 3, (l - 1) % 3 + 1)
                    if p < NPAIR:
                        level_ts(p, l)

            def turn_y(src, b0, done, wait):
                for kp in range(KT):
                    wait(kp)
                    if kp >= 4:
                        pe.wait_ge(y_op_ready, done + kp - 3)
                    for k in range(2):
                        for t in range(NT):
                            mm = pe.transpose(bank(b0 + kp % 4, P)[:, 2 * k + t, :], src[:, t, (2 * kp + k) * P:(2 * kp + k + 1) * P], ident)
                    mm.then_inc(yT_turned, 1)

            turn_y(zo, 0, 0, lambda kp: pe.wait_ge(og_ready, NT))
            pe.wait_ge(y_op_ready, KT)
            phase("gdn_out", yT_hi, yT_lo, False, deep=True)

            pre_norm(1)
            phase("sc_in", hT_hi, hT_lo, True, norm=1)
            pe.wait_ge(ada_used, ADA_PIECES)
            for a in range(ADA_PIECES):
                mm = pe.matmul(psum[:, 7, a:a + 1], ada_sum[:, a, :], ones[:, 0:1], start=True, stop=True)
            mm.then_inc(mod_done, 1)
            pe.wait_ge(y_op_ready, 2 * KT)
            phase("sc_out", yT_hi, yT_lo, False, deep=True)

            pre_norm(2)
            phase("glu", hT_hi, hT_lo, True, norm=2)
            phase("qk", hT_hi, hT_lo, True)
            def scores(c):
                if c == 0:
                    pe.wait_ge(rp_step, 2 * RH)
                if c < RH:
                    b = psum[:, 4 + c, :]
                    for o, keys, queries in ((b[:, 0:SEQ], slice(0, P), slice(0, SEQ)), (b[:, SEQ:SEQ + P], slice(P, SEQ), slice(P, SEQ))):
                        for d in range(2):
                            mm = pe.matmul(o, qkT[:, KT + 2 * c + d, keys], qkT[:, 2 * c + d, queries], start=(d == 0), stop=(d == 1))
                    mm.then_inc(sco_done, 1)
            phase("v", hT_hi, hT_lo, False, beside=scores)

            def weighted_sums(c):
                h, t = c // NT, c % NT
                pe.wait_ge(st_ready, min(RH, c + 1))
                if c >= 4:
                    pe.wait_ge(gn_ready, c - 3)
                vh = slice(h * RDV, (h + 1) * RDV)
                o = psum[:, 4 + c % 4, :]
                mm = pe.matmul(o, st[:, h, t * P:(t + 1) * P], vt[:, 0, vh], start=True, stop=(t == 0))
                if t:
                    mm = pe.matmul(o, st[:, h, SEQ:SEQ + P], vt[:, 1, vh], start=False, stop=True)
                mm.then_inc(ro_done, 1)
            phase("zret", hT_hi, hT_lo, False, beside=weighted_sums)

            def turn_two(c):
                for kp in (2 * c, 2 * c + 1):
                    if kp == 0:
                        pe.wait_ge(rg_ready, NT * RH)
                    if kp >= 4:
                        pe.wait_ge(y_op_ready, 2 * KT + kp - 3)
                    for k in range(2):
                        for t in range(NT):
                            mm = pe.transpose(bank(4 + kp % 4, P)[:, 2 * k + t, :], vt[:, t, (2 * kp + k) * P:(2 * kp + k + 1) * P], ident)
                    mm.then_inc(yT_turned, 1)
            phase("zconv", hT_hi, hT_lo, True, beside=turn_two)

            def layer_norm(c):
                if c == 0:
                    pe.wait_ge(y_op_ready, 3 * KT)
                    pe.wait_ge(gate_diag, 1)
                    for k in range(KT):
                        mm = pe.matmul(bank(6 + k // 4, P)[:, k % 4, :], ones, gdiag[:, k, :], start=True, stop=True)
                    mm.then_inc(gate_row, 1)
                if c == 2:
                    for n in range(KT):
                        if n < CONV_DVE:
                            pe.wait_ge(cv_ready, n + 1)
                        else:
                            pe.wait_ge(cv_pool_step, (CW + 1) * (n - CONV_DVE + 1))
                        mm = pe.matmul(psum[:, 4, 0:SEQ], ones, cv[:, n, :], start=(n == 0), stop=(n == KT - 1))
                    mm.then_inc(mean_done, 1)
                if c == 4:
                    for n in range(KT):
                        pe.wait_ge(a2_ready, n // 2 + 1)
                        mm = pe.matmul(psum[:, 5, 0:SEQ], ones, a2[:, n, :], start=(n == 0), stop=(n == KT - 1))
                    mm.then_inc(var_done, 1)
            phase("gates", hT_hi, hT_lo, True, beside=layer_norm)
            pe.wait_ge(cop_ready, KT // 2)
            phase("conv_out", cT_hi, cT_lo, True)
            phase("ret_out", yT_hi, yT_lo, True, deep=True)
            pe.wait_ge(mop_ready, KT // 2)
            phase("w_out", hT_hi, hT_lo, False)

        @block.scalar
        def _(act):
            def split_hi(g0, i, j, h):
                if isinstance(i, int) and g0 + 4 * i + j >= CHUNKS:
                    return
                slot = j % RING
                if h == 0:
                    act.wait_ge(raw_ready[slot], i * 16 + 16 * ((g0 + j) // RING + 1))
                act.wait_ge(half_done, i * 8 + (2 * (g0 + j) + h + 1))
                act.activation(w_hi[j % 2 * 2 + h][:, :, :], raw[slot][:, h * KH2:(h + 1) * KH2, :], ACT.Copy).then_inc(hi_ready, 1)

            def split_ahead(g0, i, j):
                split_hi(g0, i, j + 1, 1)
                split_hi(g0, i, j + 2, 0)

            def chunks(name, each=None, unroll=False):
                g0 = FIRST[name]

                def step(i):
                    for j in range(4):
                        split_ahead(g0, i, j)
                        if each is not None:
                            each(i, j, i * 8 + (2 * (g0 + j) + 6))
                if unroll:
                    for i in range(COUNT[name] // 4):
                        step(i)
                else:
                    loop(act, COUNT[name] // 4, step)

            def pre_norm(n, gain=None):
                for t in range(NT):
                    if n == 0:
                        act.wait_ge(x_loaded[t], 16)
                    else:
                        act.wait_ge(x_ready, NT * (n - 1) + t + 1)
                    act.activation(junk[:, t, :], x[:, t, :], ACT.Square, scale=D ** -0.5, accum_out=ss[:, t:t + 1]).then_inc(pre_ss, 1)
                    act.wait_ge(pre_ss, NT * n + t + 1)
                    act.activation(ms[:, t:t + 1], ss[:, t:t + 1], ACT.Sqrt, bias=eps_r[:, :]).then_inc(pre_std, 1)
                if n == 0:
                    split_hi(0, 0, 0, 0)
                    act.wait_ge(par_ready, 1)
                for kp in range(KT // 2):
                    if n < 2:
                        act.wait_ge(turned, KT // 2 * n + kp + 1)
                        for k in range(2):
                            i = act.activation(hT_hi[:, 2 * kp + k, :], bank(4 + kp)[:, k, :], ACT.Copy, scale=gain(2 * kp + k))
                    else:
                        act.wait_ge(hx_ready, kp + 1)
                        i = act.activation(hT_hi[:, 2 * kp:2 * kp + 2, :], hx[:, 2 * kp:2 * kp + 2, :], ACT.Copy)
                    i.then_inc(hhi_ready, 1)
                if n == 0:
                    split_hi(0, 0, 0, 1)
                    split_hi(0, 0, 1, 0)

            def y_squares(n, b, block):
                act.wait_ge(y_ready, block + (4 * n + 1))
                for t in range(NT):
                    i = act.activation(junk[:, t, bass.ds(block * CC, CC)], bank(b)[:, t, :], ACT.Square, scale=D ** -0.5, accum_out=yss[:, t, bass.ds(block, 1)])
                return i

            def post_norm(n):
                act.wait_ge(post_ss, n + 1)
                act.activation(ms[:, 2:2 + NT], ss[:, 2:2 + NT], ACT.Sqrt, bias=eps_r[:, :]).then_inc(post_std, 1)

            def y_halves(n):
                def each(i, j, done):
                    if j % 2:
                        y_squares(n, j // 2, i * 2 + j // 2).then_inc(bank_free, 2)
                return each

            def col(v):
                return lambda k: par[:, 1, v + k:v + k + 1]

            act.wait_ge(cleared, 1)
            pre_norm(0, col(V_PRE))

            def qkv_step(i):
                g0 = FIRST["qkv"]

                def silu(j):
                    act.wait_ge(bank_free, i * 4 + (4 + g0 + j + 1))
                    act.activation(qkvT[:, bass.ds(i * 8 + 2 * j, 2), :], cacc[j % 2][:, :, :], ACT.Silu).then_inc(qkv_ready, 1)
                for j in range(4):
                    split_ahead(g0, i, j)
                    act.wait_ge(half_done, i * 8 + (2 * (g0 + j) + 6))
                    for m in range(2):
                        w = par[:, 0, bass.ds(i * 8 + ((GCONV - 1) * 32 + 2 * j + m), 1)]
                        a = act.activation(cacc[j % 2][:, m, :], bank(j)[:, m, :], ACT.Copy, scale=w)
                    a.then_inc(tap0, 1)
                    if j:
                        silu(j - 1)
                        act.wait_ge(qkv_ready, i * 4 + j)
                silu(3)
                act.wait_ge(qkv_ready, i * 4 + 4)
            loop(act, COUNT["qkv"] // 4, qkv_step)
            act.wait_ge(ba_loaded, 32)
            act.activation(ba_hi[:, :, :], ba_raw[:, :, :], ACT.Copy).then_inc(ba_hi_ready, 1)

            def z_out(i, j, done):
                act.wait_ge(half_done, done)
                act.activation(zo[:, :, bass.ds(i * 1024 + j * CC, CC)], bank(j), ACT.Silu).then_inc(bank_free, 1)
            gr = slice(G_ROW, G_ROW + VH)

            def beside_z(i, j, done):
                z_out(i, j, done)
                c = 4 * i + j
                if c == 0:
                    act.wait_ge(small_loaded, SMALL)
                    act.wait_ge(ba_done, 1)
                    act.wait_ge(cleared, 1)
                    act.activation(bg[0:VH, :], psum[0:VH, 6, 0:SEQ], ACT.Sigmoid).then_inc(beta_ready, 1)
                    act.activation(acols[gr, 2:3], acols[gr, 0:1], ACT.Exp).then_inc(gate_a, 1)
                    act.wait_ge(gate_v, 2)
                    act.activation(gl[gr, :], gl[gr, :], ACT.Exp, scale=-1.0).then_inc(gate_a, 1)
                if c == 1:
                    act.wait_ge(l2_sum, KT)
                    act.activation(lnss[:, :, :].rearrange("p t n -> p (t n)"), psum[:, 7, 0:NT * VH], ACT.Ln, bias=eps_r[:, :]).then_inc(lnss_ready, 1)
                    act.wait_ge(gate_a, 2)
                    act.activation(gs[gr, :], gl[gr, :], ACT.Ln, bias=1.0).then_inc(gate_a, 1)
                if c == 4:
                    act.wait_ge(bgt_ready, 1)
                    act.activation(eg[:, :, :], bgt[:, :, gr], ACT.Exp)
                    act.wait_ge(gk_ready, 1)
                    act.activation(lnss[:, :, :], lnss[:, :, :], ACT.Exp, scale=-0.5).then_inc(eg_ready, 1)
                    act.wait_ge(wd_sub, 1)
                    act.activation(wdec[:, :], wdec[:, :], ACT.Exp).then_inc(wd_ready, 1)
            chunks("z", beside_z, unroll=True)

            def prep(p, c, stage):
                n = NT * p + c
                if stage == 1:
                    act.wait_ge(d_ready, n + 1)
                    act.activation(E[:, :, :], E[:, :, :], ACT.Exp, scale=-1.0).then_inc(e_ready, 1)
                if stage == 3:
                    act.wait_ge(ap_turned, n + 1)
                    if p >= LIVE:
                        act.wait_ge(o1_done, p - LIVE + 1)
                    act.activation(PT[:, p % LIVE, c, :, :], bank(5, P), ACT.Copy).then_inc(pt_ready, 1)

            def level(p, l):
                for c in range(NT):
                    act.wait_ge(ts_done[c], (NLEV - 1) * p + l)
                    if l < NLEV - 1:
                        act.activation(half_heads(T[p % 2][c], l, 0), half_heads(bank(2 * c, P), l, 0), ACT.Copy).then_inc(t_ready[c], 1)

            def apply(p, stage):
                if stage == 1:
                    act.wait_ge(u_done, p + 1)
                    act.activation(U[:, :, :], bank(6, P), ACT.Copy).then_inc(u_ready, 1)
                if stage == 2:
                    act.wait_ge(o0_done, p + 1)
                    act.activation(osq[:, :, :], bank(7, P), ACT.Square).then_inc(osq_ready, 1)
                    act.wait_ge(s1_done, p + 1)
                    act.activation(s1[:, :, :], bank(6, P), ACT.Copy).then_inc(s1_ready, 1)
                if stage == 3:
                    act.wait_ge(qs_done, p + 1)
                    for a in range(HG):
                        h = HG * p + a
                        i = act.activation(qS[:, a, :], bank(7, P)[:, a, :], ACT.Copy, scale=eg[:, 1, h:h + 1])
                    i.then_inc(qs_ready, 1)
                if stage == 4:
                    act.wait_ge(vn_done, p + 1)
                    act.activation(U[:, :, :], bank(6, P), ACT.Copy).then_inc(vn_ready, 1)
                if stage == 5:
                    act.wait_ge(o1_ready, p + 1)
                    act.activation(osq[:, :, :], qS[:, :, :], ACT.Square).then_inc(osq_ready, 1)

            for c in range(NT):
                prep(0, c, 1)
                prep(0, c, 3)
            for p in range(NPAIR + 1):
                for l in range(1, NLEV):
                    if p >= 1:
                        apply(p - 1, l)
                    if p < NPAIR - 1:
                        prep(p + 1, (l - 1) // 3, (l - 1) % 3 + 1)
                    if p < NPAIR:
                        level(p, l)
            act.wait_ge(o_ready, 2 * NPAIR)
            act.activation(o_rs[:, :, :], o_ss[:, :, :], ACT.Sqrt, scale=1.0 / HD, bias=eps_r[:, :]).then_inc(o_std, 1)

            def turn_y(b0, turns):
                for kp in range(KT):
                    act.wait_ge(yT_turned, turns + kp + 1)
                    act.activation(yT_hi[:, 2 * kp:2 * kp + 2, :], bank(b0 + kp % 4), ACT.Copy).then_inc(yhi_ready, 1)

            turn_y(0, 0)

            chunks("gdn_out", y_halves(0))
            post_norm(0)
            pre_norm(1, col(V_PRE + KT))

            def sc_each(i, j, done):
                g = FIRST["sc_in"]
                if j == 0:
                    act.wait_ge(half_done, done)
                    act.activation(sc_u[:, :, :], bank(0), ACT.Copy).then_inc(sc_u_ready, 1)
                if j == 2:
                    act.wait_ge(bank_free, i * 4 + (4 + g + 2))
                    for m in range(2):
                        w = par[:, 1, bass.ds(i * 2 + (V_SC + (SCONV - 1) * 16 + m), 1)]
                        a = act.activation(sc_v[:, m, :], sc_cu[:, m, :], ACT.Copy, scale=w)
                    a.then_inc(sc_v0, 1)
                if j == 3:
                    act.wait_ge(half_done, done)
                    act.activation(sc_z[:, :, :], bank(3), ACT.Silu).then_inc(sc_z_ready, 1)
                    act.wait_ge(bank_free, i * 4 + (4 + g + 4))
                    act.activation(yT_hi[:, bass.ds(i * 2, 2), :], sc_yz[:, :, :], ACT.Copy).then_inc(yhi_ready, 1)
            chunks("sc_in", sc_each)
            chunks("sc_out", y_halves(1))
            post_norm(1)
            pre_norm(2)

            act.wait_ge(ang_ready, 1)
            act.activation(trig[:, :, :], turn[:, :, :], ACT.Sin).then_inc(trig_ready, 1)

            def glu_each(i, j, done):
                if j % 2 == 0:
                    act.wait_ge(half_done, done)
                    act.activation((glu, rp1)[j // 2][:, :, :], bank(j), ACT.Sigmoid).then_inc(glu_ready, 1)
            chunks("glu", glu_each)
            chunks("qk")

            def tokens_out(dst, func):
                def each(i, j, done):
                    act.wait_ge(half_done, done)
                    act.activation(dst[:, :, bass.ds(i * 1024 + j * CC, CC)], bank(j), func).then_inc(bank_free, 1)
                return each

            def channels_out(dst, func):
                def each(i, j, done):
                    act.wait_ge(half_done, done)
                    act.activation(dst[:, bass.ds(i * 8 + 2 * j, 2), :], bank(j), func).then_inc(bank_free, 1)
                return each
            chunks("v", tokens_out(vt, ACT.Copy))
            z_ret = tokens_out(zr, ACT.Silu)

            def group_norm(i, j, done):
                z_ret(i, j, done)
                if j % NT == NT - 1:
                    h = (4 * i + j) // NT
                    act.wait_ge(gn_step, 2 * NT * (h + 1))
                    if h:
                        act.wait_ge(gn_ready, NT * h)
                    act.activation(grs[:, :], gmv[:, :, 1], ACT.Sqrt, bias=eps_n[:, :]).then_inc(gn_std, 1)
                    act.wait_ge(gn_rec, 2 * (h + 1))
                    for t in range(NT):
                        n = NT * h + t
                        if h:
                            act.wait_ge(rg_ready, n - 1)
                        act.activation(og[t][:, :], psum[:, 4 + n % 4, :], ACT.Identity, scale=grs[:, t:t + 1], bias=gnm[:, t:t + 1]).then_inc(gn_ready, 1)
            chunks("zret", group_norm, unroll=True)
            z_conv = channels_out(zc, ACT.Silu)

            def turned_pairs(i, j, done):
                z_conv(i, j, done)
                if j == 0:
                    act.wait_ge(rg_ready, NT * RH)
                for kp in (2 * j, 2 * j + 1):
                    act.wait_ge(yT_turned, KT + kp + 1)
                    act.activation(yT_hi[:, 2 * kp:2 * kp + 2, :], bank(4 + kp % 4), ACT.Copy).then_inc(yhi_ready, 1)
            chunks("zconv", turned_pairs, unroll=True)
            gates = channels_out(gab, ACT.Sigmoid)

            def layer_norm(i, j, done):
                gates(i, j, done)
                c = 4 * i + j
                if c == 2:
                    for q in range(KT // 2):
                        pair = slice(2 * q, 2 * q + 2)
                        act.wait_ge(xc_ready, q + 1)
                        act.activation(a2[:, pair, :], cv[:, pair, :], ACT.Square).then_inc(a2_ready, 1)
                if c == 4:
                    act.wait_ge(var_done, 1)
                    act.activation(lnm[:, 1, :], psum[:, 5, 0:SEQ], ACT.Sqrt, scale=1.0 / D, bias=eps_n[:, :]).then_inc(ln_step, 1)
                if c == 5:
                    for n in range(KT):
                        act.wait_ge(lns_ready, n // 2 + 1)
                        act.activation(cv[:, n, :], cv[:, n, :], ACT.Silu, scale=par[:, 1, V_LG + n:V_LG + n + 1],
                                       bias=par[:, 1, V_LB + n:V_LB + n + 1]).then_inc(lna_ready, 1)
                if c == 6:
                    for q in range(KT // 2):
                        pair = slice(2 * q, 2 * q + 2)
                        act.wait_ge(lnz_ready, q + 1)
                        act.activation(cT_hi[:, pair, :], cv[:, pair, :], ACT.Copy).then_inc(chi_ready, 1)
            chunks("gates", layer_norm, unroll=True)
            chunks("conv_out")

            def merged(i, j, done):
                if j % 2:
                    b = i * 2 + j // 2
                    act.wait_ge(mg_ready, b + 1)
                    act.activation(hT_hi[:, bass.ds(b * 2, 2), :], rp2[:, :, :], ACT.Copy).then_inc(mhi_ready, 1)
            chunks("ret_out", merged)

            def y_out(i, j, done):
                y_squares(2, j, j).then_inc(bank_free, 1)
            chunks("w_out", y_out)
            post_norm(2)

        @block.gpsimd
        def _(pool):
            pool.memset(ba_raw[:, :, :], 0.0).then_inc(padded, 1)
            for n in range(KT):
                pool.wait_ge(qkv_ready, n + 1)
                if n >= 2:
                    pool.wait_ge(l2_sum, n - 1)
                qk = qkvT[:, 2 * n:2 * n + 2, :]
                pool.tensor_tensor(sq[n % 2][:, :, :], qk, qk, ALU.mult).then_inc(sq_ready, 1)
            pool.wait_ge(small_loaded, SMALL)
            for c in range(COUNT["z"]):
                pool.wait_ge(bank_free, 4 + FIRST["z"] + c + 1)
                z = zo[:, :, c * CC:(c + 1) * CC].rearrange("p t (h d) -> p t h d", d=HD)
                w = nw_row[:, :].rearrange("p (t h d) -> p t h d", t=1, h=1).to_broadcast([P, NT, CC // HD, HD])
                pool.tensor_tensor(z, z, w, ALU.mult).then_inc(zn_ready, 1)

            def prep(p, c, stage):
                n = NT * p + c
                if stage == 1:
                    pool.wait_ge(e_ready, n + 1)
                    if n:
                        pool.wait_ge(l_ready, n)
                        pool.wait_ge(chain_ready, n)
                    pool.tensor_tensor(A[:, :, :], E[:, :, :], heads(const[:, C_LOW, :], HG), ALU.mult).then_inc(masked, 1)
                if stage == 3:
                    pool.wait_ge(ap_turned, n + 1)
                    pool.tensor_tensor(A[:, :, :], A[:, :, :], heads(ident, HG), ALU.add).then_inc(l_ready, 1)
                    pool.wait_ge(l_ready, n + 1)
                    pool.tensor_tensor(T[p % 2][c][:, :, :], A[:, :, :], heads(const[:, C_M0, :], HG), ALU.mult)
                    pool.wait_ge(lt_ready, n + 1)
                    if p >= LIVE:
                        pool.wait_ge(vn_done, p - LIVE + 1)
                    pool.tensor_tensor(S[:, p % LIVE, c, :, :], LT[p % 2][c][:, :, :], heads(const[:, C_M0T, :], HG), ALU.mult).then_inc(chain_ready, 1)

            def apply(p, stage):
                if stage == 1:
                    pool.wait_ge(wd_ready, 1)
                    pool.wait_ge(ktok_ready, 2)
                    if p:
                        pool.wait_ge(s1_done, p)
                    for a in range(HG):
                        h = HG * p + a
                        i = pool.tensor_scalar(kdec[:, a, :], ktok[:, h // 2, :], wdec[:, h:h + 1], None, ALU.mult)
                    i.then_inc(kdec_ready, 1)

            def odd_columns(l):
                for c in range(NT):
                    i = pool.tensor_copy(half_heads(Z[l][c], l, 1), half_of_each(ident, l, 1))
                i.then_inc(odd_ready, 1)
            pool.wait_ge(v_turned, 2 * NPAIR)
            for l in (1, 2):
                odd_columns(l)
            for c in range(NT):
                prep(0, c, 1)
                prep(0, c, 3)
            pool.wait_ge(lo_ready, 2 * FIRST["gdn_out"])
            for l in range(3, NLEV):
                odd_columns(l)
            for p in range(NPAIR + 1):
                for l in range(1, NLEV):
                    if p >= 1:
                        apply(p - 1, l)
                    if p < NPAIR - 1:
                        prep(p + 1, (l - 1) // 3, (l - 1) % 3 + 1)
            def ada_pieces(i):
                for j in range(ADA_SLOTS):
                    a = ada[j]
                    pool.wait_ge(ada_ready[j], i * 16 + 16)
                    c = par[:, 1, V_C:V_C + KT].rearrange("p (k n) -> p k n", n=1).to_broadcast([P, KT, P])
                    pool.tensor_tensor(a[:, :, :], a[:, :, :], c, ALU.mult).then_inc(ada_step, 1)
                    for q, n in enumerate((4, 2)):
                        pool.wait_ge(ada_step, i * (3 * ADA_SLOTS) + (3 * j + q + 1))
                        pool.tensor_tensor(a[:, 0:n, :], a[:, 0:n, :], a[:, n:2 * n, :], ALU.add).then_inc(ada_step, 1)
                    pool.wait_ge(ada_step, i * (3 * ADA_SLOTS) + (3 * j + 3))
                    pool.tensor_tensor(ada_sum[:, bass.ds(i * ADA_SLOTS + j, 1), :], a[:, 0:1, :], a[:, 1:2, :], ALU.add).then_inc(ada_used, 1)
            pool.wait_ge(par_ready, 1)
            loop(pool, ADA_PIECES // ADA_SLOTS, ada_pieces)
            def tap_product(n, j, tap):
                w = par[:, 2:4, :].rearrange("p a n -> p (a n)")[:, bass.ds(tap * KT + n, 1)].to_broadcast([P, SEQ])
                pool.tensor_tensor(tapped[:, j, :], aP[:, n, bass.ds(tap, SEQ)], w, ALU.mult).then_inc(tapped_ready, 1)

            def first_tap(n):
                q = n - CONV_DVE
                pool.tensor_tensor(cv[:, n, :], aP[:, n, 0:SEQ], par[:, 2, n:n + 1].to_broadcast([P, SEQ]), ALU.mult).then_inc(cv_pool_step, 1)
                pool.wait_ge(cv_pool_step, CW * q + q + 1)
                pool.tensor_tensor(cv[:, n, :], cv[:, n, :], par[:, 1, V_CB + n:V_CB + n + 1].to_broadcast([P, SEQ]), ALU.add).then_inc(cv_pool_step, 1)

            def pairs_of_taps(n, first, last):
                q = n - CONV_DVE
                with pool.Fori(first, last) as i:
                    for j in range(2):
                        tap_product(n, j, i * 2 + (1 + j))
                    for j in range(2):
                        pool.wait_ge(tapped_ready, i * 2 + (q * (CW - 1) + j + 1))
                        pool.wait_ge(cv_pool_step, i * 2 + (q * (CW + 1) + 2 + j))
                        pool.tensor_tensor(cv[:, n, :], cv[:, n, :], tapped[:, j, :], ALU.add).then_inc(cv_pool_step, 1)
                    pool.wait_ge(cv_pool_step, i * 2 + (q * (CW + 1) + 4))
            pool.wait_ge(padded, 2)
            pool.wait_ge(bank_free, 4 + FIRST["qk"])
            half_taps = (CW - 1) // 2
            for n in range(CONV_DVE, KT - 1):
                first_tap(n)
                pairs_of_taps(n, 0, half_taps)
            first_tap(KT - 1)
            shares = [half_taps * h // RH for h in range(RH + 1)]
            for h in range(RH):
                pairs_of_taps(KT - 1, shares[h], shares[h + 1])
                for t in range(NT):
                    n = NT * h + t
                    pool.wait_ge(gn_ready, n + 1)
                    vh = slice(h * RDV, (h + 1) * RDV)
                    pool.tensor_tensor(vt[:, t, vh], og[t][:, :], zr[:, t, vh], ALU.mult).then_inc(rg_ready, 1)

        @block.vector
        def _(dve):
            def part_lo(o, whole, hi):
                return dve.tensor_tensor(o, whole, hi.bitcast(F32), ALU.subtract)

            def split_lo(g0, i, j, h):
                if isinstance(i, int) and g0 + 4 * i + j >= CHUNKS:
                    return
                s = j % 2 * 2 + h
                dve.wait_ge(hi_ready, i * 8 + (2 * (g0 + j) + h + 1))
                part_lo(w_lo[s][:, :, :], raw[j % RING][:, h * KH2:(h + 1) * KH2, :], w_hi[s][:, :, :]).then_inc(lo_ready, 1)

            def chunks(name, each=None, unroll=False):
                g0 = FIRST[name]

                def step(i):
                    for j in range(4):
                        split_lo(g0, i, j + 1, 1)
                        split_lo(g0, i, j + 2, 0)
                        if each is not None:
                            each(i, j, i * 8 + (2 * (g0 + j) + 6))
                if unroll:
                    for i in range(COUNT[name] // 4):
                        step(i)
                else:
                    loop(dve, COUNT[name] // 4, step)

            def pre_norm(n, gain, shift=None, between=None):
                for t in range(NT):
                    dve.wait_ge(pre_std, NT * n + t + 1)
                    dve.reciprocal(rstd[:, t:t + 1], ms[:, t:t + 1]).then_inc(pre_rstd, 1)
                    dve.wait_ge(pre_rstd, NT * n + t + 1)
                    dve.tensor_scalar(xn[:, t, :], x[:, t, :], rstd[:, t:t + 1], None, ALU.mult).then_inc(xn_ready, 1)
                if between is not None:
                    between()
                def shifted(kp):
                    dve.wait_ge(turned, KT // 2 * n + kp + 1)
                    for k in (2 * kp, 2 * kp + 1):
                        i = dve.tensor_scalar(hx[:, k, :], bank(4 + kp)[:, k % 2, :], gain(k), shift(k), ALU.mult, ALU.add)
                    i.then_inc(hx_ready, 1)

                for kp in range(KT // 2):
                    if shift is not None and kp % 2 == 0:
                        shifted(kp)
                        shifted(kp + 1)
                    dve.wait_ge(hhi_ready, KT // 2 * n + kp + 1)
                    if shift is not None:
                        pair = slice(2 * kp, 2 * kp + 2)
                        i = part_lo(hT_lo[:, pair, :], hx[:, pair, :], hT_hi[:, pair, :])
                    else:
                        for k in (2 * kp, 2 * kp + 1):
                            i = dve.scalar_tensor_tensor(out=hT_lo[:, k, :], in0=bank(4 + kp)[:, k % 2, :], scalar=gain(k),
                                                         in1=hT_hi[:, k, :].bitcast(F32), op0=ALU.mult, op1=ALU.subtract)
                    i.then_inc(h_ready, 1)

            def y_block(n, b, block, columns):
                dve.wait_ge(row_loaded, 16 * (n + 1))
                w = row[:, columns].rearrange("p (a n) -> p a n", a=1).to_broadcast([P, NT, CC])
                dve.tensor_tensor(xn[:, :, columns], bank(b), w, ALU.mult).then_inc(y_ready, 1)

            def y_halves(n):
                def each(i, j, done):
                    if j % 2:
                        dve.wait_ge(half_done, done)
                        y_block(n, j // 2, i * 2 + j // 2, bass.ds(i * (2 * CC) + j // 2 * CC, CC))
                return each

            def post_norm(n, name):
                dve.wait_ge(bank_free, 4 + FIRST[name] + COUNT[name])
                dve.tensor_reduce(ss[:, 2:2 + NT], yss[:, :, :], AX_X, ALU.add).then_inc(post_ss, 1)
                dve.wait_ge(post_std, n + 1)
                dve.reciprocal(rstd[:, 2:2 + NT], ms[:, 2:2 + NT]).then_inc(post_rstd, 1)
                dve.wait_ge(post_rstd, n + 1)
                for t in range(NT):
                    dve.scalar_tensor_tensor(out=x[:, t, :], in0=xn[:, t, :], scalar=rstd[:, 2 + t:3 + t], in1=x[:, t, :],
                                             op0=ALU.mult, op1=ALU.add).then_inc(x_ready, 1)

            def col(v, k):
                return par[:, 1, v + k:v + k + 1]

            dve.memset(eps_r[:, :], RMS_EPS)
            dve.memset(eps_n[:, :], NORM_EPS)
            dve.memset(bg[:, :], 0.0).then_inc(cleared, 1)
            dve.memset(gain2[:, 0:1], 0.0).then_inc(bank_free, 4)
            dve.memset(gain2[:, 1:2], 0.0).then_inc(half_done, 4)
            def small_columns():
                dve.wait_ge(par_turned, 1)
                dve.tensor_copy(par[:, :, :].rearrange("p a n -> p (a n)")[:, 0:504], psum[:, 7, 0:504]).then_inc(par_ready, 1)
                split_lo(0, 0, 0, 0)
                dve.wait_ge(par_ready, 1)
            pre_norm(0, lambda k: col(V_PRE, k), between=small_columns)
            split_lo(0, 0, 0, 1)
            split_lo(0, 0, 1, 0)

            def taps(i, j, done):
                g0 = FIRST["qkv"]
                dve.wait_ge(tap0, i * 4 + (g0 + j + 1))
                n = 0
                for tap in range(GCONV - 2, -1, -1):
                    s = GCONV - 1 - tap
                    for m in range(2):
                        if n >= 2:
                            dve.wait_ge(tap_step, i * 20 + (5 * j + n - 1))
                        o = cacc[j % 2][:, m, s:SEQ]
                        a = dve.scalar_tensor_tensor(out=o, in0=bank(j)[:, m, 0:SEQ - s],
                                                     scalar=par[:, 0, bass.ds(i * 8 + (tap * 32 + 2 * j + m), 1)],
                                                     in1=o, op0=ALU.mult, op1=ALU.add)
                        n += 1
                        if n < 6:
                            a.then_inc(tap_step, 1)
                        else:
                            a.then_inc(bank_free, 1)
            chunks("qkv", taps)
            dve.wait_ge(ba_hi_ready, 1)
            part_lo(ba_lo[:, :, :], ba_raw[:, :, :], ba_hi[:, :, :]).then_inc(ba_lo_ready, 1)
            gr = slice(G_ROW, G_ROW + VH)

            def beside_z(i, j, done):
                c = 4 * i + j
                if c == 0:
                    dve.wait_ge(small_loaded, SMALL)
                    dve.wait_ge(ba_done, 1)
                    dve.tensor_scalar(gz[gr, :], psum[gr, 6, 0:SEQ], acols[gr, 1:2], None, ALU.add).then_inc(gate_v, 1)
                    dve.wait_ge(gate_v, 1)
                    dve.scalar_tensor_tensor(out=gl[gr, :], in0=gz[gr, :], scalar=-1.0, in1=gz[gr, :], op0=ALU.mult, op1=ALU.max).then_inc(gate_v, 1)
                if c == 2:
                    dve.wait_ge(gate_a, 3)
                    dve.scalar_tensor_tensor(out=gs[gr, :], in0=gz[gr, :], scalar=0.0, in1=gs[gr, :], op0=ALU.max, op1=ALU.add).then_inc(gate_v, 1)
                    dve.wait_ge(gate_v, 3)
                    dve.tensor_scalar(gz[gr, :], gs[gr, :], acols[gr, 2:3], -1.0, ALU.mult, ALU.mult).then_inc(gate_v, 1)
                    dve.wait_ge(gate_v, 4)
                    for t in range(NT):
                        cs = slice(t * P, (t + 1) * P)
                        dve.tensor_tensor_scan(bg[gr, cs], const[gr, C_ONE, :], gz[gr, cs], 0.0, ALU.mult, ALU.add).then_inc(g_ready, 1)
                if c == 3:
                    dve.wait_ge(bg_turned, 1)
                    dve.tensor_copy(bgt[:, :, :], bank(6, P)[:, 0:NT, :]).then_inc(bgt_ready, 1)
                    dve.wait_ge(bgt_ready, 1)
                    dve.wait_ge(lnss_ready, 1)
                    for t in range(NT):
                        lk = lnss[:, t, KH:2 * KH].rearrange("p (n r) -> p n r", r=1).to_broadcast([P, KH, 2])
                        i = dve.scalar_tensor_tensor(out=gk[:, t, :].rearrange("p (n r) -> p n r", r=2), in0=lk, scalar=0.5,
                                                     in1=bgt[:, t, gr].rearrange("p (n r) -> p n r", r=2), op0=ALU.mult, op1=ALU.add)
                    i.then_inc(gk_ready, 1)
                    dve.wait_ge(gk_ready, 1)
                    dve.wait_ge(glast_ready, 1)
                    dve.tensor_tensor(wdec[:, :], psum[:, 7, 2 * VH:3 * VH], gk[:, 0, :], ALU.subtract).then_inc(wd_sub, 1)
                if c >= 4:
                    for n in (2 * (c - 4), 2 * (c - 4) + 1):
                        t, q = n // NPAIR, n % NPAIR
                        dve.wait_ge(v_turned, n + 1)
                        for a in range(HG):
                            h = HG * q + a
                            v = dve.tensor_scalar(vb[:, t, h, :], bank(6 + n % 2, P)[:, a, :], bgt[:, t, h:h + 1], None, ALU.mult)
                        v.then_inc(vb_ready, 1)
                if c == 5:
                    dve.wait_ge(eg_ready, 1)
                    rk, rq = two_each(lnss[:, :, KH:2 * KH]), lnss[:, :, 0:KH]
                    def pairs_of(ap):
                        return ap.rearrange("p t (n r) -> p t n r", r=2)
                    dve.tensor_scalar(rqs[:, :, :], rq, HD ** -0.5, None, ALU.mult).then_inc(rows_step, 1)
                    dve.tensor_tensor(pairs_of(brk[:, :, :]), pairs_of(bgt[:, :, 0:VH]), rk, ALU.mult).then_inc(rows_step, 1)
                    dve.wait_ge(rows_step, 2)
                    dve.scalar_tensor_tensor(out=nbeg[:, :, :], in0=brk[:, :, :], scalar=-1.0, in1=eg[:, :, :], op0=ALU.mult,
                                             op1=ALU.mult).then_inc(rows_step, 1)
                    dve.wait_ge(rows_step, 3)
                    dve.tensor_tensor(pairs_of(eg[:, :, :]), pairs_of(eg[:, :, :]), two_each(rqs[:, :, :]), ALU.mult).then_inc(rows_step, 1)
                    dve.wait_ge(rows_step, 4)
                if c == COUNT["z"] - 1:
                    for n in range(2):
                        dve.wait_ge(k_turned, n + 1)
                        dve.tensor_copy(ktok[:, HG * n:HG * (n + 1), :], bank(6 + n, P)).then_inc(ktok_ready, 1)
            chunks("z", beside_z, unroll=True)

            def prep(p, c, stage):
                n = NT * p + c
                if stage == 1:
                    dve.wait_ge(grow_ready, n + 1)
                    for a in range(HG):
                        g = G_ROW + HG * p + a
                        i = dve.scalar_tensor_tensor(out=E[:, a, :], in0=bank(4, P)[:, a, :], scalar=bgt[:, c, g:g + 1], in1=const[:, C_FLOOR, :],
                                                     op0=ALU.subtract, op1=ALU.max)
                    i.then_inc(d_ready, 1)
                if stage == 2:
                    dve.wait_ge(kq_ready, n + 1)
                    dve.wait_ge(e_ready, n + 1)
                    if n:
                        dve.wait_ge(ap_turned, n)
                    for e in range(2):
                        q = bank(5, P)[:, 2 + e, :].rearrange("p (r n) -> p r n", r=1).to_broadcast([P, 2, P])
                        dve.scalar_tensor_tensor(out=Di[:, 2 * e:2 * e + 2, :], in0=q, scalar=rqs[:, c, 2 * p + e:2 * p + e + 1],
                                                 in1=E[:, 2 * e:2 * e + 2, :], op0=ALU.mult, op1=ALU.mult)
                    dve.wait_ge(masked, n + 1)
                    for a in range(HG):
                        h = HG * p + a
                        i = dve.scalar_tensor_tensor(out=A[:, a, :], in0=bank(5, P)[:, a // 2, :], scalar=brk[:, c, h:h + 1],
                                                     in1=A[:, a, :], op0=ALU.mult, op1=ALU.mult)
                    i.then_inc(ap_ready, 1)
                if stage == 3:
                    dve.wait_ge(ap_turned, n + 1)
                    dve.tensor_tensor(LT[p % 2][c][:, :, :], bank(4, P), heads(ident, HG), ALU.add).then_inc(lt_ready, 1)

            def level_z(p, l):
                for c in range(NT):
                    dve.wait_ge(w_done[c], (NLEV - 1) * p + l)
                    dve.tensor_tensor(half_heads(Z[l][c], l, 0), half_heads(bank(2 * c, P), l, 0), half_of_each(const[:, C_MASK + l - 1, :], l, 0), ALU.mult).then_inc(z_ready[c], 1)

            def level_s(p, l):
                for c in range(NT):
                    dve.wait_ge(ts_done[c], (NLEV - 1) * p + l)
                    dve.tensor_copy(half_heads(S[:, p % LIVE, c, :, :], l, 1), half_heads(bank(2 * c + 1, P), l, 1)).then_inc(s_ready[c], 1)

            def gated(p, t, o):
                hs = slice(HG * p, HG * (p + 1))
                dve.wait_ge(osq_ready, 2 * p + t + 1)
                dve.tensor_reduce(o_ss[:, t, hs], osq[:, :, :], AX_X, ALU.add)
                z = zo[:, t, HG * p * HD:HG * (p + 1) * HD].rearrange("p (h d) -> p h d", d=HD)
                dve.tensor_tensor(z, o, z, ALU.mult).then_inc(o_ready, 1)

            def apply(p, stage):
                if stage == 2:
                    dve.wait_ge(zn_ready, COUNT["z"])
                    gated(p, 0, bank(7, P))
                if stage == 3:
                    dve.wait_ge(ks_done, p + 1)
                    for a in range(HG):
                        h = HG * p + a
                        i = dve.scalar_tensor_tensor(out=R[:, a, :], in0=bank(6, P)[:, a, :], scalar=nbeg[:, 1, h:h + 1],
                                                     in1=vb[:, 1, h, :], op0=ALU.mult, op1=ALU.add)
                    i.then_inc(r_ready, 1)
                if stage == 5:
                    dve.wait_ge(o1_done, p + 1)
                    dve.tensor_tensor(qS[:, :, :], bank(7, P), qS[:, :, :], ALU.add).then_inc(o1_ready, 1)
                    dve.wait_ge(o1_ready, p + 1)
                    gated(p, 1, qS[:, :, :])

            for c in range(NT):
                for stage in (1, 2, 3):
                    prep(0, c, stage)
            for p in range(NPAIR + 1):
                for l in range(1, NLEV):
                    if p < NPAIR:
                        level_z(p, l)
                    if p >= 1:
                        apply(p - 1, l)
                    if p < NPAIR - 1:
                        prep(p + 1, (l - 1) // 3, (l - 1) % 3 + 1)
                    if p < NPAIR:
                        level_s(p, l)
            dve.wait_ge(o_ready, 2 * NPAIR)
            dve.wait_ge(o_std, 1)
            dve.reciprocal(o_rs[:, :, :], o_rs[:, :, :]).then_inc(o_rstd, 1)
            dve.wait_ge(o_rstd, 1)
            for t in range(NT):
                z = zo[:, t, :].rearrange("p (h d) -> p h d", d=HD)
                r = o_rs[:, t, :].rearrange("p (h d) -> p h d", d=1).to_broadcast([P, VH, HD])
                dve.tensor_tensor(z, z, r, ALU.mult).then_inc(og_ready, 1)

            def turn_y(b0, done):
                for kp in range(KT):
                    pair = slice(2 * kp, 2 * kp + 2)
                    dve.wait_ge(yhi_ready, done + kp + 1)
                    part_lo(yT_lo[:, pair, :], bank(b0 + kp % 4), yT_hi[:, pair, :]).then_inc(y_op_ready, 1)

            turn_y(0, 0)
            chunks("gdn_out", y_halves(0))
            post_norm(0, "gdn_out")
            pre_norm(1, lambda k: col(V_PRE + KT, k))

            def sc_each(i, j, done):
                g = FIRST["sc_in"]
                if j == 1:
                    dve.wait_ge(half_done, done)
                    dve.wait_ge(sc_u_ready, i + 1)
                    dve.tensor_tensor(sc_cu[:, :, :], bank(1), sc_u[:, :, :], ALU.mult).then_inc(bank_free, 2)
                if j == 2:
                    dve.wait_ge(sc_v0, i + 1)
                    n = 0
                    for tap in range(SCONV - 2, -1, -1):
                        s = SCONV - 1 - tap
                        for m in range(2):
                            if n >= 2:
                                dve.wait_ge(sc_step, i * 4 + (n - 1))
                            o = sc_v[:, m, s:SEQ]
                            dve.scalar_tensor_tensor(out=o, in0=sc_cu[:, m, 0:SEQ - s],
                                                     scalar=par[:, 1, bass.ds(i * 2 + (V_SC + tap * 16 + m), 1)],
                                                     in1=o, op0=ALU.mult, op1=ALU.add).then_inc(sc_step, 1)
                            n += 1
                    dve.wait_ge(half_done, done)
                    dve.wait_ge(sc_step, i * 4 + 4)
                    dve.tensor_tensor(sc_y[:, :, :], bank(2), sc_v[:, :, :], ALU.mult).then_inc(bank_free, 1)
                if j == 3:
                    dve.wait_ge(sc_z_ready, i + 1)
                    dve.wait_ge(bank_free, i * 4 + (4 + g + 3))
                    dve.tensor_tensor(sc_yz[:, :, :], sc_y[:, :, :], sc_z[:, :, :], ALU.mult).then_inc(bank_free, 1)
                    dve.wait_ge(yhi_ready, i + (KT + 1))
                    pair = bass.ds(i * 2, 2)
                    part_lo(yT_lo[:, pair, :], sc_yz[:, :, :], yT_hi[:, pair, :]).then_inc(y_op_ready, 1)
            chunks("sc_in", sc_each)
            def shift_scale_gate():
                dve.wait_ge(mod_done, 1)
                dve.tensor_tensor(mod[:, :], psum[:, 7, 0:3 * KT], par[:, 1, V_BADA:V_BADA + 3 * KT], ALU.add).then_inc(mod_ready, 1)
                dve.wait_ge(mod_ready, 1)
                dve.scalar_tensor_tensor(out=gain2[:, :], in0=mod[:, KT:2 * KT], scalar=1.0, in1=par[:, 1, V_PRE2:V_PRE2 + KT],
                                         op0=ALU.add, op1=ALU.mult).then_inc(gain2_ready, 1)

            def angles():
                pi = math.pi
                c1 = 6.28125
                c2 = float(np.float32(np.float32((2 * pi - c1) * 2 ** 20).astype(np.int32) / np.float32(2 ** 20)))
                c3 = 2 * pi - c1 - c2
                magic = 1.5 * 2.0 ** 23
                cos_t, sin_t = turn[:, 0, :], turn[:, 1, :]
                angle_steps = [0]

                def angle(i):
                    angle_steps[0] += 1
                    i.then_inc(ang_step, 1)
                    dve.wait_ge(ang_step, angle_steps[0])
                dve.wait_ge(rope_loaded, 16)
                angle(dve.tensor_copy(ang[:, :], pos_i[:, :]))
                angle(dve.tensor_scalar(ang[:, :], ang[:, :], freq[:, :], None, ALU.mult))
                angle(dve.tensor_scalar(cos_t, ang[:, :], 1.0 / (2 * pi), magic, ALU.mult, ALU.add))
                angle(dve.tensor_scalar(cos_t, cos_t, magic, None, ALU.subtract))
                for c in (c1, c2, c3):
                    angle(dve.scalar_tensor_tensor(out=ang[:, :], in0=cos_t, scalar=-c, in1=ang[:, :], op0=ALU.mult, op1=ALU.add))
                lim = float(np.nextafter(np.float32(pi), np.float32(0)))
                angle(dve.tensor_scalar(sin_t, ang[:, :], lim, -lim, ALU.min, ALU.max))
                angle(dve.tensor_scalar(ang[:, :], ang[:, :], pi / 2, None, ALU.add))
                angle(dve.tensor_scalar(cos_t, ang[:, :], pi, -2 * pi, ALU.is_gt, ALU.mult))
                angle(dve.tensor_tensor(cos_t, cos_t, ang[:, :], ALU.add))
                dve.tensor_scalar(cos_t, cos_t, lim, -lim, ALU.min, ALU.max).then_inc(ang_ready, 1)

            def beside_sc_out(i, j, done):
                y_halves(1)(i, j, done)
                if i == 0 and j == 0:
                    shift_scale_gate()
                if i == 0 and j == 2:
                    angles()
            chunks("sc_out", beside_sc_out, unroll=True)
            post_norm(1, "sc_out")
            dve.wait_ge(gain2_ready, 1)
            pre_norm(2, lambda k: gain2[:, k:k + 1], lambda k: mod[:, k:k + 1])
            dve.memset(aP[:, :, 0:CPAD], 0.0).then_inc(padded, 1)

            def glu_each(i, j, done):
                if j % 2:
                    dve.wait_ge(half_done, done)
                    dve.wait_ge(glu_ready, i * 2 + (j // 2 + 1))
                    dve.tensor_tensor(aP[:, bass.ds(i * 4 + j // 2 * 2, 2), CPAD:CPAD + SEQ], bank(j), (glu, rp1)[j // 2][:, :, :],
                                      ALU.mult).then_inc(bank_free, 2)
            chunks("glu", glu_each)
            dve.wait_ge(trig_ready, 1)
            cos2, sin2 = (trig[:, s, :].rearrange("p (a n) -> p a n", a=1).to_broadcast([P, 2, SEQ]) for s in range(2))

            def rotate(i, j, done):
                dve.wait_ge(half_done, done)
                dve.tensor_tensor(rp1[:, :, :], bank(j), cos2, ALU.mult)
                dve.tensor_tensor(rp2[:, :, :], bank(j), sin2, ALU.mult).then_inc(bank_free, 1)
                dve.wait_ge(bank_free, i * 4 + (4 + FIRST["qk"] + j + 1))
                dve.tensor_tensor(qkT[:, bass.ds(i * 8 + 2 * j, 1), :], rp1[:, 0:1, :], rp2[:, 1:2, :], ALU.subtract)
                dve.tensor_tensor(qkT[:, bass.ds(i * 8 + (2 * j + 1), 1), :], rp2[:, 0:1, :], rp1[:, 1:2, :], ALU.add).then_inc(rp_step, 1)
                dve.wait_ge(rp_step, i * 4 + (j + 1))
            chunks("qk", rotate)

            def conv_op(n, tap):
                def w(j):
                    return par[:, 2 + j // 16, j % 16 * KT + n:j % 16 * KT + n + 1]
                step = CW * n + tap
                if 2 <= tap < CW:
                    dve.wait_ge(cv_step, step - 1)
                if tap == 1 and n:
                    dve.wait_ge(cv_ready, n)
                o = cvo[:, :] if tap % 2 else cv[:, n, :]
                if tap < CW:
                    src = aP[:, n, tap:tap + SEQ]
                if tap == CW:
                    dve.wait_ge(cv_step, step)
                    dve.tensor_tensor(cv[:, n, :], cv[:, n, :], cvo[:, :], ALU.add).then_inc(cv_ready, 1)
                elif tap == 0:
                    dve.tensor_scalar(o, src, w(0), col(V_CB, n), ALU.mult, ALU.add).then_inc(cv_step, 1)
                elif tap == 1:
                    dve.tensor_scalar(o, src, w(1), None, ALU.mult).then_inc(cv_step, 1)
                else:
                    dve.scalar_tensor_tensor(out=o, in0=src, scalar=w(tap), in1=o, op0=ALU.mult, op1=ALU.add).then_inc(cv_step, 1)

            conv_ops = [(n, tap) for n in range(CONV_DVE) for tap in range(CW + 1)]

            def conv_share(n):
                for _ in range(min(n, len(conv_ops))):
                    conv_op(*conv_ops.pop(0))

            def decayed(i, j, done):
                c = 4 * i + j
                conv_share(8)
                if c < RH:
                    dve.wait_ge(sco_done, c + 1)
                    dve.tensor_tensor(st[:, c, :], psum[:, 4 + c, 0:3 * P], decay[:, c, :], ALU.mult).then_inc(st_ready, 1)
            dve.wait_ge(padded, 2)
            dve.wait_ge(decay_loaded, 16)
            dve.wait_ge(bank_free, 4 + FIRST["v"])
            chunks("v", decayed, unroll=True)

            def group_norm(i, j, done):
                n = 4 * i + j
                h, t = n // NT, n % NT
                conv_share(6)
                dve.wait_ge(ro_done, n + 1)
                dve.bn_stats(gst[:, t, :], psum[:, 4 + n % 4, :]).then_inc(gn_step, 1)
                dve.wait_ge(gn_step, 2 * n + 1)
                if h:
                    dve.wait_ge(gn_rec, 2 * h)
                dve.bn_aggr(gmv[:, t, :], gst[:, t, :]).then_inc(gn_step, 1)
                if t == NT - 1:
                    dve.wait_ge(gn_std, h + 1)
                    dve.reciprocal(grs[:, :], grs[:, :]).then_inc(gn_rec, 1)
                    dve.wait_ge(gn_rec, 2 * h + 1)
                    dve.scalar_tensor_tensor(out=gnm[:, :], in0=gmv[:, :, 0], scalar=-1.0, in1=grs[:, :], op0=ALU.mult, op1=ALU.mult).then_inc(gn_rec, 1)
            chunks("zret", group_norm, unroll=True)

            def turned_pairs(i, j, done):
                conv_share(8)
                for kp in (2 * j, 2 * j + 1):
                    pair = slice(2 * kp, 2 * kp + 2)
                    dve.wait_ge(yhi_ready, 2 * KT + kp + 1)
                    part_lo(yT_lo[:, pair, :], bank(4 + kp % 4), yT_hi[:, pair, :]).then_inc(y_op_ready, 1)
            chunks("zconv", turned_pairs, unroll=True)
            mean, inv = (lnm[:, s, :].rearrange("p (a n) -> p a n", a=1).to_broadcast([P, 2, SEQ]) for s in range(2))
            pairs = [slice(2 * q, 2 * q + 2) for q in range(KT // 2)]

            def layer_norm(i, j, done):
                c = 4 * i + j
                if c == 0:
                    for k in range(KT):
                        i = dve.tensor_scalar(gdiag[:, k, :], ident, mod[:, 2 * KT + k:2 * KT + k + 1], None, ALU.mult)
                    i.then_inc(gate_diag, 1)
                if c < 2:
                    conv_share(len(conv_ops) if c else 8)
                if c == 2:
                    dve.wait_ge(gate_row, 1)
                    dve.wait_ge(row_loaded, 16 * 3)
                    for s in range(2):
                        half = slice(512 * s, 512 * (s + 1))
                        dve.tensor_tensor(row[:, half], row[:, half], psum[:, 6 + s, :], ALU.mult).then_inc(row_mul, 1)
                    dve.wait_ge(mean_done, 1)
                    dve.tensor_scalar(lnm[:, 0, :], psum[:, 4, 0:SEQ], 1.0 / D, None, ALU.mult).then_inc(ln_mean, 1)
                    dve.wait_ge(ln_mean, 1)
                    for pair in pairs:
                        dve.tensor_tensor(cv[:, pair, :], cv[:, pair, :], mean, ALU.subtract).then_inc(xc_ready, 1)
                if c == 4:
                    dve.wait_ge(ln_step, 1)
                    dve.reciprocal(lnm[:, 1, :], lnm[:, 1, :]).then_inc(ln_rstd, 1)
                    dve.wait_ge(ln_rstd, 1)
                    dve.wait_ge(xc_ready, KT // 2)
                    for pair in pairs:
                        dve.tensor_tensor(cv[:, pair, :], cv[:, pair, :], inv, ALU.mult).then_inc(lns_ready, 1)
                if c == 5:
                    for q, pair in enumerate(pairs):
                        dve.wait_ge(lna_ready, 2 * q + 2)
                        dve.tensor_tensor(cv[:, pair, :], cv[:, pair, :], zc[:, pair, :], ALU.mult).then_inc(lnz_ready, 1)
                if c == 6:
                    for q, pair in enumerate(pairs):
                        dve.wait_ge(chi_ready, q + 1)
                        part_lo(cT_lo[:, pair, :], cv[:, pair, :], cT_hi[:, pair, :]).then_inc(cop_ready, 1)
            chunks("gates", layer_norm, unroll=True)

            def conv_gated(i, j, done):
                dve.wait_ge(half_done, done)
                o = gab[:, KT + 2 * j:KT + 2 * j + 2, :]
                dve.tensor_tensor(o, bank(j), o, ALU.mult).then_inc(bank_free, 1)
            chunks("conv_out", conv_gated)

            def merged(i, j, done):
                if j % 2:
                    b = 2 * i + j // 2
                    pair = slice(2 * b, 2 * b + 2)
                    dve.wait_ge(half_done, done)
                    dve.tensor_tensor(rp2[:, :, :], bank(j // 2), gab[:, pair, :], ALU.mult).then_inc(bank_free, 2)
                    dve.wait_ge(bank_free, 4 + FIRST["ret_out"] + 2 * (b + 1))
                    dve.tensor_tensor(rp2[:, :, :], rp2[:, :, :], gab[:, KT + 2 * b:KT + 2 * b + 2, :], ALU.add).then_inc(mg_ready, 1)
                    dve.wait_ge(mg_ready, b + 1)
                    dve.wait_ge(mhi_ready, b + 1)
                    part_lo(hT_lo[:, pair, :], rp2[:, :, :], hT_hi[:, pair, :]).then_inc(mop_ready, 1)
            chunks("ret_out", merged, unroll=True)
            dve.wait_ge(row_mul, 2)

            def y_out(i, j, done):
                dve.wait_ge(half_done, done)
                y_block(2, j, j, slice(j * CC, (j + 1) * CC))
            chunks("w_out", y_out)
            post_norm(2, "w_out")


_INS = ["x", "pre_norm_w", "post_norm_w", "gdn_w_in", "gdn_conv_w", "gdn_A_log", "gdn_dt_bias", "gdn_norm_w",
        "gdn_w_out", "sc_w_in", "sc_conv_w", "sc_w_out", "c_2", "positions_2", "w_ada_2", "b_ada_2", "pre_norm_g_2",
        "w_in_2", "conv_w_2", "conv_b_2", "conv_ln_g_2", "conv_ln_b_2", "w_ret_out_2", "w_conv_out_2", "w_out_2",
        "post_norm_g_2"]


def shape_constants():
    import numpy as _np

    i = _np.arange(P)
    masks = _np.zeros((P, NCONST, P), _np.float32)
    masks[:, C_ID] = _np.eye(P)
    masks[:, C_ONE] = 1.0
    masks[:, C_LOW] = i[:, None] > i[None, :]
    masks[:, C_FLOOR] = _np.where(i[:, None] >= i[None, :], E_LEAST, 1e30)
    for level in range(NLEV):
        b = 2 ** level
        same = (i[:, None] // (2 * b)) == (i[None, :] // (2 * b))
        low = same & (i[:, None] // b % 2 == 1) & (i[None, :] // b % 2 == 0)
        signed = _np.eye(P) - low
        if level == 0:
            masks[:, C_M0], masks[:, C_M0T] = signed, signed.T
        else:
            masks[:, C_MASK + level - 1] = signed
    log_g = _np.log1p(-_np.exp2(-5.0 - _np.arange(RH)))
    diff = _np.arange(SEQ)[None, :] - i[:, None]
    decays = _np.zeros((P, RH, 3 * P), _np.float32)
    for h in range(RH):
        d = _np.where(diff >= 0, _np.exp(log_g[h] * _np.maximum(diff, 0)), 0.0) * RDK ** -0.5
        decays[:, h, :SEQ] = d
        decays[:, h, SEQ:] = d[:, :P]
    freqs = (_np.float32(ROPE_BASE) ** (-_np.arange(P, dtype=_np.float32) / _np.float32(P))).astype(_np.float32)
    return masks, decays, freqs.reshape(P, 1)


def kernel(**inputs):
    import numpy as _np
    import concourse.bacc as _bacc
    from concourse import mybir as _mybir
    from concourse.bass_utils import run_bass_kernel_spmd as _run

    nc = _bacc.Bacc("TRN2", target_bir_lowering=False, num_devices=1)
    arrays, args = {}, []
    given = [(name, _np.ascontiguousarray(inputs[name])) for name in _INS]
    given += list(zip(("masks", "decays", "freqs"), shape_constants()))
    for name, a in given:
        arrays[f"in_{name}_dram"] = a
        args.append(nc.dram_tensor(f"in_{name}_dram", a.shape, _mybir.dt.from_np(a.dtype), kind="ExternalInput").ap())
    out = nc.dram_tensor("out_0_dram", (1, SEQ, D), F32, kind="ExternalOutput").ap()
    build(nc, *args, out)
    r = _run(nc, [arrays], core_ids=[0])
    return r.results[0]["out_0_dram"]
```

```python
import math
from contextlib import ExitStack

import numpy as np

import concourse.bass as bass
from concourse import mybir

F32 = mybir.dt.float32
F32R = mybir.dt.float32r
I32 = mybir.dt.int32
ACT = mybir.ActivationFunctionType
ALU = mybir.AluOpType
AX_X = mybir.AxisListType.X

P = 128
SEQ = 256
NT = SEQ // P
D = 1024
KT = D // P
KH2 = KT // 2
ROPE_BASE = 10000.0
RMS_EPS = 1e-6
NORM_EPS = 1e-5

VH, KH = 16, 8
HD = 128
GQK, GV = KH * HD, VH * HD
GCONV = 4
GQKV = 2 * GQK + GV
SCW = 2 * D
SCONV = 3
RH, RDK, RDV = 4, 256, 512
CW = 31
CPAD = CW - 1
CONV_DVE = 5
HG = 4
NPAIR = VH // HG
LIVE = 3
NLEV = 7

CC = 256
RING = 4
PHASES = [("qkv", 16), ("z", 8), ("gdn_out", 8), ("sc_in", 32), ("sc_out", 8), ("glu", 8), ("qk", 8), ("v", 8),
          ("zret", 8), ("zconv", 4), ("gates", 8), ("conv_out", 4), ("ret_out", 8), ("w_out", 4)]
ORDER = [name for name, _ in PHASES]
READ_BY = {name: "act" if name in ("z", "gdn_out", "sc_out", "v", "zret", "zconv", "gates", "w_out") else "dve" for name in ORDER}
DEEP = ("gdn_out", "sc_out", "ret_out")
OUT_PIECES = 2
HANDED = [name for before, name in zip(ORDER, ORDER[1:]) if READ_BY[name] != READ_BY[before]]
FIRST = {}
COUNT = dict(PHASES)
_g = 0
for _n, _c in PHASES:
    FIRST[_n] = _g
    _g += _c
CHUNKS = _g
ADA_PIECES = 3 * D // P
ADA_SLOTS = ADA_PIECES // (COUNT["sc_in"] // 4)
assert ADA_SLOTS * COUNT["sc_in"] == 4 * ADA_PIECES and ADA_SLOTS <= 4

C_ID, C_ONE, C_LOW, C_FLOOR, C_M0, C_M0T, C_MASK = 0, 1, 2, 3, 4, 5, 6
NCONST = C_MASK + NLEV - 1

V_PRE, V_PRE2, V_BADA, V_CB, V_LG, V_LB, V_C, V_SC = 0, 16, 24, 48, 56, 64, 72, 80
E_LEAST = 0.5 * math.log(RMS_EPS) - 0.1
G_ROW = 32


def build(nc, x_in, pre_norm_w, post_norm_w, gdn_w_in, gdn_conv_w, gdn_A_log, gdn_dt_bias, gdn_norm_w, gdn_w_out,
          sc_w_in, sc_conv_w, sc_w_out, c_2, positions_2, w_ada_2, b_ada_2, pre_norm_g_2, w_in_2, conv_w_2, conv_b_2,
          conv_ln_g_2, conv_ln_b_2, w_ret_out_2, w_conv_out_2, w_out_2, post_norm_g_2, masks, decays, freqs, out):
    ctx = ExitStack()
    with ctx:
        def sem(name):
            return ctx.enter_context(nc.semaphore(name))

        base = (nc.sbuf_base + 63) // 64 * 64
        fence = ctx.enter_context(nc.sbuf_tensor("fence", [P, (nc.sbuf_usable_end - base) // 64 * 16 - 16], F32))
        top = [base]

        def at(name, offset, shape, dt=F32):
            return nc.alloc_sbuf_tensor_at(name, shape, dt, offset=offset)

        def room(nbytes):
            offset = top[0]
            top[0] += (nbytes + 31) // 32 * 32
            assert top[0] <= nc.sbuf_usable_end, (top[0], nc.sbuf_usable_end)
            return offset

        def new(name, shape, dt=F32):
            n = 4
            for s in shape[1:]:
                n *= s
            return at(name, room(n), shape, dt)

        K = 1024
        o_raw = top[0]
        raw = [new(f"w_raw{s}", [P, KT, CC]) for s in range(RING)]
        w_hi = [new(f"w_hi{s}", [P, KH2, CC], F32R) for s in range(4)]
        w_lo = [new(f"w_lo{s}", [P, KH2, CC], F32R) for s in range(4)]
        x = new("x", [P, NT, D])
        o_hT, o_yT, o_ada, o_ar = room(16 * K), room(32 * K), room(8 * K), room(64 * K)
        hT_hi, hT_lo = at("hT_hi", o_hT, [P, KT, SEQ], F32R), at("hT_lo", o_hT + 8 * K, [P, KT, SEQ], F32R)
        yT_hi, yT_lo = at("yT_hi", o_yT, [P, 2 * KT, SEQ], F32R), at("yT_lo", o_yT + 16 * K, [P, 2 * KT, SEQ], F32R)
        ada = [at(f"ada{s}", o_ar + (44 + 4 * s) * K, [P, KT, P]) for s in range(ADA_SLOTS)]
        ada_sum = at("ada_sum", o_ar + 32 * K, [P, ADA_PIECES, P])
        const = new("const", [P, NCONST, P])
        ident, ones = const[:, C_ID, :], const[:, C_ONE, :]
        o_row = room(4 * K)
        row = at("row", o_row, [P, D])
        nw_row = new("nw_row", [P, HD])
        par = new("par", [P, 4, P])
        bg = new("bg", [P, SEQ])
        bgt = new("bgt", [P, NT, P])
        eg = new("eg", [P, NT, VH])
        nbeg = new("nbeg", [P, NT, VH])
        wdec = new("wdec", [P, VH])
        lnss = at("lnss", o_ar + 63 * K, [P, NT, 2 * KH])
        gk, brk = (at(n, o_ar + 63 * K + 128 * (s + 1), [P, NT, VH]) for s, n in enumerate(("gk", "brk")))
        rqs = at("rqs", o_ar + 63 * K + 384, [P, NT, KH])
        acols = new("acols", [P, 4])
        mod = new("mod", [P, 3 * KT])
        gain1, gain2 = new("gain1", [P, 2 * KT]), new("gain2", [P, KT])
        eps_r, eps_n = new("eps_r", [P, 1]), new("eps_n", [P, 1])
        warm = new("warm", [P, 3])
        ss, ms, rstd, yss = new("ss", [P, 4]), new("ms", [P, 4]), new("rstd", [P, 4]), new("yss", [P, NT, D // CC])
        o_ss, o_rs = new("o_ss", [P, NT, VH]), new("o_rs", [P, NT, VH])
        freq = new("freq", [P, 1])
        gst, gmv, grs, gnm = new("gst", [P, NT, 6]), new("gmv", [P, NT, 2]), new("grs", [P, NT]), new("gnm", [P, NT])

        xn = at("xn", o_ar, [P, NT, D])
        hx = at("hx", o_ar + 8 * K, [P, KT, SEQ])
        junk = at("junk", o_ar + 8 * K, [P, NT, D])
        vecs = at("vecs", o_ada + 4 * K, [P, 4, P])
        qkvT = at("qkvT", o_ar, [P, 4 * KT, SEQ])
        S = at("S", o_ar + 16 * K, [P, LIVE, NT, HG, P])
        zo = at("zo", o_ar + 32 * K, [P, NT, GV])
        PT = at("PT", o_ar + 48 * K, [P, LIVE, NT, HG, P])
        cacc = [at(f"cacc{s}", o_ar + (48 + 2 * s) * K, [P, 2, SEQ]) for s in range(2)]
        ba_raw = at("ba_raw", o_ar + 52 * K, [P, KT, P])
        ba_hi = at("ba_hi", o_ar + 56 * K, [P, KT, P], F32R)
        ba_lo = at("ba_lo", o_ar + 60 * K, [P, KT, P], F32R)
        vb = at("vb", o_yT, [P, NT, VH, HD])
        ktok = at("ktok", o_yT + 16 * K, [P, KH, HD])
        LT = [[at(f"LT{q}{t}", o_yT + (20 + 2 * (2 * q + t)) * K, [P, HG, P]) for t in range(NT)] for q in range(2)]
        o_Z = [o_yT + 28 * K, o_ar + 28 * K] + [o_raw + (16 + 4 * l) * K for l in range(NLEV - 3)]
        Z = [None] + [[at(f"Z{l + 1}{t}", o_Z[l] + 2 * t * K, [P, HG, P]) for t in range(NT)] for l in range(NLEV - 1)]
        sq = [at(f"sq{s}", o_yT + (20 + 2 * s) * K, [P, 2, SEQ]) for s in range(2)]
        gz, gl, gs = (at(f"gate{s}", o_ar + (60 + s) * K, [P, SEQ]) for s in range(3))
        E, Di, A = (at(n, o_ada + 2 * s * K, [P, HG, P]) for s, n in enumerate(("E", "Di", "A")))
        o_T = [[o_ada + 6 * K, o_ar + 60 * K], [o_hT + 8 * K, o_hT + 10 * K]]
        T = [[at(f"T{q}{t}", o_T[q][t], [P, HG, P]) for t in range(NT)] for q in range(2)]
        qS = at("qS", o_hT + 12 * K, [P, HG, P])
        kdec, R, U, s1 = (at(n, o_hT + 2 * s * K, [P, HG, P]) for s, n in enumerate(("kdec", "R", "U", "s1")))
        osq = at("osq", o_row, [P, HG, P])
        sc_u = at("sc_u", o_ar + 16 * K, [P, 2, SEQ])
        sc_cu = at("sc_cu", o_ar + 18 * K, [P, 2, SEQ])
        sc_v = at("sc_v", o_ar + 20 * K, [P, 2, SEQ])
        sc_y = at("sc_y", o_ar + 22 * K, [P, 2, SEQ])
        sc_z = at("sc_z", o_ar + 24 * K, [P, 2, SEQ])
        sc_yz = at("sc_yz", o_ar + 26 * K, [P, 2, SEQ])
        aP = at("aP", o_ar, [P, KT, CPAD + SEQ])
        cv = at("cv", o_ar + 9728, [P, KT, SEQ])
        o_q = o_ar + 9728 + 8 * K
        qkT = at("qkT", o_q, [P, 2 * KT, SEQ])
        vt = at("vt", o_q + 16 * K, [P, NT, 2 * D])
        o_t = o_q + 32 * K
        st = at("st", o_t, [P, RH, 3 * P])
        glu, rp1, rp2 = (at(n, o_t + 2 * s * K, [P, 2, SEQ]) for s, n in enumerate(("glu", "rp1", "rp2")))
        cvo = at("cvo", o_t + 6 * K, [P, SEQ])
        lnm = at("lnm", o_t + 7 * K, [P, 2, SEQ])
        tapped = at("tapped", o_t + 7 * K, [P, 2, SEQ])
        cT_hi, cT_lo = at("cT_hi", o_ar, [P, KT, SEQ], F32R), at("cT_lo", o_q + 24 * K, [P, KT, SEQ], F32R)
        og = [at(f"og{t}", o_t + (9 + 2 * t) * K, [P, RDV]) for t in range(NT)]
        zr = at("zr", o_yT, [P, NT, 2 * D])
        zc = at("zc", o_q, [P, KT, SEQ])
        gab = at("gab", o_q + 8 * K, [P, 2 * KT, SEQ])
        a2 = at("a2", o_q + 24 * K, [P, KT, SEQ])
        decay = at("decay", o_ada, [P, RH, 3 * P])
        trig = at("trig", o_ada + 6 * K, [P, 2, SEQ])
        pos_i = at("pos_i", o_ar + 28 * K, [P, SEQ], I32)
        ang, turn = at("ang", o_ar + 29 * K, [P, SEQ]), at("turn", o_ar + 30 * K, [P, 2, SEQ])
        gdiag = at("gdiag", o_t, [P, KT, P])
        ln_sum = [at(f"ln_sum{s}", o_t + (9 + 2 * s) * K, [P, 2, SEQ]) for s in range(2)]

        psum = ctx.enter_context(nc.psum_tensor("psum", [P, 8, 512], F32))

        def bank(b, inner=SEQ):
            return psum[:, b, :].rearrange("p (a n) -> p a n", n=inner)

        raw_ready = [sem(f"raw_ready{s}") for s in range(RING)]
        hi_ready, lo_ready = sem("hi_ready"), sem("lo_ready")
        half_done = sem("half_done")
        bank_free = sem("bank_free")
        ada_ready = [sem(f"ada_ready{s}") for s in range(ADA_SLOTS)]
        ada_step = sem("ada_step")
        ada_used = sem("ada_used")
        x_loaded = [sem(f"x_loaded{t}") for t in range(NT)]
        vecs_loaded, small_loaded, ba_loaded, rope_loaded = (
            sem(n) for n in ("vecs_loaded", "small_loaded", "ba_loaded", "rope_loaded"))
        row_loaded, decay_loaded, cleared, padded = (
            sem(n) for n in ("row_loaded", "decay_loaded", "cleared", "padded"))
        small_turned, small_ready = sem("small_turned"), sem("small_ready")
        pre_ss, pre_rstd, xn_ready = sem("pre_ss"), sem("pre_rstd"), sem("xn_ready")
        turned, hx_ready, hhi_ready, h_ready = (
            sem(n) for n in ("turned", "hx_ready", "hhi_ready", "h_ready"))
        y_ready, post_rstd = sem("y_ready"), sem("post_rstd")
        x_ready = sem("x_ready")
        out_done = sem("out_done")
        post_ss, post_std, pre_std, ln_rstd, o_std, gn_std = (
            sem(n) for n in ("post_ss", "post_std", "pre_std", "ln_rstd", "o_std", "gn_std"))
        taps_loaded = sem("taps_loaded")
        ident_loaded, gain_loaded, vb_act_ready, a_ready = (
            sem(n) for n in ("ident_loaded", "gain_loaded", "vb_act_ready", "a_ready"))
        tapped_ready, cv_pool_step = sem("tapped_ready"), sem("cv_pool_step")
        lnss_ready, gk_ready, glast_ready, rows_step = (
            sem(n) for n in ("lnss_ready", "gk_ready", "glast_ready", "rows_step"))
        tap0, tap_step, qkv_ready = sem("tap0"), sem("tap_step"), sem("qkv_ready")
        ba_hi_ready, ba_lo_ready, ba_done = sem("ba_hi_ready"), sem("ba_lo_ready"), sem("ba_done")
        beta_ready, gate_v, gate_a, g_ready = (
            sem(n) for n in ("beta_ready", "gate_v", "gate_a", "g_ready"))
        bg_turned, bgt_ready, eg_ready = sem("bg_turned"), sem("bgt_ready"), sem("eg_ready")
        sq_ready, l2_sum, odd_ready = sem("sq_ready"), sem("l2_sum"), sem("odd_ready")
        v_turned, vb_ready, k_turned, ktok_ready = (
            sem(n) for n in ("v_turned", "vb_ready", "k_turned", "ktok_ready"))
        zn_ready = sem("zn_ready")
        grow_ready, kq_ready, d_ready, e_ready, masked = (
            sem(n) for n in ("grow_ready", "kq_ready", "d_ready", "e_ready", "masked"))
        wd_ready, wd_sub = sem("wd_ready"), sem("wd_sub")
        ap_ready, ap_turned, lt_ready, pt_ready = (
            sem(n) for n in ("ap_ready", "ap_turned", "lt_ready", "pt_ready"))
        chain_ready = sem("chain_ready")
        w_done = [sem(f"w_done{t}") for t in range(NT)]
        z_ready = [sem(f"z_ready{t}") for t in range(NT)]
        ts_done = [sem(f"ts_done{t}") for t in range(NT)]
        t_ready = [sem(f"t_ready{t}") for t in range(NT)]
        s_ready = [sem(f"s_ready{t}") for t in range(NT)]
        kdec_ready, u_done, u_ready, o0_done, s1_done, s1_ready = (
            sem(n) for n in ("kdec_ready", "u_done", "u_ready", "o0_done", "s1_done", "s1_ready"))
        ks_done, r_ready, qs_ready, vn_done, vn_ready, o1_done, o_ready = (
            sem(n) for n in ("ks_done", "r_ready", "qs_ready", "vn_done", "vn_ready", "o1_done", "o_ready"))
        osq_ready, o_rstd, og_ready = sem("osq_ready"), sem("o_rstd"), sem("og_ready")
        yT_turned, yhi_ready, y_op_ready = sem("yT_turned"), sem("yhi_ready"), sem("y_op_ready")
        sc_u_ready, sc_v0, sc_step, sc_z_ready = (
            sem(n) for n in ("sc_u_ready", "sc_v0", "sc_step", "sc_z_ready"))
        mod_done, mod_ready, gain2_ready = sem("mod_done"), sem("mod_ready"), sem("gain2_ready")
        glu_ready, ang_step, ang_ready, trig_ready = (
            sem(n) for n in ("glu_ready", "ang_step", "ang_ready", "trig_ready"))
        rp_step = sem("rp_step")
        sco_done, st_ready, ro_done, gn_step, gn_ready = (
            sem(n) for n in ("sco_done", "st_ready", "ro_done", "gn_step", "gn_ready"))
        rg_ready = sem("rg_ready")
        ln_sum_step = sem("ln_sum_step")
        cv_step, cv_ready, mean_done, xc_ready, a2_ready, var_done, ln_step = (
            sem(n) for n in ("cv_step", "cv_ready", "mean_done", "xc_ready", "a2_ready", "var_done", "ln_step"))
        lna_ready, lns_ready, lnz_ready = sem("lna_ready"), sem("lns_ready"), sem("lnz_ready")
        chi_ready, cop_ready, mg_ready, mhi_ready, mop_ready = (
            sem(n) for n in ("chi_ready", "cop_ready", "mg_ready", "mhi_ready", "mop_ready"))
        qs_done, o1_ready, gn_rec, ln_mean = (
            sem(n) for n in ("qs_done", "o1_ready", "gn_rec", "ln_mean"))
        gate_diag, gate_row, row_mul = sem("gate_diag"), sem("gate_row"), sem("row_mul")
        block = ctx.enter_context(nc.Block())

        def loop(eng, n, step):
            if n == 1:
                step(0)
            else:
                with eng.Fori(0, n) as i:
                    step(i)

        def half(ap, l, odd):
            return ap.rearrange("p (n two b) -> p n two b", two=2, b=2 ** l)[:, :, odd, :]

        def half_heads(ap, l, odd):
            return ap.rearrange("p h (n two b) -> p h n two b", two=2, b=2 ** l)[:, :, :, odd, :]

        def half_of_each(ap, l, odd):
            o = half(ap, l, odd)
            return o.rearrange("p (h n) b -> p h n b", h=1).to_broadcast([P, HG, P // 2 // 2 ** l, 2 ** l])

        def two_each(ap):
            return ap.rearrange("p t (n r) -> p t n r", r=1).to_broadcast([P, NT, KH, 2])

        def heads(ap, n):
            return ap.rearrange("p (a n) -> p a n", a=1).to_broadcast([P, n, ap.shape[-1]])

        @block.sync
        def _(sp):
            def cols(w, r0, c, n=CC):
                return w[r0:r0 + D, bass.ds(c, n)].rearrange("(k p) n -> p k n", p=P)

            def chunk(g, slot, src, wait=True):
                if wait:
                    sp.wait_ge(lo_ready, g * 2 - 2 * (RING - 1))
                sp.dma_start(raw[slot][:, :, :], src).then_inc(raw_ready[slot], 16)

            def phase(name, where, with_ada=False, start=0):
                g0 = FIRST[name]

                def step(i):
                    for j in range(4):
                        w, r0, c = where(i, j)
                        g = i * 4 + (g0 + j)
                        chunk(g, j, cols(w, r0, c))
                        if with_ada and j < ADA_SLOTS:
                            if not isinstance(i, int):
                                sp.wait_ge(ada_used, i * ADA_SLOTS + (j + 1 - ADA_SLOTS))
                            sp.dma_start(ada[j][:, :, :], cols(w_ada_2[0], 0, i * (ADA_SLOTS * P) + j * P, P)).then_inc(ada_ready[j], 16)
                if with_ada:
                    step(0)
                    start = 1
                if COUNT[name] // 4 - start > 1:
                    with sp.Fori(start, COUNT[name] // 4) as i:
                        step(i)
                else:
                    step(start)

            def load_x(t):
                sp.dma_start(x[:, t, :], x_in[0, t * P:(t + 1) * P, :]).then_inc(x_loaded[t], 16)
            load_x(0)
            sp.dma_start(const[:, 0:2, :], masks[:, 0:2, :]).then_inc(ident_loaded, 16)
            sp.dma_start(vecs[V_PRE:V_PRE + 2 * KT, 1, :], pre_norm_w.rearrange("l (k p) -> (l k) p", p=P)).then_inc(gain_loaded, 16)
            for t in range(1, NT):
                load_x(t)
            sp.dma_start(vecs[:, 0, :], gdn_conv_w[0].rearrange("j (n p) -> (j n) p", p=P)).then_inc(taps_loaded, 16)
            chunk(0, 0, cols(gdn_w_in[0], 0, 0), wait=False)
            for at_row, v in ((V_PRE2, pre_norm_g_2), (V_BADA, b_ada_2), (V_CB, conv_b_2),
                              (V_LG, conv_ln_g_2), (V_LB, conv_ln_b_2), (V_C, c_2)):
                n = v.shape[0] * v.shape[1] // P
                sp.dma_start(vecs[at_row:at_row + n, 1, :], v.rearrange("l (k p) -> (l k) p", p=P)).then_inc(vecs_loaded, 16)
            sp.dma_start(vecs[V_SC:P, 1, :], sc_conv_w[0].rearrange("j (n p) -> (j n) p", p=P)).then_inc(vecs_loaded, 16)
            sp.dma_start(vecs[:, 2, :], conv_w_2[0, 0:16].rearrange("j (n p) -> (j n) p", p=P)).then_inc(vecs_loaded, 16)
            sp.dma_start(vecs[0:120, 3, :], conv_w_2[0, 16:CW].rearrange("j (n p) -> (j n) p", p=P)).then_inc(vecs_loaded, 16)
            sp.dma_start(acols[G_ROW:G_ROW + VH, 0:1], gdn_A_log.rearrange("l h -> h l")).then_inc(small_loaded, 16)
            sp.dma_start(acols[G_ROW:G_ROW + VH, 1:2], gdn_dt_bias.rearrange("l h -> h l")).then_inc(small_loaded, 16)
            sp.dma_start(freq[:, :], freqs).then_inc(small_loaded, 16)
            sp.dma_start(const[:, 2:NCONST, :], masks[:, 2:NCONST, :]).then_inc(small_loaded, 16)
            sp.dma_start(nw_row[:, :], gdn_norm_w.to_broadcast([P, HD])).then_inc(small_loaded, 16)
            for j in range(4):
                if j:
                    chunk(j, j, cols(gdn_w_in[0], 0, j * CC), wait=False)
            sp.wait_ge(padded, 1)
            ba0 = GQKV + GV
            sp.dma_start(ba_raw[:, :, 0:VH], cols(gdn_w_in[0], 0, ba0, VH)).then_inc(ba_loaded, 16)
            sp.dma_start(ba_raw[:, :, G_ROW:G_ROW + VH], cols(gdn_w_in[0], 0, ba0 + VH, VH)).then_inc(ba_loaded, 16)
            phase("qkv", lambda i, j: (gdn_w_in[0], 0, i * 1024 + j * CC), start=1)
            phase("z", lambda i, j: (gdn_w_in[0], 0, i * 1024 + (GQKV + j * CC)))

            def two_halves(w):
                return lambda i, j: (w, j % 2 * D, i * 512 + j // 2 * CC)

            for j in range(4):
                if j == 2:
                    sp.wait_ge(o_ready, 2 * NPAIR)
                chunk(FIRST["gdn_out"] + j, j, cols(gdn_w_out[0], j % 2 * D, j // 2 * CC))
            sp.dma_start(row[:, :], post_norm_w[0:1, :].to_broadcast([P, D])).then_inc(row_loaded, 16)
            phase("gdn_out", two_halves(gdn_w_out[0]), start=1)
            sp.wait_ge(y_op_ready, KT)
            phase("sc_in", lambda i, j: (sc_w_in[0], 0, i * CC + (0, 2 * SCW, SCW, 3 * SCW)[j]), with_ada=True)
            sp.wait_ge(x_ready, NT)
            sp.dma_start(row[:, :], post_norm_w[1:2, :].to_broadcast([P, D])).then_inc(row_loaded, 16)
            sp.dma_start(decay[:, :, :], decays).then_inc(decay_loaded, 16)
            sp.dma_start(pos_i[:, :], positions_2.to_broadcast([P, SEQ])).then_inc(rope_loaded, 16)
            phase("sc_out", two_halves(sc_w_out[0]))
            win = w_in_2[0]
            o_k, o_v, o_zr, o_uv, o_ug, o_zc, o_g = 0, 2 * D, 4 * D, 6 * D, 7 * D, 8 * D, 9 * D
            phase("glu", lambda i, j: (win, 0, i * 512 + ((o_uv if j % 2 else o_ug) + j // 2 * CC)))
            sp.wait_ge(x_ready, 2 * NT)
            sp.dma_start(row[:, :], post_norm_g_2[0:1, :].to_broadcast([P, D])).then_inc(row_loaded, 16)
            phase("qk", lambda i, j: (win, 0, i * 1024 + (o_k + j * CC)))
            phase("v", lambda i, j: (win, 0, i * 1024 + (o_v + j * CC)))
            phase("zret", lambda i, j: (win, 0, i * 1024 + (o_zr + j * CC)))
            phase("zconv", lambda i, j: (win, 0, o_zc + j * CC))
            phase("gates", lambda i, j: (win, 0, i * 1024 + (o_g + j * CC)))
            phase("conv_out", lambda i, j: (w_conv_out_2[0], 0, j * CC))
            phase("ret_out", two_halves(w_ret_out_2[0]))
            phase("w_out", lambda i, j: (w_out_2[0], 0, j * CC))
            for t in range(NT):
                for q in range(OUT_PIECES):
                    c = slice(q * D // OUT_PIECES, (q + 1) * D // OUT_PIECES)
                    sp.wait_ge(x_ready, 2 * NT + t * OUT_PIECES + q + 1)
                    sp.dma_start(out[0, t * P:(t + 1) * P, c], x[:, t, c]).then_inc(out_done, 16)
            sp.wait_ge(out_done, 16 * NT * OUT_PIECES)

        VECS, SMALL = 16 * 9, 16 * 5

        @block.tensor
        def _(pe):
            def product(o, l_hi, l_lo, r_hi, r_lo, start, stop):
                pe.matmul(o, l_hi, r_hi, start=start, stop=False, skip_group_check=True)
                pe.matmul(o, l_hi, r_lo, start=False, stop=False, skip_group_check=True)
                return pe.matmul(o, l_lo, r_hi, start=False, stop=stop, skip_group_check=True)

            def chunk(i, g0, j, b, a_hi, a_lo, k0, channels, part, operand=None):
                o = bank(b)
                if part is None:
                    pe.wait_ge(bank_free, i * 4 + (g0 + j + 1))
                elif part == 0:
                    pe.wait_ge(bank_free, i * 4 + (g0 + j + 2))
                for h in range(2):
                    s = j % 2 * 2 + h
                    if operand is not None:
                        ready, before = operand
                        pe.wait_ge(ready, before + KT // 4 * (h + 1))
                    pe.wait_ge(lo_ready, i * 8 + (2 * (g0 + j) + h + 1))
                    for m in range(2):
                        mine = slice(m * P, (m + 1) * P)
                        for k in range(KH2):
                            ka = k0 + h * KH2 + k
                            first = m == 0 and h == 0 and k == 0 and part != 1
                            last = h == 1 and k == KH2 - 1 and part != 0
                            if channels:
                                mm = product(o[:, m, :], w_hi[s][:, k, mine], w_lo[s][:, k, mine], a_hi[:, ka, :], a_lo[:, ka, :], first, last)
                            else:
                                mm = product(o[:, m, :], a_hi[:, ka, mine], a_lo[:, ka, mine], w_hi[s][:, k, :], w_lo[s][:, k, :], first, last)
                    mm.then_inc(half_done, 1)

            def phase(name, a_hi, a_lo, channels, deep=False, operand=None, beside=None, loop_beside=None, begun=False):
                g0 = FIRST[name]
                if name in HANDED and ORDER[ORDER.index(name) - 1] in DEEP:
                    pe.wait_ge(bank_free, 4 + g0)

                if deep:
                    pe.wait_ge(*operand)

                def step(i, i_beside=None, start=0):
                    for j in range(start, 4):
                        if deep:
                            chunk(i, g0, j, j // 2, a_hi, a_lo, j % 2 * KT, channels, j % 2, operand if j == 1 else None)
                        else:
                            chunk(i, g0, j, j, a_hi, a_lo, 0, channels, None, operand if j == 0 else None)
                        if beside is not None:
                            beside(4 * i + j)
                        if i_beside is not None:
                            loop_beside(i_beside, j)
                if beside is not None:
                    for i in range(COUNT[name] // 4):
                        step(i)
                elif begun:
                    step(0, start=1)
                    loop(pe, COUNT[name] // 4 - 1, lambda i: step(i + 1))
                elif loop_beside is not None:
                    n = COUNT[name] // 4
                    with pe.Fori(0, n - KT // 4) as i:
                        step(i)
                    with pe.Fori(0, KT // 4) as i:
                        step(i + (n - KT // 4), i)
                else:
                    loop(pe, COUNT[name] // 4, step)

            def pre_norm(n):
                for t in range(NT):
                    pe.wait_ge(xn_ready, NT * n + t + 1)
                    for k in range(KT):
                        mm = pe.transpose(bank(4 + k // 2, P)[:, k % 2 * NT + t, :], xn[:, t, k * P:(k + 1) * P], ident)
                        if t == NT - 1 and k % 2:
                            mm.then_inc(turned, 1)

            pe.wait_ge(ident_loaded, 16)
            pe.wait_ge(gain_loaded, 16)
            pe.transpose(psum[:, 7, 0:2 * KT], vecs[0:2 * KT, 1, :], ident[0:2 * KT, 0:2 * KT]).then_inc(small_turned, 1)
            pe.wait_ge(taps_loaded, 16)
            pe.transpose(psum[:, 3, 0:P], vecs[:, 0, :], ident).then_inc(small_turned, 1)
            pre_norm(0)

            def squares(i, j):
                pe.wait_ge(sq_ready, i * 4 + (j + 1))
                for m in range(2):
                    for t in range(NT):
                        mm = pe.matmul(psum[:, 7, bass.ds(i * 8 + (t * VH + 2 * j + m), 1)], sq[j % 2][:, m, t * P:(t + 1) * P],
                                       ones[:, 0:1], start=True, stop=True)
                mm.then_inc(l2_sum, 1)
            phase("qkv", hT_hi, hT_lo, True, operand=(h_ready, 0), loop_beside=squares)
            def prep(p, c, stage):
                n, cs = NT * p + c, slice(c * P, (c + 1) * P)
                if stage == 1:
                    if n:
                        pe.wait_ge(lt_ready, n)
                    for a in range(HG):
                        h = HG * p + a
                        mm = pe.matmul(bank(4, P)[:, a, :], gk[:, c, h:h + 1].to_broadcast([P, P]), ident, start=True, stop=True)
                    mm.then_inc(grow_ready, 1)
                    if n:
                        pe.wait_ge(pt_ready, n)
                    for e in range(2):
                        k = qkvT[:, KT + 2 * p + e, cs]
                        pe.matmul(bank(5, P)[:, e, :], k, k, start=True, stop=True)
                        mm = pe.matmul(bank(5, P)[:, 2 + e, :], qkvT[:, 2 * p + e, cs], k, start=True, stop=True)
                    mm.then_inc(kq_ready, 1)
                if stage == 3:
                    pe.wait_ge(ap_ready, n + 1)
                    for a in range(HG):
                        pe.transpose(bank(4, P)[:, a, :], A[:, a, :], ident)
                        mm = pe.transpose(bank(5, P)[:, a, :], Di[:, a, :], ident)
                    mm.then_inc(ap_turned, 1)

            def beside_z(c):
                if c == 2:
                    pe.wait_ge(vecs_loaded, VECS)
                    for n in range(3):
                        r = 120 if n == 2 else P
                        mm = pe.transpose(bank(5, P)[:, n, 0:r], vecs[0:r, n + 1, :], ident[0:r, 0:r])
                    mm.then_inc(small_turned, 1)
                if c == 3:
                    pe.wait_ge(g_ready, NT)
                    for t in range(NT):
                        mm = pe.transpose(bank(6, P)[:, t, :], bg[:, t * P:(t + 1) * P], ident)
                    mm.then_inc(bg_turned, 1)
                    pe.wait_ge(lnss_ready, 1)
                    pe.matmul(psum[:, 7, 2 * VH:3 * VH], bg[:, P - 1:P].to_broadcast([P, P]), ident[:, G_ROW:G_ROW + VH], start=True,
                              stop=True).then_inc(glast_ready, 1)
                    pe.wait_ge(qkv_ready, COUNT["qkv"])
                if c == 6:
                    prep(0, 0, 3)
                if c == 7:
                    prep(0, 1, 3)
                if c >= 4:
                    for n in (2 * (c - 4), 2 * (c - 4) + 1):
                        t, q = n // NPAIR, n % NPAIR
                        if n >= 2:
                            pe.wait_ge(vb_act_ready if n % 2 else vb_ready, n // 2)
                        elif n == 0:
                            pe.wait_ge(bgt_ready, 1)
                        else:
                            pe.wait_ge(wd_sub, 1)
                        for a in range(HG):
                            mm = pe.transpose(bank(6 + n % 2, P)[:, a, :], qkvT[:, 2 * KT + HG * q + a, t * P:(t + 1) * P], ident)
                        mm.then_inc(v_turned, 1)
                if c == 4:
                    pe.wait_ge(gk_ready, 1)
                    pe.wait_ge(small_ready, 3)
                    prep(0, 0, 1)
                if c == 6:
                    prep(0, 1, 1)
                if c == COUNT["z"] - 1:
                    pe.wait_ge(bank_free, 4 + FIRST["z"] + 7)
                    for n in range(2):
                        for a in range(HG):
                            mm = pe.transpose(bank(2 - n, P)[:, a, :], qkvT[:, KT + HG * n + a, 0:P], ident)
                        mm.then_inc(k_turned, 1)
            pe.wait_ge(ba_lo_ready, 1)
            for k in range(KT):
                mm = product(psum[:, 6, 0:SEQ], ba_hi[:, k, :], ba_lo[:, k, :], hT_hi[:, k, :], hT_lo[:, k, :], k == 0, k == KT - 1)
            mm.then_inc(ba_done, 1)
            phase("z", hT_hi, hT_lo, False, beside=beside_z)

            def level_w(p, l):
                for c in range(NT):
                    if l == 1:
                        pe.wait_ge(chain_ready, NT * p + c + 1)
                        if p == 0 and c == 1:
                            pe.wait_ge(ktok_ready, 1)
                    else:
                        pe.wait_ge(t_ready[c], (NLEV - 2) * p + l - 1)
                    for a in range(HG):
                        mm = pe.matmul(bank(2 * c, P)[:, a, :], LT[p % 2][c][:, a, :], T[p % 2][c][:, a, :], start=True, stop=True)
                    mm.then_inc(w_done[c], 1)

            def level_ts(p, l):
                for c in range(NT):
                    done = (NLEV - 1) * p + l
                    pe.wait_ge(z_ready[c], done)
                    if p == 0:
                        pe.wait_ge(odd_ready, l)
                        if l == 1:
                            pe.wait_ge(ktok_ready, 2)
                    if done > 1:
                        pe.wait_ge(s_ready[c], done - 1)
                    for a in range(HG):
                        if l < NLEV - 1:
                            pe.matmul(bank(2 * c, P)[:, a, :], S[:, p % LIVE, c, a, :], Z[l][c][:, a, :], start=True, stop=True)
                        mm = pe.matmul(bank(2 * c + 1, P)[:, a, :], Z[l][c][:, a, :], S[:, p % LIVE, c, a, :], start=True, stop=True)
                    mm.then_inc(ts_done[c], 1)

            def apply(p, stage):
                b6, b7 = bank(6, P), bank(7, P)

                def four(b, left, right, done):
                    for a in range(HG):
                        mm = pe.matmul(b[:, a, :], left(a), right(a), start=True, stop=True)
                    mm.then_inc(done, 1)
                last_s = (NLEV - 1) * (p + 1)
                if stage == 1:
                    pe.wait_ge(s_ready[0], last_s)
                    if p:
                        pe.wait_ge(vn_ready, p)
                    four(b6, lambda a: S[:, p % LIVE, 0, a, :], lambda a: vb[:, 0, HG * p + a, :], u_done)
                if stage == 2:
                    pe.wait_ge(u_ready, p + 1)
                    pe.wait_ge(kdec_ready, p + 1)
                    if p:
                        pe.wait_ge(o_ready, 2 * p)
                    four(b7, lambda a: PT[:, p % LIVE, 0, a, :], lambda a: U[:, a, :], o0_done)
                    four(b6, lambda a: kdec[:, a, :], lambda a: U[:, a, :], s1_done)
                if stage == 3:
                    pe.wait_ge(s1_ready, p + 1)
                    four(b6, lambda a: qkvT[:, KT + (HG * p + a) // 2, P:2 * P], lambda a: s1[:, a, :], ks_done)
                    pe.wait_ge(o_ready, 2 * p + 1)
                    four(b7, lambda a: qkvT[:, (HG * p + a) // 2, P:2 * P], lambda a: s1[:, a, :], qs_done)
                if stage == 4:
                    pe.wait_ge(s_ready[1], last_s)
                    pe.wait_ge(r_ready, p + 1)
                    four(b6, lambda a: S[:, p % LIVE, 1, a, :], lambda a: R[:, a, :], vn_done)
                if stage == 5:
                    pe.wait_ge(vn_ready, p + 1)
                    pe.wait_ge(qs_ready, p + 1)
                    four(b7, lambda a: PT[:, p % LIVE, 1, a, :], lambda a: U[:, a, :], o1_done)

            def turn_y(q):
                pe.wait_ge(og_ready, q + 1)
                for kp in (2 * q, 2 * q + 1):
                    if kp >= 4:
                        pe.wait_ge(y_op_ready, kp - 3)
                    for k in range(2):
                        for t in range(NT):
                            mm = pe.transpose(bank(kp % 4, P)[:, 2 * k + t, :], zo[:, t, (2 * kp + k) * P:(2 * kp + k + 1) * P], ident)
                    mm.then_inc(yT_turned, 1)

            for p in range(NPAIR + 1):
                for l in range(1, NLEV):
                    if p < NPAIR:
                        level_w(p, l)
                    if p >= 1:
                        apply(p - 1, l)
                    if p == NPAIR and 2 <= l <= NPAIR:
                        turn_y(l - 2)
                    if p < NPAIR - 1:
                        prep(p + 1, (l - 1) // 3, (l - 1) % 3 + 1)
                    if p < NPAIR:
                        level_ts(p, l)

            pe.wait_ge(y_op_ready, 5)
            chunk(0, FIRST["gdn_out"], 0, 0, yT_hi, yT_lo, 0, False, 0)
            turn_y(NPAIR - 1)
            phase("gdn_out", yT_hi, yT_lo, False, deep=True, operand=(y_op_ready, KT // 2), begun=True)

            pre_norm(1)
            phase("sc_in", hT_hi, hT_lo, True, operand=(h_ready, KT // 2))
            phase("sc_out", yT_hi, yT_lo, False, deep=True, operand=(y_op_ready, KT + KT // 2))

            pe.wait_ge(ada_used, ADA_PIECES)
            for a in range(ADA_PIECES):
                mm = pe.matmul(psum[:, 3, a:a + 1], ada_sum[:, a, :], ones[:, 0:1], start=True, stop=True)
            mm.then_inc(mod_done, 1)
            pre_norm(2)
            phase("glu", hT_hi, hT_lo, True, operand=(h_ready, KT))
            phase("qk", hT_hi, hT_lo, True)
            def scores(c):
                if c == 0:
                    pe.wait_ge(rp_step, 2 * RH)
                if c < RH:
                    b = psum[:, 4 + c, :]
                    for o, keys, queries in ((b[:, 0:SEQ], slice(0, P), slice(0, SEQ)), (b[:, SEQ:SEQ + P], slice(P, SEQ), slice(P, SEQ))):
                        for d in range(2):
                            mm = pe.matmul(o, qkT[:, KT + 2 * c + d, keys], qkT[:, 2 * c + d, queries], start=(d == 0), stop=(d == 1))
                    mm.then_inc(sco_done, 1)
            phase("v", hT_hi, hT_lo, False, beside=scores)

            def weighted_sums(c):
                h, t = c // NT, c % NT
                pe.wait_ge(st_ready, min(RH, c + 1))
                if c >= 4:
                    pe.wait_ge(gn_ready, c - 3)
                vh = slice(h * RDV, (h + 1) * RDV)
                o = psum[:, 4 + c % 4, :]
                mm = pe.matmul(o, st[:, h, t * P:(t + 1) * P], vt[:, 0, vh], start=True, stop=(t == 0))
                if t:
                    mm = pe.matmul(o, st[:, h, SEQ:SEQ + P], vt[:, 1, vh], start=False, stop=True)
                mm.then_inc(ro_done, 1)
            phase("zret", hT_hi, hT_lo, False, beside=weighted_sums)

            def turn_two(c):
                for kp in (2 * c, 2 * c + 1):
                    if kp == 0:
                        pe.wait_ge(rg_ready, NT * RH)
                    if kp >= 4:
                        pe.wait_ge(y_op_ready, 2 * KT + kp - 3)
                    for k in range(2):
                        for t in range(NT):
                            mm = pe.transpose(bank(4 + kp % 4, P)[:, 2 * k + t, :], vt[:, t, (2 * kp + k) * P:(2 * kp + k + 1) * P], ident)
                    mm.then_inc(yT_turned, 1)
            phase("zconv", hT_hi, hT_lo, True, beside=lambda c: turn_two(c - 1) if c else None)

            def layer_norm(c):
                if c == 0:
                    turn_two(KT // 2 - 1)
                if c == 1:
                    pe.wait_ge(y_op_ready, 2 * KT + 6)
                    pe.wait_ge(gate_diag, 1)
                    for k in range(KT):
                        mm = pe.matmul(bank(4 + k // 4, P)[:, k % 4, :], ones, gdiag[:, k, :], start=True, stop=True)
                    mm.then_inc(gate_row, 1)
                if c == 2:
                    pe.wait_ge(y_op_ready, 3 * KT)
                    pe.wait_ge(ln_sum_step, 2)
                    pe.wait_ge(cv_pool_step, (CW + 1) * (KT - CONV_DVE))
                    pe.wait_ge(cv_ready, CONV_DVE)
                    rest = [ln_sum[0][:, 0, :], ln_sum[0][:, 1, :], cv[:, KT - 1, :], cv[:, CONV_DVE - 1, :]]
                    for n, part in enumerate(rest):
                        mm = pe.matmul(psum[:, 6, 0:SEQ], ones, part, start=(n == 0), stop=(n == len(rest) - 1))
                    mm.then_inc(mean_done, 1)
                if c == 3:
                    pe.wait_ge(a2_ready, KT // 2)
                    pe.wait_ge(ln_sum_step, 4)
                    rest = [a2[:, KT - 2, :], a2[:, KT - 1, :], ln_sum[1][:, 0, :], ln_sum[1][:, 1, :]]
                    for n, part in enumerate(rest):
                        mm = pe.matmul(psum[:, 7, 0:SEQ], ones, part, start=(n == 0), stop=(n == len(rest) - 1))
                    mm.then_inc(var_done, 1)
            phase("gates", hT_hi, hT_lo, True, beside=layer_norm)
            phase("conv_out", cT_hi, cT_lo, True, operand=(cop_ready, 0))
            phase("ret_out", yT_hi, yT_lo, True, deep=True, operand=(y_op_ready, 2 * KT + KT // 2))
            phase("w_out", hT_hi, hT_lo, False, operand=(mop_ready, 0))

        @block.scalar
        def _(act):
            def split_hi(g0, i, j, h):
                if isinstance(i, int) and g0 + 4 * i + j >= CHUNKS:
                    return
                slot = j % RING
                if h == 0:
                    act.wait_ge(raw_ready[slot], i * 16 + 16 * ((g0 + j) // RING + 1))
                act.wait_ge(half_done, i * 8 + (2 * (g0 + j) + h + 1))
                act.activation(w_hi[j % 2 * 2 + h][:, :, :], raw[slot][:, h * KH2:(h + 1) * KH2, :], ACT.Copy).then_inc(hi_ready, 1)

            def split_ahead(g0, i, j):
                split_hi(g0, i, j + 1, 1)
                split_hi(g0, i, j + 2, 0)

            def chunks(name, each=None, unroll=False):
                g0 = FIRST[name]

                def step(i):
                    for j in range(4):
                        split_ahead(g0, i, j)
                        if j == 0 and name in HANDED and READ_BY[name] == "act":
                            act.wait_ge(bank_free, 4 + g0)
                        if each is not None:
                            each(i, j, i * 8 + (2 * (g0 + j) + 6))
                if unroll:
                    for i in range(COUNT[name] // 4):
                        step(i)
                else:
                    loop(act, COUNT[name] // 4, step)

            def pre_norm(n, gain=None):
                for t in range(NT):
                    if n == 0:
                        act.wait_ge(x_loaded[t], 16)
                    else:
                        act.wait_ge(x_ready, NT * (n - 1) + t + 1)
                    act.activation(junk[:, t, :], x[:, t, :], ACT.Square, scale=D ** -0.5, accum_out=ss[:, t:t + 1]).then_inc(pre_ss, 1)
                    act.wait_ge(pre_ss, NT * n + t + 1)
                    act.activation(ms[:, t:t + 1], ss[:, t:t + 1], ACT.Sqrt, bias=eps_r[:, :]).then_inc(pre_std, 1)
                if n == 0:
                    act.wait_ge(small_ready, 1)
                for kp in range(KT // 2):
                    if n < 2:
                        act.wait_ge(turned, KT // 2 * n + kp + 1)
                        for k in range(2):
                            i = act.activation(hT_hi[:, 2 * kp + k, :], bank(4 + kp)[:, k, :], ACT.Copy, scale=gain(2 * kp + k))
                    else:
                        act.wait_ge(hx_ready, kp + 1)
                        i = act.activation(hT_hi[:, 2 * kp:2 * kp + 2, :], hx[:, 2 * kp:2 * kp + 2, :], ACT.Copy)
                    i.then_inc(hhi_ready, 1)
                    if n == 0 and kp == KT // 4 - 1:
                        split_hi(0, 0, 0, 0)
                if n == 0:
                    split_hi(0, 0, 0, 1)
                    split_hi(0, 0, 1, 0)

            def y_squares(n, b, block):
                act.wait_ge(y_ready, block + (4 * n + 1))
                for t in range(NT):
                    i = act.activation(junk[:, t, bass.ds(block * CC, CC)], bank(b)[:, t, :], ACT.Square, scale=D ** -0.5, accum_out=yss[:, t, bass.ds(block, 1)])
                return i

            def post_norm(n):
                act.wait_ge(post_ss, n + 1)
                act.activation(ms[:, 2:2 + NT], ss[:, 2:2 + NT], ACT.Sqrt, bias=eps_r[:, :]).then_inc(post_std, 1)

            def y_halves(n):
                def each(i, j, done):
                    if j % 2:
                        y_squares(n, j // 2, i * 2 + j // 2).then_inc(bank_free, 2)
                return each

            def col(v):
                return lambda k: par[:, 1, v + k:v + k + 1]

            act.wait_ge(cleared, 1)
            act.activation(warm[:, 2:3], eps_r[:, :], ACT.Sqrt)
            pre_norm(0, lambda k: gain1[:, k:k + 1])
            act.wait_ge(small_ready, 2)

            def qkv_step(i):
                g0 = FIRST["qkv"]

                def silu(j):
                    act.wait_ge(bank_free, i * 4 + (4 + g0 + j + 1))
                    act.activation(qkvT[:, bass.ds(i * 8 + 2 * j, 2), :], cacc[j % 2][:, :, :], ACT.Silu).then_inc(qkv_ready, 1)
                for j in range(4):
                    split_ahead(g0, i, j)
                    act.wait_ge(half_done, i * 8 + (2 * (g0 + j) + 6))
                    for m in range(2):
                        w = par[:, 0, bass.ds(i * 8 + ((GCONV - 1) * 32 + 2 * j + m), 1)]
                        a = act.activation(cacc[j % 2][:, m, :], bank(j)[:, m, :], ACT.Copy, scale=w)
                    a.then_inc(tap0, 1)
                    if j:
                        silu(j - 1)
                        act.wait_ge(qkv_ready, i * 4 + j)
                silu(3)
                act.wait_ge(qkv_ready, i * 4 + 4)
            loop(act, COUNT["qkv"] // 4 - 1, qkv_step)
            act.wait_ge(ba_loaded, 32)
            act.activation(ba_hi[:, :, :], ba_raw[:, :, :], ACT.Copy).then_inc(ba_hi_ready, 1)
            qkv_step(COUNT["qkv"] // 4 - 1)

            def z_out(i, j, done):
                act.wait_ge(half_done, done)
                act.activation(zo[:, :, bass.ds(i * 1024 + j * CC, CC)], bank(j), ACT.Silu).then_inc(bank_free, 1)
            def prep(p, c, stage):
                n = NT * p + c
                if stage == 1:
                    act.wait_ge(d_ready, n + 1)
                    act.activation(E[:, :, :], E[:, :, :], ACT.Exp, scale=-1.0).then_inc(e_ready, 1)
                if stage == 3:
                    act.wait_ge(ap_turned, n + 1)
                    if p >= LIVE:
                        act.wait_ge(o1_done, p - LIVE + 1)
                    act.activation(LT[p % 2][c][:, :, :], bank(4, P), ACT.Copy).then_inc(lt_ready, 1)
                    act.activation(PT[:, p % LIVE, c, :, :], bank(5, P), ACT.Copy).then_inc(pt_ready, 1)

            gr = slice(G_ROW, G_ROW + VH)

            def beside_z(i, j, done):
                z_out(i, j, done)
                c = 4 * i + j
                if c == 0:
                    act.wait_ge(small_loaded, SMALL)
                    act.wait_ge(ba_done, 1)
                    act.wait_ge(cleared, 1)
                    act.activation(bg[0:VH, :], psum[0:VH, 6, 0:SEQ], ACT.Sigmoid).then_inc(beta_ready, 1)
                    act.activation(acols[gr, 2:3], acols[gr, 0:1], ACT.Exp).then_inc(gate_a, 1)
                    act.wait_ge(gate_v, 2)
                    act.activation(gl[gr, :], gl[gr, :], ACT.Exp, scale=-1.0).then_inc(gate_a, 1)
                if c == 1:
                    act.wait_ge(l2_sum, KT)
                    act.activation(lnss[:, :, :].rearrange("p t n -> p (t n)"), psum[:, 7, 0:NT * VH], ACT.Ln, bias=eps_r[:, :]).then_inc(lnss_ready, 1)
                    act.wait_ge(gate_a, 2)
                    act.activation(gs[gr, :], gl[gr, :], ACT.Ln, bias=1.0).then_inc(gate_a, 1)
                if c == 4:
                    act.wait_ge(bgt_ready, 1)
                    act.activation(eg[:, :, :], bgt[:, :, gr], ACT.Exp)
                    act.wait_ge(gk_ready, 1)
                    act.activation(lnss[:, :, :], lnss[:, :, :], ACT.Exp, scale=-0.5).then_inc(eg_ready, 1)
                    act.wait_ge(wd_sub, 1)
                    act.activation(wdec[:, :], wdec[:, :], ACT.Exp).then_inc(wd_ready, 1)
                if c == 6:
                    prep(0, 0, 3)
                if c == 7:
                    prep(0, 1, 3)
                if c >= 4:
                    n = 2 * (c - 4) + 1
                    t, q = n // NPAIR, n % NPAIR
                    act.wait_ge(v_turned, n + 1)
                    for a in range(HG):
                        h = HG * q + a
                        v = act.activation(vb[:, t, h, :], bank(7, P)[:, a, :], ACT.Copy, scale=bgt[:, t, h:h + 1])
                    v.then_inc(vb_act_ready, 1)
                if c == 4:
                    prep(0, 0, 1)
                if c == 6:
                    prep(0, 1, 1)
            chunks("z", beside_z, unroll=True)

            def level(p, l):
                for c in range(NT):
                    act.wait_ge(ts_done[c], (NLEV - 1) * p + l)
                    if l < NLEV - 1:
                        act.activation(half_heads(T[p % 2][c], l, 0), half_heads(bank(2 * c, P), l, 0), ACT.Copy).then_inc(t_ready[c], 1)

            def apply(p, stage):
                if stage == 1:
                    act.wait_ge(u_done, p + 1)
                    act.activation(U[:, :, :], bank(6, P), ACT.Copy).then_inc(u_ready, 1)
                if stage == 2:
                    act.wait_ge(o0_done, p + 1)
                    act.activation(osq[:, :, :], bank(7, P), ACT.Square).then_inc(osq_ready, 1)
                    act.wait_ge(s1_done, p + 1)
                    act.activation(s1[:, :, :], bank(6, P), ACT.Copy).then_inc(s1_ready, 1)
                if stage == 3:
                    act.wait_ge(qs_done, p + 1)
                    for a in range(HG):
                        h = HG * p + a
                        i = act.activation(qS[:, a, :], bank(7, P)[:, a, :], ACT.Copy, scale=eg[:, 1, h:h + 1])
                    i.then_inc(qs_ready, 1)
                if stage == 4:
                    act.wait_ge(vn_done, p + 1)
                    act.activation(U[:, :, :], bank(6, P), ACT.Copy).then_inc(vn_ready, 1)
                if stage == 5:
                    act.wait_ge(o1_ready, p + 1)
                    act.activation(osq[:, :, :], qS[:, :, :], ACT.Square).then_inc(osq_ready, 1)
                if stage == 6:
                    hs = slice(HG * p, HG * (p + 1))
                    act.wait_ge(o_ready, 2 * (p + 1))
                    act.activation(o_rs[:, :, hs], o_ss[:, :, hs], ACT.Sqrt, scale=1.0 / HD, bias=eps_r[:, :]).then_inc(o_std, 1)

            def turn_y(q):
                for kp in (2 * q, 2 * q + 1):
                    act.wait_ge(yT_turned, kp + 1)
                    act.activation(yT_hi[:, 2 * kp:2 * kp + 2, :], bank(kp % 4), ACT.Copy).then_inc(yhi_ready, 1)

            for p in range(NPAIR + 1):
                for l in range(1, NLEV):
                    if p >= 1:
                        apply(p - 1, l)
                    if p == NPAIR and 2 <= l <= NPAIR:
                        turn_y(l - 2)
                    if p < NPAIR - 1:
                        prep(p + 1, (l - 1) // 3, (l - 1) % 3 + 1)
                    if p < NPAIR:
                        level(p, l)
            turn_y(NPAIR - 1)
            chunks("gdn_out", y_halves(0))
            post_norm(0)
            pre_norm(1, lambda k: gain1[:, KT + k:KT + k + 1])

            def sc_each(i, j, done):
                g = FIRST["sc_in"]
                if j == 0:
                    act.wait_ge(half_done, done)
                    act.activation(sc_u[:, :, :], bank(0), ACT.Copy).then_inc(sc_u_ready, 1)
                if j == 2:
                    act.wait_ge(bank_free, i * 4 + (4 + g + 2))
                    for m in range(2):
                        w = par[:, 1, bass.ds(i * 2 + (V_SC + (SCONV - 1) * 16 + m), 1)]
                        a = act.activation(sc_v[:, m, :], sc_cu[:, m, :], ACT.Copy, scale=w)
                    a.then_inc(sc_v0, 1)
                if j == 3:
                    act.wait_ge(half_done, done)
                    act.activation(sc_z[:, :, :], bank(3), ACT.Silu).then_inc(sc_z_ready, 1)
                    act.wait_ge(bank_free, i * 4 + (4 + g + 4))
                    act.activation(yT_hi[:, bass.ds(i * 2, 2), :], sc_yz[:, :, :], ACT.Copy).then_inc(yhi_ready, 1)
            chunks("sc_in", sc_each)
            halves = y_halves(1)

            def beside_sc_out(i, j, done):
                halves(i, j, done)
                if i == 1 and j == 0:
                    act.wait_ge(ang_ready, 1)
                    act.activation(trig[:, :, :], turn[:, :, :], ACT.Sin).then_inc(trig_ready, 1)
                    act.activation(warm[:, 0:1], eps_r[:, :], ACT.Sqrt)
            chunks("sc_out", beside_sc_out, unroll=True)
            post_norm(1)
            pre_norm(2)

            def glu_each(i, j, done):
                if j % 2 == 0:
                    act.wait_ge(half_done, done)
                    act.activation((glu, rp1)[j // 2][:, :, :], bank(j), ACT.Sigmoid).then_inc(glu_ready, 1)
            chunks("glu", glu_each)
            chunks("qk")

            def tokens_out(dst, func):
                def each(i, j, done):
                    act.wait_ge(half_done, done)
                    act.activation(dst[:, :, bass.ds(i * 1024 + j * CC, CC)], bank(j), func).then_inc(bank_free, 1)
                return each

            def channels_out(dst, func):
                def each(i, j, done):
                    act.wait_ge(half_done, done)
                    act.activation(dst[:, bass.ds(i * 8 + 2 * j, 2), :], bank(j), func).then_inc(bank_free, 1)
                return each
            chunks("v", tokens_out(vt, ACT.Copy))
            z_ret = tokens_out(zr, ACT.Silu)

            def group_norm(i, j, done):
                z_ret(i, j, done)
                if j % NT == NT - 1:
                    h = (4 * i + j) // NT
                    act.wait_ge(gn_step, 2 * NT * (h + 1))
                    if h:
                        act.wait_ge(gn_ready, NT * h)
                    act.activation(grs[:, :], gmv[:, :, 1], ACT.Sqrt, bias=eps_n[:, :]).then_inc(gn_std, 1)
                    act.wait_ge(gn_rec, 2 * (h + 1))
                    for t in range(NT):
                        n = NT * h + t
                        if h:
                            act.wait_ge(rg_ready, n - 1)
                        act.activation(og[t][:, :], psum[:, 4 + n % 4, :], ACT.Identity, scale=grs[:, t:t + 1], bias=gnm[:, t:t + 1]).then_inc(gn_ready, 1)
            chunks("zret", group_norm, unroll=True)
            z_conv = channels_out(zc, ACT.Silu)

            def turned_pairs(i, j, done):
                z_conv(i, j, done)
                if j == 1:
                    act.wait_ge(rg_ready, NT * RH)
                if j:
                    split_two(j - 1)

            def split_two(q):
                for kp in (2 * q, 2 * q + 1):
                    act.wait_ge(yT_turned, KT + kp + 1)
                    act.activation(yT_hi[:, 2 * kp:2 * kp + 2, :], bank(4 + kp % 4), ACT.Copy).then_inc(yhi_ready, 1)
            chunks("zconv", turned_pairs, unroll=True)
            gates = channels_out(gab, ACT.Sigmoid)

            def layer_norm(i, j, done):
                gates(i, j, done)
                c = 4 * i + j
                if c == 0:
                    split_two(KT // 2 - 1)
                if c == 2:
                    for q in range(KT // 2):
                        pair = slice(2 * q, 2 * q + 2)
                        act.wait_ge(xc_ready, q + 1)
                        act.activation(a2[:, pair, :], cv[:, pair, :], ACT.Square).then_inc(a2_ready, 1)
                if c == 3:
                    act.wait_ge(var_done, 1)
                    act.activation(lnm[:, 1, :], psum[:, 7, 0:SEQ], ACT.Sqrt, scale=1.0 / D, bias=eps_n[:, :]).then_inc(ln_step, 1)
                if c == 4:
                    for n in range(KT):
                        act.wait_ge(lns_ready, n // 2 + 1)
                        act.activation(cv[:, n, :], cv[:, n, :], ACT.Silu, scale=par[:, 1, V_LG + n:V_LG + n + 1],
                                       bias=par[:, 1, V_LB + n:V_LB + n + 1]).then_inc(lna_ready, 1)
                if c == 5:
                    for q in range(KT // 2):
                        pair = slice(2 * q, 2 * q + 2)
                        act.wait_ge(lnz_ready, q + 1)
                        act.activation(cT_hi[:, pair, :], cv[:, pair, :], ACT.Copy).then_inc(chi_ready, 1)
            chunks("gates", layer_norm, unroll=True)
            chunks("conv_out")

            def merged(i, j, done):
                if j % 2:
                    b = i * 2 + j // 2
                    act.wait_ge(mg_ready, b + 1)
                    act.activation(hT_hi[:, bass.ds(b * 2, 2), :], rp2[:, :, :], ACT.Copy).then_inc(mhi_ready, 1)
            act.activation(warm[:, 1:2], eps_r[:, :], ACT.Sqrt)
            chunks("ret_out", merged)

            def y_out(i, j, done):
                y_squares(2, j, j).then_inc(bank_free, 1)
            chunks("w_out", y_out)
            post_norm(2)

        @block.gpsimd
        def _(pool):
            pool.memset(ba_raw[:, :, :], 0.0).then_inc(padded, 1)
            def prep(p, c, stage):
                n = NT * p + c
                if stage == 1:
                    pool.wait_ge(e_ready, n + 1)
                    if n:
                        pool.wait_ge(ap_turned, n)
                        pool.wait_ge(chain_ready, n)
                    pool.tensor_tensor(A[:, :, :], E[:, :, :], heads(const[:, C_LOW, :], HG), ALU.mult).then_inc(masked, 1)
                if stage == 3:
                    pool.wait_ge(ap_ready, n + 1)
                    pool.tensor_tensor(T[p % 2][c][:, :, :], A[:, :, :], heads(const[:, C_M0, :], HG), ALU.mult)
                    pool.wait_ge(lt_ready, n + 1)
                    if p == 0:
                        pool.wait_ge(v_turned, NPAIR + 1)
                    if p >= LIVE:
                        pool.wait_ge(vn_done, p - LIVE + 1)
                    pool.tensor_tensor(S[:, p % LIVE, c, :, :], LT[p % 2][c][:, :, :], heads(const[:, C_M0T, :], HG), ALU.mult).then_inc(chain_ready, 1)

            for n in range(KT):
                pool.wait_ge(qkv_ready, n + 1)
                if n >= 2:
                    pool.wait_ge(l2_sum, n - 1)
                qk = qkvT[:, 2 * n:2 * n + 2, :]
                pool.tensor_tensor(sq[n % 2][:, :, :], qk, qk, ALU.mult).then_inc(sq_ready, 1)
            pool.wait_ge(small_loaded, SMALL)
            for c in range(COUNT["z"]):
                pool.wait_ge(bank_free, 4 + FIRST["z"] + c + 1)
                z = zo[:, :, c * CC:(c + 1) * CC].rearrange("p t (h d) -> p t h d", d=HD)
                w = nw_row[:, :].rearrange("p (t h d) -> p t h d", t=1, h=1).to_broadcast([P, NT, CC // HD, HD])
                pool.tensor_tensor(z, z, w, ALU.mult).then_inc(zn_ready, 1)
                if c == 4:
                    prep(0, 0, 1)
                if c == 6:
                    prep(0, 0, 3)
                    prep(0, 1, 1)
                if c == 7:
                    prep(0, 1, 3)

            def apply(p, stage):
                if stage == 1:
                    pool.wait_ge(wd_ready, 1)
                    pool.wait_ge(ktok_ready, 2)
                    if p:
                        pool.wait_ge(s1_done, p)
                    for a in range(HG):
                        h = HG * p + a
                        i = pool.tensor_scalar(kdec[:, a, :], ktok[:, h // 2, :], wdec[:, h:h + 1], None, ALU.mult)
                    i.then_inc(kdec_ready, 1)

            def odd_columns(l):
                for c in range(NT):
                    i = pool.tensor_copy(half_heads(Z[l][c], l, 1), half_of_each(ident, l, 1))
                i.then_inc(odd_ready, 1)
            pool.wait_ge(v_turned, 2 * NPAIR)
            for l in (1, 2):
                odd_columns(l)
            pool.wait_ge(lo_ready, 2 * FIRST["gdn_out"])
            for l in range(3, NLEV):
                odd_columns(l)
            for p in range(NPAIR + 1):
                for l in range(1, NLEV):
                    if p >= 1:
                        apply(p - 1, l)
                    if p < NPAIR - 1:
                        prep(p + 1, (l - 1) // 3, (l - 1) % 3 + 1)
            def ada_pieces(i):
                for j in range(ADA_SLOTS):
                    a = ada[j]
                    pool.wait_ge(ada_ready[j], i * 16 + 16)
                    c = par[:, 1, V_C:V_C + KT].rearrange("p (k n) -> p k n", n=1).to_broadcast([P, KT, P])
                    pool.tensor_tensor(a[:, :, :], a[:, :, :], c, ALU.mult).then_inc(ada_step, 1)
                    for q, n in enumerate((4, 2)):
                        pool.wait_ge(ada_step, i * (3 * ADA_SLOTS) + (3 * j + q + 1))
                        pool.tensor_tensor(a[:, 0:n, :], a[:, 0:n, :], a[:, n:2 * n, :], ALU.add).then_inc(ada_step, 1)
                    pool.wait_ge(ada_step, i * (3 * ADA_SLOTS) + (3 * j + 3))
                    pool.tensor_tensor(ada_sum[:, bass.ds(i * ADA_SLOTS + j, 1), :], a[:, 0:1, :], a[:, 1:2, :], ALU.add).then_inc(ada_used, 1)
            pool.wait_ge(small_ready, 3)
            loop(pool, ADA_PIECES // ADA_SLOTS, ada_pieces)
            def tap_product(n, j, tap):
                w = par[:, 2:4, :].rearrange("p a n -> p (a n)")[:, bass.ds(tap * KT + n, 1)].to_broadcast([P, SEQ])
                pool.tensor_tensor(tapped[:, j, :], aP[:, n, bass.ds(tap, SEQ)], w, ALU.mult).then_inc(tapped_ready, 1)

            def first_tap(n):
                q = n - CONV_DVE
                pool.tensor_tensor(cv[:, n, :], aP[:, n, 0:SEQ], par[:, 2, n:n + 1].to_broadcast([P, SEQ]), ALU.mult).then_inc(cv_pool_step, 1)
                pool.wait_ge(cv_pool_step, CW * q + q + 1)
                pool.tensor_tensor(cv[:, n, :], cv[:, n, :], par[:, 1, V_CB + n:V_CB + n + 1].to_broadcast([P, SEQ]), ALU.add).then_inc(cv_pool_step, 1)

            def pairs_of_taps(n, first, last):
                q = n - CONV_DVE
                with pool.Fori(first, last) as i:
                    for j in range(2):
                        tap_product(n, j, i * 2 + (1 + j))
                    for j in range(2):
                        pool.wait_ge(tapped_ready, i * 2 + (q * (CW - 1) + j + 1))
                        pool.wait_ge(cv_pool_step, i * 2 + (q * (CW + 1) + 2 + j))
                        pool.tensor_tensor(cv[:, n, :], cv[:, n, :], tapped[:, j, :], ALU.add).then_inc(cv_pool_step, 1)
                    pool.wait_ge(cv_pool_step, i * 2 + (q * (CW + 1) + 4))
            pool.wait_ge(padded, 2)
            pool.wait_ge(bank_free, 4 + FIRST["qk"])
            half_taps = (CW - 1) // 2
            for n in range(CONV_DVE, KT - 1):
                first_tap(n)
                pairs_of_taps(n, 0, half_taps)
            first_tap(KT - 1)
            shares = [2 * h for h in range(RH + 1)]
            for h in range(RH):
                pairs_of_taps(KT - 1, shares[h], shares[h + 1])
                for t in range(NT):
                    n = NT * h + t
                    pool.wait_ge(gn_ready, n + 1)
                    vh = slice(h * RDV, (h + 1) * RDV)
                    pool.tensor_tensor(vt[:, t, vh], og[t][:, :], zr[:, t, vh], ALU.mult).then_inc(rg_ready, 1)
            pairs_of_taps(KT - 1, shares[RH], half_taps)
            pool.wait_ge(cv_ready, 4)
            pool.tensor_tensor(ln_sum[0][:, :, :], cv[:, 0:2, :], cv[:, 2:4, :], ALU.add).then_inc(ln_sum_step, 1)
            pool.wait_ge(ln_sum_step, 1)
            pool.wait_ge(cv_pool_step, (CW + 1) * (KT - CONV_DVE))
            pool.tensor_tensor(ln_sum[0][:, :, :], ln_sum[0][:, :, :], cv[:, 5:7, :], ALU.add).then_inc(ln_sum_step, 1)
            pool.wait_ge(a2_ready, 2)
            pool.tensor_tensor(ln_sum[1][:, :, :], a2[:, 0:2, :], a2[:, 2:4, :], ALU.add).then_inc(ln_sum_step, 1)
            pool.wait_ge(ln_sum_step, 3)
            pool.wait_ge(a2_ready, 3)
            pool.tensor_tensor(ln_sum[1][:, :, :], ln_sum[1][:, :, :], a2[:, 4:6, :], ALU.add).then_inc(ln_sum_step, 1)

        @block.vector
        def _(dve):
            def part_lo(o, whole, hi):
                return dve.tensor_tensor(o, whole, hi.bitcast(F32), ALU.subtract)

            def split_lo(g0, i, j, h):
                if isinstance(i, int) and g0 + 4 * i + j >= CHUNKS:
                    return
                s = j % 2 * 2 + h
                dve.wait_ge(hi_ready, i * 8 + (2 * (g0 + j) + h + 1))
                part_lo(w_lo[s][:, :, :], raw[j % RING][:, h * KH2:(h + 1) * KH2, :], w_hi[s][:, :, :]).then_inc(lo_ready, 1)

            def chunks(name, each=None, unroll=False, before_last=None):
                g0 = FIRST[name]

                def step(i):
                    for j in range(4):
                        split_lo(g0, i, j + 1, 1)
                        split_lo(g0, i, j + 2, 0)
                        if j == 0 and name in HANDED and READ_BY[name] == "dve":
                            dve.wait_ge(bank_free, 4 + g0)
                        if each is not None:
                            each(i, j, i * 8 + (2 * (g0 + j) + 6))
                if unroll:
                    for i in range(COUNT[name] // 4):
                        step(i)
                elif before_last is not None:
                    loop(dve, COUNT[name] // 4 - 1, step)
                    before_last()
                    step(COUNT[name] // 4 - 1)
                else:
                    loop(dve, COUNT[name] // 4, step)

            def pre_norm(n, gain, shift=None, between=None):
                for t in range(NT):
                    dve.wait_ge(pre_std, NT * n + t + 1)
                    dve.reciprocal(rstd[:, t:t + 1], ms[:, t:t + 1]).then_inc(pre_rstd, 1)
                    dve.wait_ge(pre_rstd, NT * n + t + 1)
                    dve.tensor_scalar(xn[:, t, :], x[:, t, :], rstd[:, t:t + 1], None, ALU.mult).then_inc(xn_ready, 1)
                if between is not None:
                    between()
                def shifted(kp):
                    dve.wait_ge(turned, KT // 2 * n + kp + 1)
                    for k in (2 * kp, 2 * kp + 1):
                        i = dve.tensor_scalar(hx[:, k, :], bank(4 + kp)[:, k % 2, :], gain(k), shift(k), ALU.mult, ALU.add)
                    i.then_inc(hx_ready, 1)

                for kp in range(KT // 2):
                    if shift is not None and kp % 2 == 0:
                        shifted(kp)
                        shifted(kp + 1)
                    dve.wait_ge(hhi_ready, KT // 2 * n + kp + 1)
                    if shift is not None:
                        pair = slice(2 * kp, 2 * kp + 2)
                        i = part_lo(hT_lo[:, pair, :], hx[:, pair, :], hT_hi[:, pair, :])
                    else:
                        for k in (2 * kp, 2 * kp + 1):
                            i = dve.scalar_tensor_tensor(out=hT_lo[:, k, :], in0=bank(4 + kp)[:, k % 2, :], scalar=gain(k),
                                                         in1=hT_hi[:, k, :].bitcast(F32), op0=ALU.mult, op1=ALU.subtract)
                    i.then_inc(h_ready, 1)
                    if n == 0 and kp == KT // 4 - 1:
                        split_lo(0, 0, 0, 0)

            def y_block(n, b, block, columns):
                dve.wait_ge(row_loaded, 16 * (n + 1))
                w = row[:, columns].rearrange("p (a n) -> p a n", a=1).to_broadcast([P, NT, CC])
                dve.tensor_tensor(xn[:, :, columns], bank(b), w, ALU.mult).then_inc(y_ready, 1)

            def y_halves(n):
                def each(i, j, done):
                    if j % 2:
                        dve.wait_ge(half_done, done)
                        y_block(n, j // 2, i * 2 + j // 2, bass.ds(i * (2 * CC) + j // 2 * CC, CC))
                return each

            def post_norm(n, name):
                dve.wait_ge(bank_free, 4 + FIRST[name] + COUNT[name])
                dve.tensor_reduce(ss[:, 2:2 + NT], yss[:, :, :], AX_X, ALU.add).then_inc(post_ss, 1)
                dve.wait_ge(post_std, n + 1)
                dve.reciprocal(rstd[:, 2:2 + NT], ms[:, 2:2 + NT]).then_inc(post_rstd, 1)
                dve.wait_ge(post_rstd, n + 1)
                pieces = OUT_PIECES if name == ORDER[-1] else 1
                for t in range(NT):
                    for q in range(pieces):
                        c = slice(q * D // pieces, (q + 1) * D // pieces)
                        dve.scalar_tensor_tensor(out=x[:, t, c], in0=xn[:, t, c], scalar=rstd[:, 2 + t:3 + t], in1=x[:, t, c],
                                                 op0=ALU.mult, op1=ALU.add).then_inc(x_ready, 1)

            def col(v, k):
                return par[:, 1, v + k:v + k + 1]

            dve.memset(eps_r[:, :], RMS_EPS)
            dve.memset(eps_n[:, :], NORM_EPS)
            dve.memset(bg[:, :], 0.0).then_inc(cleared, 1)
            dve.memset(gain2[:, 0:1], 0.0).then_inc(bank_free, 4)
            dve.memset(gain2[:, 1:2], 0.0).then_inc(half_done, 4)
            dve.wait_ge(small_turned, 1)
            dve.tensor_copy(gain1[:, :], psum[:, 7, 0:2 * KT]).then_inc(small_ready, 1)
            dve.wait_ge(small_ready, 1)
            def between():
                dve.wait_ge(small_turned, 2)
                dve.tensor_copy(par[:, 0, :], psum[:, 3, 0:P]).then_inc(small_ready, 1)
            pre_norm(0, lambda k: gain1[:, k:k + 1], between=between)
            split_lo(0, 0, 0, 1)
            split_lo(0, 0, 1, 0)
            dve.wait_ge(small_ready, 2)

            def taps(i, j, done):
                g0 = FIRST["qkv"]
                dve.wait_ge(tap0, i * 4 + (g0 + j + 1))
                n = 0
                for tap in range(GCONV - 2, -1, -1):
                    s = GCONV - 1 - tap
                    for m in range(2):
                        if n >= 2:
                            dve.wait_ge(tap_step, i * 20 + (5 * j + n - 1))
                        o = cacc[j % 2][:, m, s:SEQ]
                        a = dve.scalar_tensor_tensor(out=o, in0=bank(j)[:, m, 0:SEQ - s],
                                                     scalar=par[:, 0, bass.ds(i * 8 + (tap * 32 + 2 * j + m), 1)],
                                                     in1=o, op0=ALU.mult, op1=ALU.add)
                        n += 1
                        if n < 6:
                            a.then_inc(tap_step, 1)
                        else:
                            a.then_inc(bank_free, 1)

            def beta_weights():
                dve.wait_ge(ba_hi_ready, 1)
                part_lo(ba_lo[:, :, :], ba_raw[:, :, :], ba_hi[:, :, :]).then_inc(ba_lo_ready, 1)
            chunks("qkv", taps, before_last=beta_weights)

            def prep(p, c, stage):
                n = NT * p + c
                if stage == 1:
                    dve.wait_ge(grow_ready, n + 1)
                    for a in range(HG):
                        g = G_ROW + HG * p + a
                        i = dve.scalar_tensor_tensor(out=E[:, a, :], in0=bank(4, P)[:, a, :], scalar=bgt[:, c, g:g + 1], in1=const[:, C_FLOOR, :],
                                                     op0=ALU.subtract, op1=ALU.max)
                    i.then_inc(d_ready, 1)
                if stage == 2:
                    dve.wait_ge(kq_ready, n + 1)
                    dve.wait_ge(e_ready, n + 1)
                    if n:
                        dve.wait_ge(ap_turned, n)
                    for e in range(2):
                        q = bank(5, P)[:, 2 + e, :].rearrange("p (r n) -> p r n", r=1).to_broadcast([P, 2, P])
                        dve.scalar_tensor_tensor(out=Di[:, 2 * e:2 * e + 2, :], in0=q, scalar=rqs[:, c, 2 * p + e:2 * p + e + 1],
                                                 in1=E[:, 2 * e:2 * e + 2, :], op0=ALU.mult, op1=ALU.mult)
                    dve.wait_ge(masked, n + 1)
                    for a in range(HG):
                        h = HG * p + a
                        i = dve.scalar_tensor_tensor(out=A[:, a, :], in0=bank(5, P)[:, a // 2, :], scalar=brk[:, c, h:h + 1],
                                                     in1=A[:, a, :], op0=ALU.mult, op1=ALU.mult)
                    i.then_inc(a_ready, 1)
                    dve.wait_ge(a_ready, n + 1)
                    dve.tensor_tensor(A[:, :, :], A[:, :, :], heads(ident, HG), ALU.add).then_inc(ap_ready, 1)

            gr = slice(G_ROW, G_ROW + VH)

            def beside_z(i, j, done):
                c = 4 * i + j
                if c == 0:
                    dve.wait_ge(small_loaded, SMALL)
                    dve.wait_ge(ba_done, 1)
                    dve.tensor_scalar(gz[gr, :], psum[gr, 6, 0:SEQ], acols[gr, 1:2], None, ALU.add).then_inc(gate_v, 1)
                    dve.wait_ge(gate_v, 1)
                    dve.scalar_tensor_tensor(out=gl[gr, :], in0=gz[gr, :], scalar=-1.0, in1=gz[gr, :], op0=ALU.mult, op1=ALU.max).then_inc(gate_v, 1)
                if c == 2:
                    dve.wait_ge(small_turned, 3)
                    dve.tensor_copy(par[:, 1:4, :].rearrange("p a n -> p (a n)")[:, 0:376], psum[:, 5, 0:376]).then_inc(small_ready, 1)
                    dve.wait_ge(gate_a, 3)
                    dve.scalar_tensor_tensor(out=gs[gr, :], in0=gz[gr, :], scalar=0.0, in1=gs[gr, :], op0=ALU.max, op1=ALU.add).then_inc(gate_v, 1)
                    dve.wait_ge(gate_v, 3)
                    dve.tensor_scalar(gz[gr, :], gs[gr, :], acols[gr, 2:3], -1.0, ALU.mult, ALU.mult).then_inc(gate_v, 1)
                    dve.wait_ge(gate_v, 4)
                    for t in range(NT):
                        cs = slice(t * P, (t + 1) * P)
                        dve.tensor_tensor_scan(bg[gr, cs], const[gr, C_ONE, :], gz[gr, cs], 0.0, ALU.mult, ALU.add).then_inc(g_ready, 1)
                if c == 3:
                    dve.wait_ge(bg_turned, 1)
                    dve.tensor_copy(bgt[:, :, :], bank(6, P)[:, 0:NT, :]).then_inc(bgt_ready, 1)
                    dve.wait_ge(bgt_ready, 1)
                    dve.wait_ge(lnss_ready, 1)
                    for t in range(NT):
                        lk = lnss[:, t, KH:2 * KH].rearrange("p (n r) -> p n r", r=1).to_broadcast([P, KH, 2])
                        i = dve.scalar_tensor_tensor(out=gk[:, t, :].rearrange("p (n r) -> p n r", r=2), in0=lk, scalar=0.5,
                                                     in1=bgt[:, t, gr].rearrange("p (n r) -> p n r", r=2), op0=ALU.mult, op1=ALU.add)
                    i.then_inc(gk_ready, 1)
                    dve.wait_ge(gk_ready, 1)
                    dve.wait_ge(glast_ready, 1)
                    dve.tensor_tensor(wdec[:, :], psum[:, 7, 2 * VH:3 * VH], gk[:, 0, :], ALU.subtract).then_inc(wd_sub, 1)
                if c >= 4:
                    n = 2 * (c - 4)
                    t, q = n // NPAIR, n % NPAIR
                    dve.wait_ge(v_turned, n + 1)
                    for a in range(HG):
                        h = HG * q + a
                        v = dve.tensor_scalar(vb[:, t, h, :], bank(6, P)[:, a, :], bgt[:, t, h:h + 1], None, ALU.mult)
                    v.then_inc(vb_ready, 1)
                if c == 5:
                    dve.wait_ge(eg_ready, 1)
                    rk, rq = two_each(lnss[:, :, KH:2 * KH]), lnss[:, :, 0:KH]
                    def pairs_of(ap):
                        return ap.rearrange("p t (n r) -> p t n r", r=2)
                    dve.tensor_scalar(rqs[:, :, :], rq, HD ** -0.5, None, ALU.mult).then_inc(rows_step, 1)
                    dve.tensor_tensor(pairs_of(brk[:, :, :]), pairs_of(bgt[:, :, 0:VH]), rk, ALU.mult).then_inc(rows_step, 1)
                    dve.wait_ge(rows_step, 2)
                    dve.scalar_tensor_tensor(out=nbeg[:, :, :], in0=brk[:, :, :], scalar=-1.0, in1=eg[:, :, :], op0=ALU.mult,
                                             op1=ALU.mult).then_inc(rows_step, 1)
                    dve.wait_ge(rows_step, 3)
                    dve.tensor_tensor(pairs_of(eg[:, :, :]), pairs_of(eg[:, :, :]), two_each(rqs[:, :, :]), ALU.mult).then_inc(rows_step, 1)
                    dve.wait_ge(rows_step, 4)
                if c == 4:
                    prep(0, 0, 1)
                if c == 5:
                    prep(0, 0, 2)
                if c == 6:
                    prep(0, 1, 1)
                    prep(0, 1, 2)
                if c == COUNT["z"] - 1:
                    for n in range(2):
                        dve.wait_ge(k_turned, n + 1)
                        dve.tensor_copy(ktok[:, HG * n:HG * (n + 1), :], bank(2 - n, P)).then_inc(ktok_ready, 1)
            chunks("z", beside_z, unroll=True)

            def level_z(p, l):
                for c in range(NT):
                    dve.wait_ge(w_done[c], (NLEV - 1) * p + l)
                    dve.tensor_tensor(half_heads(Z[l][c], l, 0), half_heads(bank(2 * c, P), l, 0), half_of_each(const[:, C_MASK + l - 1, :], l, 0), ALU.mult).then_inc(z_ready[c], 1)

            def level_s(p, l):
                for c in range(NT):
                    dve.wait_ge(ts_done[c], (NLEV - 1) * p + l)
                    dve.tensor_copy(half_heads(S[:, p % LIVE, c, :, :], l, 1), half_heads(bank(2 * c + 1, P), l, 1)).then_inc(s_ready[c], 1)

            def gated(p, t, o):
                hs = slice(HG * p, HG * (p + 1))
                dve.wait_ge(osq_ready, 2 * p + t + 1)
                dve.tensor_reduce(o_ss[:, t, hs], osq[:, :, :], AX_X, ALU.add)
                z = zo[:, t, HG * p * HD:HG * (p + 1) * HD].rearrange("p (h d) -> p h d", d=HD)
                dve.tensor_tensor(z, o, z, ALU.mult).then_inc(o_ready, 1)

            def apply(p, stage):
                if stage == 2:
                    dve.wait_ge(zn_ready, COUNT["z"])
                    gated(p, 0, bank(7, P))
                if stage == 3:
                    dve.wait_ge(ks_done, p + 1)
                    for a in range(HG):
                        h = HG * p + a
                        i = dve.scalar_tensor_tensor(out=R[:, a, :], in0=bank(6, P)[:, a, :], scalar=nbeg[:, 1, h:h + 1],
                                                     in1=vb[:, 1, h, :], op0=ALU.mult, op1=ALU.add)
                    i.then_inc(r_ready, 1)
                if stage == 5:
                    dve.wait_ge(o1_done, p + 1)
                    dve.tensor_tensor(qS[:, :, :], bank(7, P), qS[:, :, :], ALU.add).then_inc(o1_ready, 1)
                    dve.wait_ge(o1_ready, p + 1)
                    gated(p, 1, qS[:, :, :])

            def scaled(p):
                hs = slice(HG * p, HG * (p + 1))
                dve.wait_ge(o_std, p + 1)
                dve.reciprocal(o_rs[:, :, hs], o_rs[:, :, hs]).then_inc(o_rstd, 1)
                dve.wait_ge(o_rstd, p + 1)
                z = zo[:, :, HG * p * HD:HG * (p + 1) * HD].rearrange("p t (h d) -> p t h d", d=HD)
                r = o_rs[:, :, hs].rearrange("p t (h d) -> p t h d", d=1).to_broadcast([P, NT, HG, HD])
                dve.tensor_tensor(z, z, r, ALU.mult).then_inc(og_ready, 1)

            def turn_y(q):
                if q == 0:
                    dve.wait_ge(kdec_ready, NPAIR)
                for kp in (2 * q, 2 * q + 1):
                    pair = slice(2 * kp, 2 * kp + 2)
                    dve.wait_ge(yhi_ready, kp + 1)
                    part_lo(yT_lo[:, pair, :], bank(kp % 4), yT_hi[:, pair, :]).then_inc(y_op_ready, 1)

            for p in range(NPAIR + 1):
                for l in range(1, NLEV):
                    if p < NPAIR:
                        level_z(p, l)
                    if p >= 1:
                        apply(p - 1, l)
                    if p < NPAIR - 1:
                        prep(p + 1, (l - 1) // 3, (l - 1) % 3 + 1)
                    if p < NPAIR:
                        level_s(p, l)
                    if p >= 1 and l == NLEV - 1:
                        scaled(p - 1)
                    if p == NPAIR and 2 <= l <= NPAIR:
                        turn_y(l - 2)
            turn_y(NPAIR - 1)
            chunks("gdn_out", y_halves(0))
            post_norm(0, "gdn_out")
            pre_norm(1, lambda k: gain1[:, KT + k:KT + k + 1])

            def sc_each(i, j, done):
                g = FIRST["sc_in"]
                if j == 1:
                    dve.wait_ge(half_done, done)
                    dve.wait_ge(sc_u_ready, i + 1)
                    dve.tensor_tensor(sc_cu[:, :, :], bank(1), sc_u[:, :, :], ALU.mult).then_inc(bank_free, 2)
                if j == 2:
                    dve.wait_ge(sc_v0, i + 1)
                    n = 0
                    for tap in range(SCONV - 2, -1, -1):
                        s = SCONV - 1 - tap
                        for m in range(2):
                            if n >= 2:
                                dve.wait_ge(sc_step, i * 4 + (n - 1))
                            o = sc_v[:, m, s:SEQ]
                            dve.scalar_tensor_tensor(out=o, in0=sc_cu[:, m, 0:SEQ - s],
                                                     scalar=par[:, 1, bass.ds(i * 2 + (V_SC + tap * 16 + m), 1)],
                                                     in1=o, op0=ALU.mult, op1=ALU.add).then_inc(sc_step, 1)
                            n += 1
                    dve.wait_ge(half_done, done)
                    dve.wait_ge(sc_step, i * 4 + 4)
                    dve.tensor_tensor(sc_y[:, :, :], bank(2), sc_v[:, :, :], ALU.mult).then_inc(bank_free, 1)
                if j == 3:
                    dve.wait_ge(sc_z_ready, i + 1)
                    dve.wait_ge(bank_free, i * 4 + (4 + g + 3))
                    dve.tensor_tensor(sc_yz[:, :, :], sc_y[:, :, :], sc_z[:, :, :], ALU.mult).then_inc(bank_free, 1)
                    dve.wait_ge(yhi_ready, i + (KT + 1))
                    pair = bass.ds(i * 2, 2)
                    part_lo(yT_lo[:, pair, :], sc_yz[:, :, :], yT_hi[:, pair, :]).then_inc(y_op_ready, 1)
            chunks("sc_in", sc_each)
            def shift_scale_gate():
                dve.wait_ge(mod_done, 1)
                dve.tensor_tensor(mod[:, :], psum[:, 3, 0:3 * KT], par[:, 1, V_BADA:V_BADA + 3 * KT], ALU.add).then_inc(mod_ready, 1)
                dve.wait_ge(mod_ready, 1)
                dve.scalar_tensor_tensor(out=gain2[:, :], in0=mod[:, KT:2 * KT], scalar=1.0, in1=par[:, 1, V_PRE2:V_PRE2 + KT],
                                         op0=ALU.add, op1=ALU.mult).then_inc(gain2_ready, 1)
                dve.wait_ge(gain2_ready, 1)

            def angles():
                pi = math.pi
                c1 = 6.28125
                c2 = float(np.float32(np.float32((2 * pi - c1) * 2 ** 20).astype(np.int32) / np.float32(2 ** 20)))
                c3 = 2 * pi - c1 - c2
                magic = 1.5 * 2.0 ** 23
                cos_t, sin_t = turn[:, 0, :], turn[:, 1, :]
                angle_steps = [0]

                def angle(i):
                    angle_steps[0] += 1
                    i.then_inc(ang_step, 1)
                    dve.wait_ge(ang_step, angle_steps[0])
                dve.wait_ge(rope_loaded, 16)
                angle(dve.tensor_copy(ang[:, :], pos_i[:, :]))
                angle(dve.tensor_scalar(ang[:, :], ang[:, :], freq[:, :], None, ALU.mult))
                angle(dve.tensor_scalar(cos_t, ang[:, :], 1.0 / (2 * pi), magic, ALU.mult, ALU.add))
                angle(dve.tensor_scalar(cos_t, cos_t, magic, None, ALU.subtract))
                for c in (c1, c2, c3):
                    angle(dve.scalar_tensor_tensor(out=ang[:, :], in0=cos_t, scalar=-c, in1=ang[:, :], op0=ALU.mult, op1=ALU.add))
                lim = float(np.nextafter(np.float32(pi), np.float32(0)))
                angle(dve.tensor_scalar(sin_t, ang[:, :], lim, -lim, ALU.min, ALU.max))
                angle(dve.tensor_scalar(ang[:, :], ang[:, :], pi / 2, None, ALU.add))
                angle(dve.tensor_scalar(cos_t, ang[:, :], pi, -2 * pi, ALU.is_gt, ALU.mult))
                angle(dve.tensor_tensor(cos_t, cos_t, ang[:, :], ALU.add))
                dve.tensor_scalar(cos_t, cos_t, lim, -lim, ALU.min, ALU.max).then_inc(ang_ready, 1)

            def beside_sc_out(i, j, done):
                y_halves(1)(i, j, done)
                if i == 0 and j == 2:
                    angles()
            chunks("sc_out", beside_sc_out, unroll=True)
            post_norm(1, "sc_out")
            pre_norm(2, lambda k: gain2[:, k:k + 1], lambda k: mod[:, k:k + 1], between=shift_scale_gate)
            dve.memset(aP[:, :, 0:CPAD], 0.0).then_inc(padded, 1)

            def glu_each(i, j, done):
                if j % 2:
                    dve.wait_ge(half_done, done)
                    dve.wait_ge(glu_ready, i * 2 + (j // 2 + 1))
                    dve.tensor_tensor(aP[:, bass.ds(i * 4 + j // 2 * 2, 2), CPAD:CPAD + SEQ], bank(j), (glu, rp1)[j // 2][:, :, :],
                                      ALU.mult).then_inc(bank_free, 2)
            chunks("glu", glu_each)
            dve.wait_ge(trig_ready, 1)
            cos2, sin2 = (trig[:, s, :].rearrange("p (a n) -> p a n", a=1).to_broadcast([P, 2, SEQ]) for s in range(2))

            def rotate(i, j, done):
                dve.wait_ge(half_done, done)
                dve.tensor_tensor(rp1[:, :, :], bank(j), cos2, ALU.mult)
                dve.tensor_tensor(rp2[:, :, :], bank(j), sin2, ALU.mult).then_inc(bank_free, 1)
                dve.wait_ge(bank_free, i * 4 + (4 + FIRST["qk"] + j + 1))
                dve.tensor_tensor(qkT[:, bass.ds(i * 8 + 2 * j, 1), :], rp1[:, 0:1, :], rp2[:, 1:2, :], ALU.subtract)
                dve.tensor_tensor(qkT[:, bass.ds(i * 8 + (2 * j + 1), 1), :], rp2[:, 0:1, :], rp1[:, 1:2, :], ALU.add).then_inc(rp_step, 1)
                dve.wait_ge(rp_step, i * 4 + (j + 1))
            dve.wait_ge(bank_free, 4 + FIRST["qk"])
            chunks("qk", rotate)

            def conv_op(n, tap):
                def w(j):
                    return par[:, 2 + j // 16, j % 16 * KT + n:j % 16 * KT + n + 1]
                step = CW * n + tap
                if 2 <= tap < CW:
                    dve.wait_ge(cv_step, step - 1)
                if tap == 1 and n:
                    dve.wait_ge(cv_ready, n)
                o = cvo[:, :] if tap % 2 else cv[:, n, :]
                if tap < CW:
                    src = aP[:, n, tap:tap + SEQ]
                if tap == CW:
                    dve.wait_ge(cv_step, step)
                    dve.tensor_tensor(cv[:, n, :], cv[:, n, :], cvo[:, :], ALU.add).then_inc(cv_ready, 1)
                elif tap == 0:
                    dve.tensor_scalar(o, src, w(0), col(V_CB, n), ALU.mult, ALU.add).then_inc(cv_step, 1)
                elif tap == 1:
                    dve.tensor_scalar(o, src, w(1), None, ALU.mult).then_inc(cv_step, 1)
                else:
                    dve.scalar_tensor_tensor(out=o, in0=src, scalar=w(tap), in1=o, op0=ALU.mult, op1=ALU.add).then_inc(cv_step, 1)

            conv_ops = [(n, tap) for n in range(CONV_DVE) for tap in range(CW + 1)]

            def conv_share(n):
                for _ in range(min(n, len(conv_ops))):
                    conv_op(*conv_ops.pop(0))

            def decayed(i, j, done):
                c = 4 * i + j
                conv_share(8)
                if c < RH:
                    dve.wait_ge(sco_done, c + 1)
                    dve.tensor_tensor(st[:, c, :], psum[:, 4 + c, 0:3 * P], decay[:, c, :], ALU.mult).then_inc(st_ready, 1)
            dve.wait_ge(padded, 2)
            dve.wait_ge(decay_loaded, 16)
            dve.wait_ge(bank_free, 4 + FIRST["v"])
            chunks("v", decayed, unroll=True)

            def group_norm(i, j, done):
                n = 4 * i + j
                h, t = n // NT, n % NT
                conv_share(6)
                dve.wait_ge(ro_done, n + 1)
                dve.bn_stats(gst[:, t, :], psum[:, 4 + n % 4, :]).then_inc(gn_step, 1)
                dve.wait_ge(gn_step, 2 * n + 1)
                if h:
                    dve.wait_ge(gn_rec, 2 * h)
                dve.bn_aggr(gmv[:, t, :], gst[:, t, :]).then_inc(gn_step, 1)
                if t == NT - 1:
                    dve.wait_ge(gn_std, h + 1)
                    dve.reciprocal(grs[:, :], grs[:, :]).then_inc(gn_rec, 1)
                    dve.wait_ge(gn_rec, 2 * h + 1)
                    dve.scalar_tensor_tensor(out=gnm[:, :], in0=gmv[:, :, 0], scalar=-1.0, in1=grs[:, :], op0=ALU.mult, op1=ALU.mult).then_inc(gn_rec, 1)
                    conv_share(6)
            chunks("zret", group_norm, unroll=True)

            def turned_pairs(i, j, done):
                if j:
                    split_two(j - 1)

            def split_two(q):
                for kp in (2 * q, 2 * q + 1):
                    conv_share(2)
                    pair = slice(2 * kp, 2 * kp + 2)
                    dve.wait_ge(yhi_ready, 2 * KT + kp + 1)
                    part_lo(yT_lo[:, pair, :], bank(4 + kp % 4), yT_hi[:, pair, :]).then_inc(y_op_ready, 1)
            chunks("zconv", turned_pairs, unroll=True)
            mean, inv = (lnm[:, s, :].rearrange("p (a n) -> p a n", a=1).to_broadcast([P, 2, SEQ]) for s in range(2))
            pairs = [slice(2 * q, 2 * q + 2) for q in range(KT // 2)]

            def layer_norm(i, j, done):
                c = 4 * i + j
                if c == 0:
                    split_two(KT // 2 - 1)
                    for k in range(KT):
                        i = dve.tensor_scalar(gdiag[:, k, :], ident, mod[:, 2 * KT + k:2 * KT + k + 1], None, ALU.mult)
                    i.then_inc(gate_diag, 1)
                if c == 1:
                    conv_share(len(conv_ops))
                if c == 2:
                    dve.wait_ge(gate_row, 1)
                    dve.wait_ge(row_loaded, 16 * 3)
                    for s in range(2):
                        half = slice(512 * s, 512 * (s + 1))
                        dve.tensor_tensor(row[:, half], row[:, half], psum[:, 4 + s, :], ALU.mult).then_inc(row_mul, 1)
                    dve.wait_ge(mean_done, 1)
                    dve.tensor_scalar(lnm[:, 0, :], psum[:, 6, 0:SEQ], 1.0 / D, None, ALU.mult).then_inc(ln_mean, 1)
                    dve.wait_ge(ln_mean, 1)
                    for pair in pairs:
                        dve.tensor_tensor(cv[:, pair, :], cv[:, pair, :], mean, ALU.subtract).then_inc(xc_ready, 1)
                if c == 3:
                    dve.wait_ge(ln_step, 1)
                    dve.reciprocal(lnm[:, 1, :], lnm[:, 1, :]).then_inc(ln_rstd, 1)
                    dve.wait_ge(ln_rstd, 1)
                    dve.wait_ge(xc_ready, KT // 2)
                    for pair in pairs:
                        dve.tensor_tensor(cv[:, pair, :], cv[:, pair, :], inv, ALU.mult).then_inc(lns_ready, 1)
                if c == 4:
                    for q, pair in enumerate(pairs):
                        dve.wait_ge(lna_ready, 2 * q + 2)
                        dve.tensor_tensor(cv[:, pair, :], cv[:, pair, :], zc[:, pair, :], ALU.mult).then_inc(lnz_ready, 1)
                if c == 5:
                    for q, pair in enumerate(pairs):
                        dve.wait_ge(chi_ready, q + 1)
                        part_lo(cT_lo[:, pair, :], cv[:, pair, :], cT_hi[:, pair, :]).then_inc(cop_ready, 1)
            chunks("gates", layer_norm, unroll=True)

            def conv_gated(i, j, done):
                dve.wait_ge(half_done, done)
                o = gab[:, KT + 2 * j:KT + 2 * j + 2, :]
                dve.tensor_tensor(o, bank(j), o, ALU.mult).then_inc(bank_free, 1)
            chunks("conv_out", conv_gated)

            def merged(i, j, done):
                if j % 2:
                    b = 2 * i + j // 2
                    pair = slice(2 * b, 2 * b + 2)
                    dve.wait_ge(half_done, done)
                    dve.tensor_tensor(rp2[:, :, :], bank(j // 2), gab[:, pair, :], ALU.mult).then_inc(bank_free, 2)
                    dve.wait_ge(bank_free, 4 + FIRST["ret_out"] + 2 * (b + 1))
                    dve.tensor_tensor(rp2[:, :, :], rp2[:, :, :], gab[:, KT + 2 * b:KT + 2 * b + 2, :], ALU.add).then_inc(mg_ready, 1)
                    dve.wait_ge(mg_ready, b + 1)
                    dve.wait_ge(mhi_ready, b + 1)
                    part_lo(hT_lo[:, pair, :], rp2[:, :, :], hT_hi[:, pair, :]).then_inc(mop_ready, 1)
            chunks("ret_out", merged, unroll=True)
            dve.wait_ge(row_mul, 2)

            def y_out(i, j, done):
                dve.wait_ge(half_done, done)
                y_block(2, j, j, slice(j * CC, (j + 1) * CC))
            chunks("w_out", y_out)
            post_norm(2, "w_out")


_INS = ["x", "pre_norm_w", "post_norm_w", "gdn_w_in", "gdn_conv_w", "gdn_A_log", "gdn_dt_bias", "gdn_norm_w",
        "gdn_w_out", "sc_w_in", "sc_conv_w", "sc_w_out", "c_2", "positions_2", "w_ada_2", "b_ada_2", "pre_norm_g_2",
        "w_in_2", "conv_w_2", "conv_b_2", "conv_ln_g_2", "conv_ln_b_2", "w_ret_out_2", "w_conv_out_2", "w_out_2",
        "post_norm_g_2"]


def shape_constants():
    import numpy as _np

    i = _np.arange(P)
    masks = _np.zeros((P, NCONST, P), _np.float32)
    masks[:, C_ID] = _np.eye(P)
    masks[:, C_ONE] = 1.0
    masks[:, C_LOW] = i[:, None] > i[None, :]
    masks[:, C_FLOOR] = _np.where(i[:, None] >= i[None, :], E_LEAST, 1e30)
    for level in range(NLEV):
        b = 2 ** level
        same = (i[:, None] // (2 * b)) == (i[None, :] // (2 * b))
        low = same & (i[:, None] // b % 2 == 1) & (i[None, :] // b % 2 == 0)
        signed = _np.eye(P) - low
        if level == 0:
            masks[:, C_M0], masks[:, C_M0T] = signed, signed.T
        else:
            masks[:, C_MASK + level - 1] = signed
    log_g = _np.log1p(-_np.exp2(-5.0 - _np.arange(RH)))
    diff = _np.arange(SEQ)[None, :] - i[:, None]
    decays = _np.zeros((P, RH, 3 * P), _np.float32)
    for h in range(RH):
        d = _np.where(diff >= 0, _np.exp(log_g[h] * _np.maximum(diff, 0)), 0.0) * RDK ** -0.5
        decays[:, h, :SEQ] = d
        decays[:, h, SEQ:] = d[:, :P]
    freqs = (_np.float32(ROPE_BASE) ** (-_np.arange(P, dtype=_np.float32) / _np.float32(P))).astype(_np.float32)
    return masks, decays, freqs.reshape(P, 1)


def kernel(**inputs):
    import numpy as _np
    import concourse.bacc as _bacc
    from concourse import mybir as _mybir
    from concourse.bass_utils import run_bass_kernel_spmd as _run

    nc = _bacc.Bacc("TRN2", target_bir_lowering=False, num_devices=1)
    arrays, args = {}, []
    given = [(name, _np.ascontiguousarray(inputs[name])) for name in _INS]
    given += list(zip(("masks", "decays", "freqs"), shape_constants()))
    for name, a in given:
        arrays[f"in_{name}_dram"] = a
        args.append(nc.dram_tensor(f"in_{name}_dram", a.shape, _mybir.dt.from_np(a.dtype), kind="ExternalInput").ap())
    out = nc.dram_tensor("out_0_dram", (1, SEQ, D), F32, kind="ExternalOutput").ap()
    build(nc, *args, out)
    r = _run(nc, [arrays], core_ids=[0])
    return r.results[0]["out_0_dram"]
```
